# Optimizing a Trainium2 kernel written in Bass

```python
import math
import jax, jax.numpy as jnp
from jax import lax
import numpy as np

D_MODEL = 1024
BATCH = 1
SEQ = 256
DEPTH = 1

HEAD_DIM = 64
SWA_HEADS = 8
SWA_KV_HEADS = 2
SWA_WINDOW = 128
SWA_BLOCK = 128
RNN_WIDTH = D_MODEL
RNN_BLOCKS = 16
RNN_BLOCK_WIDTH = RNN_WIDTH // RNN_BLOCKS
RNN_CONV = 4
RGLRU_C = 8.0
MOBA_HEADS = 8
MOBA_BLOCK = 256
MOBA_TOPK = 3
NUM_BUCKETS = 32
MAX_DISTANCE = 2048
D_FF = 2816
FFN_CONV = 3

RMS_EPS = 1e-6
NEG_INF = -1e30
N_BRANCH = 3
SWA_Q = SWA_HEADS * HEAD_DIM
SWA_KV = SWA_KV_HEADS * HEAD_DIM
MOBA_W = MOBA_HEADS * HEAD_DIM
IN_WIDTHS = (SWA_Q, SWA_KV, SWA_KV, RNN_WIDTH, RNN_WIDTH, MOBA_W, MOBA_W, MOBA_W, N_BRANCH * D_MODEL)
IN_OFFSETS = tuple(sum(IN_WIDTHS[:i + 1]) for i in range(len(IN_WIDTHS) - 1))
D_IN = sum(IN_WIDTHS)
D_MIX = SWA_Q + RNN_WIDTH + MOBA_W


def rms_norm(x, gain):
    xf = x.astype(jnp.float32)
    y = xf * lax.rsqrt(jnp.mean(xf * xf, axis=-1, keepdims=True) + RMS_EPS)
    return (y * gain.astype(jnp.float32)).astype(x.dtype)

def t5_bucket(dist):
    dist = jnp.maximum(dist, 0)
    max_exact = NUM_BUCKETS // 2
    log_ratio = jnp.log(jnp.maximum(dist, 1).astype(jnp.float32) / max_exact) / math.log(MAX_DISTANCE / max_exact)
    large = max_exact + (log_ratio * (NUM_BUCKETS - max_exact)).astype(jnp.int32)
    large = jnp.minimum(large, NUM_BUCKETS - 1)
    return jnp.where(dist < max_exact, dist, large)

def causal_dwconv(x, w, b):
    k_width = w.shape[0]
    s = x.shape[1]
    xp = jnp.pad(x, ((0, 0), (k_width - 1, 0), (0, 0)))
    return sum(xp[:, k:k + s] * w[k] for k in range(k_width)) + b

def swa_attention(q, k, v, sinks, bias_a):
    b_sz, s_len = q.shape[:2]
    L = SWA_BLOCK
    nblk = s_len // L
    grp = SWA_HEADS // SWA_KV_HEADS
    qb = q.reshape(b_sz, nblk, L, SWA_KV_HEADS, grp, HEAD_DIM)

    def band(t):
        tp = jnp.pad(t, ((0, 0), (L, 0), (0, 0), (0, 0))).reshape(b_sz, nblk + 1, L, SWA_KV_HEADS, HEAD_DIM)
        return jnp.concatenate([tp[:, :-1], tp[:, 1:]], axis=2)

    kb, vb = band(k), band(v)
    s = jnp.einsum('bnqkgd,bnskd->bnkgqs', qb, kb).astype(jnp.float32) * (HEAD_DIM ** -0.5)
    qi = jnp.arange(L)
    sj = jnp.arange(2 * L)
    diff = qi[:, None] + L - sj[None, :]
    bias = bias_a[t5_bucket(diff)].astype(jnp.float32).transpose(2, 0, 1).reshape(SWA_KV_HEADS, grp, L, 2 * L)
    key_pos = jnp.arange(nblk)[:, None] * L - L + sj[None, :]
    valid = ((diff >= 0) & (diff < SWA_WINDOW))[None] & (key_pos >= 0)[:, None, :]
    s = jnp.where(valid[None, :, None, None], s + bias, NEG_INF)
    sink = sinks.astype(jnp.float32).reshape(SWA_KV_HEADS, grp)[:, :, None, None]
    m = jnp.maximum(jnp.max(s, axis=-1, keepdims=True), sink)
    p = jnp.exp(s - m)
    p = p / (jnp.sum(p, axis=-1, keepdims=True) + jnp.exp(sink - m))
    o = jnp.einsum('bnkgqs,bnskd->bnqkgd', p.astype(v.dtype), vb)
    return o.reshape(b_sz, s_len, SWA_Q)

def rg_lru(x, ga_w, ga_b, gx_w, gx_b, lam):
    b_sz, s_len, width = x.shape
    xb = x.reshape(b_sz, s_len, RNN_BLOCKS, RNN_BLOCK_WIDTH)
    r = jax.nn.sigmoid(jnp.einsum('bsnc,ncd->bsnd', xb, ga_w).reshape(b_sz, s_len, width) + ga_b)
    i = jax.nn.sigmoid(jnp.einsum('bsnc,ncd->bsnd', xb, gx_w).reshape(b_sz, s_len, width) + gx_b)
    log_a = -RGLRU_C * r.astype(jnp.float32) * jax.nn.softplus(-lam.astype(jnp.float32))
    a = jnp.exp(log_a)
    mult = jnp.sqrt(-jnp.expm1(2.0 * log_a))
    mult = jnp.where((jnp.arange(s_len) == 0)[None, :, None], 1.0, mult)
    u = mult * (i * x).astype(jnp.float32)

    def combine(left, right):
        a_l, b_l = left
        a_r, b_r = right
        return (a_l * a_r, a_r * b_l + b_r)

    _, h = lax.associative_scan(combine, (a, u), axis=1)
    return h.astype(x.dtype)

def moba_attention(q, k, v, bias_c):
    b_sz, s_len = q.shape[:2]
    MB = MOBA_BLOCK
    nb = -(-s_len // MB)
    s_pad = nb * MB
    pad = ((0, 0), (0, s_pad - s_len), (0, 0), (0, 0))
    q, k, v = jnp.pad(q, pad), jnp.pad(k, pad), jnp.pad(v, pad)
    topk = min(MOBA_TOPK, nb)
    kb = k.reshape(b_sz, nb, MB, MOBA_HEADS, HEAD_DIM)
    vb = v.reshape(b_sz, nb, MB, MOBA_HEADS, HEAD_DIM)
    k_mean = jnp.mean(kb.astype(jnp.float32), axis=2).astype(k.dtype)
    k_bh = kb.transpose(0, 3, 1, 2, 4)
    v_bh = vb.transpose(0, 3, 1, 2, 4)
    q_chunks = q.reshape(b_sz, nb, MB, MOBA_HEADS, HEAD_DIM).transpose(1, 0, 2, 3, 4)
    k_own = kb.transpose(1, 0, 2, 3, 4)
    v_own = vb.transpose(1, 0, 2, 3, 4)
    pos = jnp.arange(MB)
    own_diff = pos[:, None] - pos[None, :]
    own_mask = own_diff >= 0
    own_bias = bias_c[t5_bucket(own_diff)].astype(jnp.float32).transpose(0, 2, 1)
    b_ix = jnp.arange(b_sz)[:, None, None, None]
    h_ix = jnp.arange(MOBA_HEADS)[None, None, :, None]
    blk_ids = jnp.arange(nb)
    scale = HEAD_DIM ** -0.5

    def one_block(args):
        n, q_c, k_c, v_c = args
        gate = jnp.einsum('bqhd,bmhd->bqhm', q_c, k_mean).astype(jnp.float32)
        gate = jnp.where(blk_ids < n, gate, NEG_INF)
        _, sel = lax.top_k(gate, topk)
        sel_valid = sel < n
        k_sel = k_bh[b_ix, h_ix, sel]
        v_sel = v_bh[b_ix, h_ix, sel]
        s_sel = jnp.einsum('bqhd,bqhtsd->bqhts', q_c, k_sel).astype(jnp.float32) * scale
        dist = (n * MB + pos)[None, :, None, None, None] - (sel[..., None] * MB + pos)
        s_sel = s_sel + bias_c[t5_bucket(dist), h_ix[..., None]].astype(jnp.float32)
        s_sel = jnp.where(sel_valid[..., None], s_sel, NEG_INF).reshape(b_sz, MB, MOBA_HEADS, topk * MB)
        s_own = jnp.einsum('bqhd,bshd->bqhs', q_c, k_c).astype(jnp.float32) * scale + own_bias
        s_own = jnp.where(own_mask[:, None, :], s_own, NEG_INF)
        p = jax.nn.softmax(jnp.concatenate([s_sel, s_own], axis=-1), axis=-1).astype(v.dtype)
        p_sel = p[..., :topk * MB].reshape(b_sz, MB, MOBA_HEADS, topk, MB)
        p_own = p[..., topk * MB:]
        return jnp.einsum('bqhts,bqhtsd->bqhd', p_sel, v_sel) + jnp.einsum('bqhs,bshd->bqhd', p_own, v_c)

    o = lax.map(one_block, (blk_ids, q_chunks, k_own, v_own))
    return o.transpose(1, 0, 2, 3, 4).reshape(b_sz, s_pad, MOBA_W)[:, :s_len]

def first_inputs(seed: int = 0) -> dict:
    key = jax.random.key(seed)
    ks = jax.random.split(key, 32)
    f32 = jnp.float32

    def nrm(k, shape, fan_in, scale=1.0):
        return jax.random.normal(k, shape, f32) * (scale * fan_in ** -0.5)

    def gain(k, shape):
        return 1.0 + 0.05 * jax.random.normal(k, shape, f32)

    def small(k, shape, scale=0.02):
        return scale * jax.random.normal(k, shape, f32)

    a_init = jax.random.uniform(ks[16], (DEPTH, RNN_WIDTH), f32, 0.9, 0.999)
    w_branch = jnp.concatenate([
        nrm(ks[20], (DEPTH, SWA_Q, D_MODEL), SWA_Q),
        nrm(ks[21], (DEPTH, RNN_WIDTH, D_MODEL), RNN_WIDTH),
        nrm(ks[22], (DEPTH, MOBA_W, D_MODEL), MOBA_W)], axis=1)
    return {
        'x': jax.random.normal(ks[0], (BATCH, SEQ, D_MODEL), f32),
        'c': jax.random.normal(ks[1], (BATCH, D_MODEL), f32),
        'w_mod': nrm(ks[2], (DEPTH, D_MODEL, 6 * D_MODEL), D_MODEL, 0.5),
        'b_mod': small(ks[3], (DEPTH, 6 * D_MODEL)),
        'norm_mix': gain(ks[4], (DEPTH, D_MODEL)),
        'norm_ffn': gain(ks[5], (DEPTH, D_MODEL)),
        'w_in': nrm(ks[6], (DEPTH, D_MODEL, D_IN), D_MODEL),
        'qnorm_a': gain(ks[7], (DEPTH, HEAD_DIM)),
        'knorm_a': gain(ks[8], (DEPTH, HEAD_DIM)),
        'sinks': small(ks[9], (DEPTH, SWA_HEADS), 0.5),
        'rnn_conv_w': nrm(ks[10], (DEPTH, RNN_CONV, RNN_WIDTH), RNN_CONV),
        'rnn_conv_b': small(ks[11], (DEPTH, RNN_WIDTH)),
        'rnn_gate_a_w': nrm(ks[12], (DEPTH, RNN_BLOCKS, RNN_BLOCK_WIDTH, RNN_BLOCK_WIDTH), RNN_BLOCK_WIDTH),
        'rnn_gate_a_b': small(ks[13], (DEPTH, RNN_WIDTH)),
        'rnn_gate_x_w': nrm(ks[14], (DEPTH, RNN_BLOCKS, RNN_BLOCK_WIDTH, RNN_BLOCK_WIDTH), RNN_BLOCK_WIDTH),
        'rnn_gate_x_b': small(ks[15], (DEPTH, RNN_WIDTH)),
        'rnn_lambda': jnp.log(a_init) - jnp.log1p(-a_init),
        'qnorm_c': gain(ks[17], (DEPTH, HEAD_DIM)),
        'knorm_c': gain(ks[18], (DEPTH, HEAD_DIM)),
        'rel_bias': small(ks[19], (NUM_BUCKETS, SWA_HEADS + MOBA_HEADS), 0.5),
        'w_branch': w_branch,
        'w_out': nrm(ks[23], (DEPTH, D_MODEL, D_MODEL), D_MODEL),
        'w_up': nrm(ks[24], (DEPTH, D_MODEL, 2 * D_FF), D_MODEL),
        'ffn_conv_w': nrm(ks[25], (DEPTH, FFN_CONV, 2 * D_FF), FFN_CONV),
        'ffn_conv_b': small(ks[26], (DEPTH, 2 * D_FF)),
        'w_down': nrm(ks[27], (DEPTH, D_FF, D_MODEL), D_FF),
    }

def first_block(x, c, w_mod, b_mod, norm_mix, norm_ffn, w_in, qnorm_a, knorm_a, sinks,
              rnn_conv_w, rnn_conv_b, rnn_gate_a_w, rnn_gate_a_b, rnn_gate_x_w, rnn_gate_x_b,
              rnn_lambda, qnorm_c, knorm_c, rel_bias, w_branch, w_out, w_up, ffn_conv_w,
              ffn_conv_b, w_down):
    b_sz, s_len, _ = x.shape
    c_act = jax.nn.silu(c)
    bias_a = rel_bias[:, :SWA_HEADS]
    bias_c = rel_bias[:, SWA_HEADS:]
    for l in range(DEPTH):
        mod = (c_act @ w_mod[l] + b_mod[l])[:, None, :]
        shift_m, scale_m, gate_m, shift_f, scale_f, gate_f = jnp.split(mod, 6, axis=-1)

        h = rms_norm(x, norm_mix[l]) * (1.0 + scale_m) + shift_m
        z = h @ w_in[l]
        qa, ka, va, xr, yr, qc, kc, vc, g_logits = jnp.split(z, IN_OFFSETS, axis=-1)

        qa = rms_norm(qa.reshape(b_sz, s_len, SWA_HEADS, HEAD_DIM), qnorm_a[l])
        ka = rms_norm(ka.reshape(b_sz, s_len, SWA_KV_HEADS, HEAD_DIM), knorm_a[l])
        va = va.reshape(b_sz, s_len, SWA_KV_HEADS, HEAD_DIM)
        o_a = swa_attention(qa, ka, va, sinks[l], bias_a)

        xr = causal_dwconv(xr, rnn_conv_w[l], rnn_conv_b[l])
        hr = rg_lru(xr, rnn_gate_a_w[l], rnn_gate_a_b[l], rnn_gate_x_w[l], rnn_gate_x_b[l], rnn_lambda[l])
        o_b = hr * jax.nn.gelu(yr)

        qc = rms_norm(qc.reshape(b_sz, s_len, MOBA_HEADS, HEAD_DIM), qnorm_c[l])
        kc = rms_norm(kc.reshape(b_sz, s_len, MOBA_HEADS, HEAD_DIM), knorm_c[l])
        vc = vc.reshape(b_sz, s_len, MOBA_HEADS, HEAD_DIM)
        o_c = moba_attention(qc, kc, vc, bias_c)

        wb = w_branch[l]
        p_a = o_a @ wb[:SWA_Q]
        p_b = o_b @ wb[SWA_Q:SWA_Q + RNN_WIDTH]
        p_c = o_c @ wb[SWA_Q + RNN_WIDTH:]
        g = jax.nn.sigmoid(g_logits.reshape(b_sz, s_len, N_BRANCH, D_MODEL))
        merged = g[:, :, 0] * p_a + g[:, :, 1] * p_b + g[:, :, 2] * p_c
        x = x + gate_m * (merged @ w_out[l])

        h = rms_norm(x, norm_ffn[l]) * (1.0 + scale_f) + shift_f
        u = causal_dwconv(h @ w_up[l], ffn_conv_w[l], ffn_conv_b[l])
        u_gate, u_val = jnp.split(u, 2, axis=-1)
        x = x + gate_f * ((jax.nn.silu(u_gate) * u_val) @ w_down[l])
    return x


DEPTH_2 = 2

CTX_LEN = 256
GRID_W = 64
N_MIXERS = 3
DA_HEADS = 8
DA_HEAD_DIM = 64
DA_V_DIM = 2 * DA_HEAD_DIM
ROPE_F = DA_HEAD_DIM // 4
ROPE_THETA = 10000.0
Q_BLOCK = 128
FN_GROUPS = 8
FN_GROUP_DIM = D_MODEL // FN_GROUPS
HY_ORDER = 2
HY_EMB = 33
HY_BANDS = (HY_EMB - 1) // 2
HY_FILTER_HIDDEN = 64
HY_SIN_FREQ = 1.0
HY_FAST_DECAY = 0.3
HY_SLOW_DECAY = 1.5
HY_TARGET = 1e-2
HY_MAX_DECAY = math.log(HY_TARGET) / HY_FAST_DECAY
HY_MIN_DECAY = math.log(HY_TARGET) / HY_SLOW_DECAY
D_FF_2 = 3584
N_EXPERTS = 8
TOP_K = 2
MOE_BLOCK = 128
EPS = 1e-6


def rms_norm_2(x, g):
    xf = x.astype(jnp.float32)
    y = xf * lax.rsqrt(jnp.mean(xf * xf, axis=-1, keepdims=True) + EPS)
    return (y * g.astype(jnp.float32)).astype(x.dtype)

def axial_rope(x, cos, sin):
    xr = x.reshape(x.shape[:-1] + (2, 2, ROPE_F))
    cs = cos[None, :, None, None].astype(x.dtype)
    sn = sin[None, :, None, None].astype(x.dtype)
    x1, x2 = xr[..., 0, :], xr[..., 1, :]
    out = jnp.stack([x1 * cs - x2 * sn, x2 * cs + x1 * sn], axis=-2)
    return out.reshape(x.shape)

def diff_attention(h_l, h_c, cos, sin, w_qkv, lq1, lk1, lq2, lk2, subln_g, w_o, lam_init, with_ctx):
    B, L, D = h_l.shape

    def project(h):
        n = h.shape[1]
        q, k, v = jnp.split(h @ w_qkv, 3, axis=-1)
        return (q.reshape(B, n, DA_HEADS, 2, DA_HEAD_DIM),
                k.reshape(B, n, DA_HEADS, 2, DA_HEAD_DIM),
                v.reshape(B, n, DA_HEADS, DA_V_DIM))

    q_l, k_l, v_l = project(h_l)
    q_c, k_c, v_c = project(h_c)
    q_l = axial_rope(q_l, cos, sin)
    k_l = axial_rope(k_l, cos, sin)
    f32 = jnp.float32
    lam = (jnp.exp(jnp.sum(lq1.astype(f32) * lk1.astype(f32)))
           - jnp.exp(jnp.sum(lq2.astype(f32) * lk2.astype(f32))) + lam_init)
    scale = DA_HEAD_DIM ** -0.5

    def attend(q, k, v):
        n = q.shape[1]
        s = jnp.einsum('bqhnd,bkhnd->bnhqk', q, k).astype(f32) * scale
        p = jax.nn.softmax(s, axis=-1)
        a = (p[:, 0] - lam * p[:, 1]).astype(v.dtype)
        o = jnp.einsum('bhqk,bkhe->bqhe', a, v)
        o = rms_norm_2(o, subln_g) * (1.0 - lam_init)
        return o.reshape(B, n, DA_HEADS * DA_V_DIM)

    k_all = jnp.concatenate([k_c, k_l], axis=1)
    v_all = jnp.concatenate([v_c, v_l], axis=1)
    qb = q_l.reshape(B, L // Q_BLOCK, Q_BLOCK, DA_HEADS, 2, DA_HEAD_DIM).swapaxes(0, 1)
    o_l = lax.map(lambda q: attend(q, k_all, v_all), qb)
    y_l = o_l.swapaxes(0, 1).reshape(B, L, -1) @ w_o
    y_c = attend(q_c, k_c, v_c) @ w_o if with_ctx else None
    return y_l, y_c

def fourier_mix(h, w_o, b_o):
    B, L, D = h.shape
    hg = h.astype(jnp.float32).reshape(B, L, FN_GROUPS, FN_GROUP_DIM)
    f = jnp.fft.fftn(hg, axes=(1, 3), norm='ortho').real
    return f.reshape(B, L, D).astype(h.dtype) @ w_o + b_o

def short_conv(u, w, b):
    up = jnp.pad(u, ((0, 0), (1, 1), (0, 0)))
    return up[:, :-2] * w[0] + up[:, 1:-1] * w[1] + up[:, 2:] * w[2] + b

def hyena_filters(L, f_w1, f_b1, f_w2, f_b2, f_w3):
    f32 = jnp.float32
    D = f_w3.shape[-1] // (2 * HY_ORDER)
    t01 = jnp.linspace(0.0, 1.0, L, dtype=f32)[:, None]
    w = 2.0 * math.pi * jnp.arange(L, dtype=f32) / L
    bands = jnp.linspace(1e-4, HY_BANDS - 1, HY_BANDS, dtype=f32)
    fw = w[:, None] * bands[None, :]
    emb = jnp.concatenate([t01, jnp.cos(fw), -jnp.sin(fw)], axis=-1)
    hdn = jnp.sin(HY_SIN_FREQ * (emb @ f_w1.astype(f32) + f_b1.astype(f32)))
    hdn = jnp.sin(HY_SIN_FREQ * (hdn @ f_w2.astype(f32) + f_b2.astype(f32)))
    filt = (hdn @ f_w3.astype(f32)).reshape(L, HY_ORDER, 2, D)
    deltas = jnp.abs(jnp.linspace(HY_MIN_DECAY, HY_MAX_DECAY, D, dtype=f32))
    decay = jnp.exp(-t01 * deltas[None, :])
    filt = filt * decay[:, None, None, :]
    fwd, bwd = filt[:, :, 0], filt[:, :, 1]
    two = jnp.concatenate([fwd, jnp.zeros((1, HY_ORDER, D), f32), bwd[1:][::-1]], axis=0)
    return jnp.fft.rfft(two, axis=0)

def hyena_mixer(h, w_in, conv_w, conv_b, f_w1, f_b1, f_w2, f_b2, f_w3, f_bias, w_o):
    L = h.shape[1]
    u = short_conv(h @ w_in, conv_w, conv_b)
    x1, x2, v = jnp.split(u, 3, axis=-1)
    kf = hyena_filters(L, f_w1, f_b1, f_w2, f_b2, f_w3)
    z = v
    for n, gate in enumerate((x1, x2)):
        zf = jnp.fft.rfft(z.astype(jnp.float32), n=2 * L, axis=1)
        y = jnp.fft.irfft(zf * kf[None, :, n], n=2 * L, axis=1)[:, :L]
        z = gate * (y.astype(h.dtype) + f_bias[n] * z)
    return z @ w_o

def swiglu(h, w1, w3, w2):
    return (jax.nn.silu(h @ w1) * (h @ w3)) @ w2

def moe_swiglu(h, router, w1, w3, w2):
    T, D = h.shape
    logits = (h @ router).astype(jnp.float32)
    top_v, top_i = lax.top_k(logits, TOP_K)
    gates = jax.nn.softmax(top_v, axis=-1).astype(h.dtype)
    flat_e = top_i.reshape(-1)
    flat_w = gates.reshape(-1)
    flat_tok = jnp.repeat(jnp.arange(T, dtype=jnp.int32), TOP_K)
    TK = T * TOP_K
    counts = jnp.bincount(flat_e, length=N_EXPERTS)
    padded = (counts + MOE_BLOCK - 1) // MOE_BLOCK * MOE_BLOCK
    pad_start = jnp.cumsum(padded) - padded
    start = jnp.cumsum(counts) - counts
    order = jnp.argsort(flat_e)
    se = flat_e[order]
    dest = pad_start[se] + jnp.arange(TK, dtype=jnp.int32) - start[se]
    n_blocks = -(-TK // MOE_BLOCK) + N_EXPERTS
    n_rows = n_blocks * MOE_BLOCK
    row_tok = jnp.full((n_rows,), T, jnp.int32).at[dest].set(flat_tok[order])
    row_w = jnp.zeros((n_rows,), h.dtype).at[dest].set(flat_w[order])
    block_start = jnp.arange(n_blocks, dtype=jnp.int32) * MOE_BLOCK
    block_e = jnp.minimum(jnp.searchsorted(jnp.cumsum(padded), block_start, side='right'), N_EXPERTS - 1)
    h_ext = jnp.concatenate([h, jnp.zeros((1, D), h.dtype)], axis=0)
    xb = h_ext[row_tok].reshape(n_blocks, MOE_BLOCK, D)

    def expert_block(args):
        xe, e = args
        return swiglu(xe, w1[e], w3[e], w2[e])

    yb = lax.map(expert_block, (xb, block_e))
    y = jnp.zeros((T + 1, D), h.dtype).at[row_tok].add(yb.reshape(n_rows, D) * row_w[:, None])
    return y[:T]

def second_inputs(seed: int = 0) -> dict:
    key = jax.random.key(seed)
    ks = iter(jax.random.split(key, 64))
    D = D_MODEL

    def nrm(shape, s):
        return jax.random.normal(next(ks), shape, jnp.float32) * s

    n_a = len(range(0, DEPTH_2, N_MIXERS))
    n_b = len(range(1, DEPTH_2, N_MIXERS))
    n_c = len(range(2, DEPTH_2, N_MIXERS))
    n_dense = len(range(0, DEPTH_2, 2))
    n_moe = len(range(1, DEPTH_2, 2))
    return {
        'x': nrm((BATCH, SEQ, D), 1.0),
        'c': nrm((BATCH, D), 1.0),
        'ctx': nrm((BATCH, CTX_LEN, D), 1.0),
        'c_ctx': nrm((D,), 1.0),
        'ada_w': nrm((DEPTH_2, D, 6 * D), 0.5 * D ** -0.5),
        'ada_b': nrm((DEPTH_2, 6 * D), 0.02),
        'norm1_g': 1.0 + nrm((DEPTH_2, D), 0.02),
        'norm2_g': 1.0 + nrm((DEPTH_2, D), 0.02),
        'attn_w_qkv': nrm((n_a, D, 3 * D), D ** -0.5),
        'attn_lq1': nrm((n_a, DA_HEAD_DIM), 0.1),
        'attn_lk1': nrm((n_a, DA_HEAD_DIM), 0.1),
        'attn_lq2': nrm((n_a, DA_HEAD_DIM), 0.1),
        'attn_lk2': nrm((n_a, DA_HEAD_DIM), 0.1),
        'attn_subln_g': 1.0 + nrm((n_a, DA_V_DIM), 0.02),
        'attn_w_o': nrm((n_a, D, D), D ** -0.5),
        'fnet_w_o': nrm((n_b, D, D), D ** -0.5),
        'fnet_b_o': nrm((n_b, D), 0.02),
        'hy_w_in': nrm((n_c, D, 3 * D), D ** -0.5),
        'hy_conv_w': nrm((n_c, 3, 3 * D), 0.5),
        'hy_conv_b': nrm((n_c, 3 * D), 0.02),
        'hy_f_w1': nrm((n_c, HY_EMB, HY_FILTER_HIDDEN), HY_EMB ** -0.5),
        'hy_f_b1': nrm((n_c, HY_FILTER_HIDDEN), 0.1),
        'hy_f_w2': nrm((n_c, HY_FILTER_HIDDEN, HY_FILTER_HIDDEN), HY_FILTER_HIDDEN ** -0.5),
        'hy_f_b2': nrm((n_c, HY_FILTER_HIDDEN), 0.1),
        'hy_f_w3': nrm((n_c, HY_FILTER_HIDDEN, HY_ORDER * 2 * D), 0.2 * HY_FILTER_HIDDEN ** -0.5),
        'hy_f_bias': nrm((n_c, HY_ORDER, D), 0.5),
        'hy_w_o': nrm((n_c, D, D), D ** -0.5),
        'ff_w1': nrm((n_dense, D, D_FF_2), D ** -0.5),
        'ff_w3': nrm((n_dense, D, D_FF_2), D ** -0.5),
        'ff_w2': nrm((n_dense, D_FF_2, D), D_FF_2 ** -0.5),
        'moe_router': nrm((n_moe, D, N_EXPERTS), D ** -0.5),
        'moe_w1': nrm((n_moe, N_EXPERTS, D, D_FF_2), D ** -0.5),
        'moe_w3': nrm((n_moe, N_EXPERTS, D, D_FF_2), D ** -0.5),
        'moe_w2': nrm((n_moe, N_EXPERTS, D_FF_2, D), D_FF_2 ** -0.5),
        'final_g': 1.0 + nrm((D,), 0.02),
    }

def second_block(x, c, ctx, c_ctx, ada_w, ada_b, norm1_g, norm2_g,
              attn_w_qkv, attn_lq1, attn_lk1, attn_lq2, attn_lk2, attn_subln_g, attn_w_o,
              fnet_w_o, fnet_b_o,
              hy_w_in, hy_conv_w, hy_conv_b, hy_f_w1, hy_f_b1, hy_f_w2, hy_f_b2, hy_f_w3, hy_f_bias, hy_w_o,
              ff_w1, ff_w3, ff_w2, moe_router, moe_w1, moe_w3, moe_w2, final_g):
    B, L, D = x.shape
    f32 = jnp.float32
    grid_rows = L // GRID_W
    row = jnp.repeat(jnp.arange(grid_rows, dtype=f32), GRID_W)
    col = jnp.tile(jnp.arange(GRID_W, dtype=f32), grid_rows)
    freqs = ROPE_THETA ** (-jnp.arange(ROPE_F, dtype=f32) / ROPE_F)
    ang = jnp.stack([row[:, None] * freqs, col[:, None] * freqs], axis=1)
    cos, sin = jnp.cos(ang), jnp.sin(ang)
    silu_c = jax.nn.silu(c)
    silu_cc = jax.nn.silu(c_ctx)

    for i in range(DEPTH_2):
        last = i == DEPTH_2 - 1
        kind, j = i % N_MIXERS, i // N_MIXERS
        mod_l = (silu_c @ ada_w[i] + ada_b[i])[:, None, :]
        mod_c = silu_cc @ ada_w[i] + ada_b[i]
        sh1_l, sc1_l, g1_l, sh2_l, sc2_l, g2_l = jnp.split(mod_l, 6, axis=-1)
        sh1_c, sc1_c, g1_c, sh2_c, sc2_c, g2_c = jnp.split(mod_c, 6, axis=-1)

        h_l = rms_norm_2(x, norm1_g[i]) * (1.0 + sc1_l) + sh1_l
        h_c = rms_norm_2(ctx, norm1_g[i]) * (1.0 + sc1_c) + sh1_c
        if kind == 0:
            y_l, y_c = diff_attention(h_l, h_c, cos, sin, attn_w_qkv[j], attn_lq1[j], attn_lk1[j],
                                      attn_lq2[j], attn_lk2[j], attn_subln_g[j], attn_w_o[j],
                                      0.8 - 0.6 * math.exp(-0.3 * i), not last)
        elif kind == 1:
            y_l = fourier_mix(h_l, fnet_w_o[j], fnet_b_o[j])
            y_c = None if last else fourier_mix(h_c, fnet_w_o[j], fnet_b_o[j])
        else:
            hp = (hy_w_in[j], hy_conv_w[j], hy_conv_b[j], hy_f_w1[j], hy_f_b1[j], hy_f_w2[j],
                  hy_f_b2[j], hy_f_w3[j], hy_f_bias[j], hy_w_o[j])
            y_l = hyena_mixer(h_l, *hp)
            y_c = None if last else hyena_mixer(h_c, *hp)
        x = x + g1_l * y_l
        if not last:
            ctx = ctx + g1_c * y_c

        h2_l = (rms_norm_2(x, norm2_g[i]) * (1.0 + sc2_l) + sh2_l).reshape(B * L, D)
        if last:
            tokens = h2_l
        else:
            h2_c = (rms_norm_2(ctx, norm2_g[i]) * (1.0 + sc2_c) + sh2_c).reshape(-1, D)
            tokens = jnp.concatenate([h2_l, h2_c], axis=0)
        if i % 2 == 0:
            k = i // 2
            f = swiglu(tokens, ff_w1[k], ff_w3[k], ff_w2[k])
        else:
            k = i // 2
            f = moe_swiglu(tokens, moe_router[k], moe_w1[k], moe_w3[k], moe_w2[k])
        x = x + g2_l * f[:B * L].reshape(B, L, D)
        if not last:
            ctx = ctx + g2_c * f[B * L:].reshape(B, -1, D)

    return rms_norm_2(x, final_g)


def setup_inputs(seed=0):
    out = dict(first_inputs(seed))
    for name, value in second_inputs(seed + 1).items():
        if name != "x":
            out[name + "_2"] = value
    return out


def reference(
    x, c, w_mod, b_mod, norm_mix, norm_ffn, w_in, qnorm_a, knorm_a, sinks, rnn_conv_w,
    rnn_conv_b, rnn_gate_a_w, rnn_gate_a_b, rnn_gate_x_w, rnn_gate_x_b, rnn_lambda, qnorm_c,
    knorm_c, rel_bias, w_branch, w_out, w_up, ffn_conv_w, ffn_conv_b, w_down, c_2, ctx_2,
    c_ctx_2, ada_w_2, ada_b_2, norm1_g_2, norm2_g_2, attn_w_qkv_2, attn_lq1_2, attn_lk1_2,
    attn_lq2_2, attn_lk2_2, attn_subln_g_2, attn_w_o_2, fnet_w_o_2, fnet_b_o_2, hy_w_in_2,
    hy_conv_w_2, hy_conv_b_2, hy_f_w1_2, hy_f_b1_2, hy_f_w2_2, hy_f_b2_2, hy_f_w3_2,
    hy_f_bias_2, hy_w_o_2, ff_w1_2, ff_w3_2, ff_w2_2, moe_router_2, moe_w1_2, moe_w3_2,
    moe_w2_2, final_g_2,
):
    x = first_block(
        x, c, w_mod, b_mod, norm_mix, norm_ffn, w_in, qnorm_a, knorm_a, sinks, rnn_conv_w,
        rnn_conv_b, rnn_gate_a_w, rnn_gate_a_b, rnn_gate_x_w, rnn_gate_x_b, rnn_lambda, qnorm_c,
        knorm_c, rel_bias, w_branch, w_out, w_up, ffn_conv_w, ffn_conv_b, w_down,
    )
    return second_block(
        x, c_2, ctx_2, c_ctx_2, ada_w_2, ada_b_2, norm1_g_2, norm2_g_2, attn_w_qkv_2,
        attn_lq1_2, attn_lk1_2, attn_lq2_2, attn_lk2_2, attn_subln_g_2, attn_w_o_2, fnet_w_o_2,
        fnet_b_o_2, hy_w_in_2, hy_conv_w_2, hy_conv_b_2, hy_f_w1_2, hy_f_b1_2, hy_f_w2_2,
        hy_f_b2_2, hy_f_w3_2, hy_f_bias_2, hy_w_o_2, ff_w1_2, ff_w3_2, ff_w2_2, moe_router_2,
        moe_w1_2, moe_w3_2, moe_w2_2, final_g_2,
    )


_drawn_inputs = setup_inputs


def setup_inputs(seed=0):
    import zlib

    import numpy as np

    out = dict(_drawn_inputs(seed))
    spreads = {}
    factors = {'norm_mix': 4.92,
     'norm_ffn': 2.797,
     'qnorm_a': 8.0,
     'knorm_a': 8.0,
     'sinks': 8.0,
     'rnn_conv_b': 7.89,
     'rnn_gate_a_b': 8.0,
     'rnn_gate_x_b': 8.0,
     'qnorm_c': 8.0,
     'knorm_c': 8.0,
     'ffn_conv_b': 5.825,
     'norm1_g_2': 8.0,
     'norm2_g_2': 3.003,
     'attn_lq1_2': 7.038,
     'attn_lk1_2': 8.0,
     'attn_subln_g_2': 6.664,
     'fnet_b_o_2': 4.639,
     'final_g_2': 2.834}
    for name, (base, spread) in spreads.items():
        noise = np.random.default_rng([zlib.crc32(name.encode()), seed]).standard_normal(out[name].shape)
        drawn = base * np.exp(spread * noise) if base else spread * noise
        out[name] = __import__('jax').numpy.asarray(drawn.astype(out[name].dtype))
    for name, factor in factors.items():
        out[name] = (out[name] * factor).astype(out[name].dtype)
    return out
```

```python
import math
from contextlib import ExitStack

import numpy as np
import concourse.bass as bass
from concourse import mybir
from concourse.alu_op_type import AluOpType as ALU

F = mybir.dt.float32
R = mybir.dt.float32r
I32 = mybir.dt.int32
ACT = mybir.ActivationFunctionType
AX = mybir.AxisListType.X

D = 1024
S = 256
EPS = 1e-6
NEG = -1e30
D_IN = 7424
FF1 = 2816
FF2 = 3584
NEXP = 8

NR = 5
NP = 3
LOOK = 2
CAP = 128

C_ID, C_BO, C_J, C_ROT = 0, 128, 256, 512
C_COS, C_SIN, C_FD, C_FL = 640, 896, 1152, 1408
C_OHA, C_OHC, C_TRI, C_IOTA, C_EIDX, C_ONE = 2432, 2816, 3200, 3328, 3456, 3464
C_END = 3592


def t5_bucket(d):
    d = max(d, 0)
    if d < 16:
        return d
    f = np.float32
    lr = np.log(f(d) / f(16)) / f(math.log(2048 / 16))
    return min(16 + int(f(lr * f(16))), 31)


def constants():
    c = np.zeros((128, C_END), np.float32)
    p = np.arange(128)
    c[:, C_ID:C_ID + 128] = np.eye(128)
    c[:, C_BO:C_BO + 128] = (p[:, None] // 64 == p[None, :] // 64)
    for m in range(128):
        half = (m // 16) % 2
        c[m + 16 if half == 0 else m - 16, C_ROT + m] = -1.0 if half == 0 else 1.0
    tok = np.arange(S, dtype=np.float32)
    row, col = np.floor(tok / 64), np.mod(tok, 64)
    freqs = (np.float32(10000.0) ** (-np.arange(16, dtype=np.float32) / np.float32(16))).astype(np.float32)
    for m in range(128):
        d = m % 64
        ang = (row if d < 32 else col) * freqs[d % 16]
        c[m, C_COS:C_COS + S] = np.cos(ang.astype(np.float32))
        c[m, C_SIN:C_SIN + S] = np.sin(ang.astype(np.float32))
    w = 2 * np.pi * np.outer(p, p) / 128
    c[:, C_FD:C_FD + 128] = np.cos(w) / math.sqrt(128)
    c[:, C_FD + 128:C_FD + 256] = np.sin(w) / math.sqrt(128)
    for tb in range(2):
        w = 2 * np.pi * np.outer(p + 128 * tb, np.arange(S)) / S
        c[:, C_FL + tb * 512:C_FL + tb * 512 + 256] = np.cos(w) / math.sqrt(S)
        c[:, C_FL + tb * 512 + 256:C_FL + tb * 512 + 512] = -np.sin(w) / math.sqrt(S)
    for t in range(384):
        diff = 255 - t
        b = t5_bucket(diff)
        c[b, C_OHA + t] = 1.0
        c[b, C_OHC + t] = 1.0
        c[32, C_OHA + t] = 0.0 if 0 <= diff < 128 else NEG
        c[32, C_OHC + t] = 0.0 if diff >= 0 else NEG
    c[:, C_TRI:C_TRI + 128] = (p[:, None] < p[None, :])
    c[:, C_IOTA:C_IOTA + 128] = p[None, :]
    c[:, C_EIDX:C_EIDX + 8] = 8 - np.arange(8)
    c[:, C_ONE:C_ONE + 128] = 1.0
    c[:, C_J:C_J + 128] = np.eye(128)[::-1]
    return c


class Queue:

    def __init__(self, eng, sem):
        self.eng, self.sem, self.n, self.seen = eng, sem, 0, {}

    def wait(self, *toks):
        for t in toks:
            if t is None:
                continue
            if isinstance(t, list):
                self.wait(*t)
                continue
            sem, val = t
            if self.seen.get(id(sem), 0) < val:
                self.seen[id(sem)] = val
                self.eng.wait_ge(sem, val)

    def do(self, fn, *toks):
        self.wait(*toks)
        self.n += 1
        fn(self.eng).then_inc(self.sem, 1)
        return (self.sem, self.n)

    def run(self, fn, *toks):
        self.wait(*toks)
        fn(self.eng)

    def now(self):
        return (self.sem, self.n)


class Slots:

    pump = None

    def __init__(self, bufs):
        self.bufs, self.free, self.order = bufs, [[] for _ in bufs], list(range(len(bufs)))

    def busy(self):
        return not self.order

    def get(self):
        while self.busy() and Slots.pump():
            pass
        assert self.order, "every slot is in use"
        k = self.order.pop(0)
        return k, self.bufs[k], self.free[k]

    def put(self, k, *toks):
        assert k not in self.order
        self.free[k] = list(toks)
        self.order.append(k)


def build(nc, a, out, dbg=None):
    ctx = ExitStack()
    dbg = dbg or {}

    def sb(name, shape, dt=F, c=ctx):
        return c.enter_context(nc.sbuf_tensor(name, shape, dt))

    def sem(name):
        return ctx.enter_context(nc.semaphore(name))

    with ctx:
        pe, act, dve, pool, sp = (Queue(g, sem("s_" + n)) for n, g in (
            ("pe", nc.tensor), ("act", nc.scalar), ("dve", nc.vector), ("pool", nc.gpsimd), ("sp", nc.sync)))

        def fence():
            return [pe.now(), act.now(), dve.now(), pool.now()]

        raw = [sb(f"raw{i}", [128, 2048]) for i in range(NR)]
        whi = [sb(f"whi{i}", [128, 2048], R) for i in range(NP)]
        wlo = [sb(f"wlo{i}", [128, 2048], R) for i in range(NP)]
        X = sb("X", [128, 8, S])
        cst = sb("cst", [128, 384])
        one = sb("one", [128, 128])
        vt = [sb(f"vt{i}", [128, 128]) for i in range(4)]
        modT = [sb("mod_m", [128, 48]), sb("mod_a0", [128, 48]), sb("mod_c0", [128, 16]), sb("mod_a1", [128, 48])]
        macc = [sb(f"macc{i}", [128, 512]) for i in range(3)]
        csil = sb("csil", [128, 24])
        nA = sb("nA", [128, 64])
        sqb = [sb(f"sqb{i}", [128, S]) for i in range(2)]
        rst = [sb(f"rst{i}", [128, S]) for i in range(2)]
        banks = [ctx.enter_context(nc.psum_tensor(f"bk{i}", [128, 512], F)) for i in range(8)]
        PG = Slots(banks[0:4])
        PT = Slots(banks[4:8])
        MA = Slots(macc)
        SQ = Slots(sqb)
        RS = Slots(rst)
        s_raw = [sem(f"s_raw{i}") for i in range(NR)]
        ident, bones, JJ = cst[:, C_ID:C_ID + 128], cst[:, C_BO:C_BO + 128], cst[:, C_J:C_J + 128]

        dma_sems = {}

        def load(name, pairs, *toks, q=pool):
            s = dma_sems.setdefault(name, [None, 0])
            if s[0] is None:
                s[0] = sem("d_" + name)
            q.wait(*toks)
            for o, i in pairs:
                s[1] += 16
                q.eng.dma_start(o, i).then_inc(s[0], 16)
            return (s[0], s[1])

        plan = []

        def gslabs(w, kts, c0, tag):
            r = []
            for k0 in range(0, kts, 8):
                nk = min(8, kts - k0)
                src = w[k0 * 128:(k0 + nk) * 128, c0:c0 + 256].rearrange("(k p) n -> p k n", p=128)
                r.append(("G", tag, src, nk, 256))
            return r

        def mslabs(w, g, which):
            return [("M", (which, g, k0), w[k0 * 512:(k0 + 1) * 512, g * 512:(g + 1) * 512]
                     .rearrange("(k p) n -> p k n", p=128), 4, 512) for k0 in range(2)]

        def mix(gs, ms):
            o, j = [], 0
            for i, g in enumerate(gs):
                o.append(g)
                while j < len(ms) and j < (i + 1) * len(ms) / len(gs):
                    o.append(ms[j])
                    j += 1
            return o + ms[j:]

        wmod, ada = a["w_mod"][0], a["ada_w_2"]
        win, wbr, wout, wup, wdn = a["w_in"][0], a["w_branch"][0], a["w_out"][0], a["w_up"][0], a["w_down"][0]
        wqkv, wo2, fwo = a["attn_w_qkv_2"][0], a["attn_w_o_2"][0], a["fnet_w_o_2"][0]
        f1, f3, f2 = a["ff_w1_2"][0], a["ff_w3_2"][0], a["ff_w2_2"][0]
        z_cols = [0, 256, 512, 2816, 3072, 3328, 3584, 3840, 4096]
        for j in range(4):
            z_cols += [768 + 256 * j, 1792 + 256 * j]
        z_cols += [4352 + 256 * j for j in range(12)]
        for g in range(4):
            plan += mslabs(wmod, g, 0)
        zs = [s for c in z_cols for s in gslabs(win, 8, c, ("z", c))]
        plan += mix(zs, [s for g in range(4, 12) for s in mslabs(wmod, g, 0)])
        bs = [s for c in range(4) for s in gslabs(wbr, 16, 256 * c, ("br", c))]
        bs += [s for c in range(4) for s in gslabs(wout, 8, 256 * c, ("out", c))]
        us = [s for c in range(11) for s in gslabs(wup, 8, 256 * c, ("ug", c)) + gslabs(wup, 8, FF1 + 256 * c, ("uv", c))]
        us += [s for c in range(4) for s in gslabs(wdn, 22, 256 * c, ("dn", c))]
        plan += mix(bs + us, [s for g in range(12) for s in mslabs(ada[0], g, 1)])
        q2 = [s for c in range(12) for s in gslabs(wqkv, 8, 256 * c, ("qkv", c))]
        q2 += [s for c in range(4) for s in gslabs(wo2, 8, 256 * c, ("wo", c))]
        q2 += [s for c in range(14) for s in gslabs(f1, 8, 256 * c, ("f1", c)) + gslabs(f3, 8, 256 * c, ("f3", c))]
        q2 += [s for c in range(4) for s in gslabs(f2, 28, 256 * c, ("f2", c))]
        plan += mix(q2, [s for g in range(12) for s in mslabs(ada[1], g, 3)])
        plan += [s for c in range(4) for s in gslabs(fwo, 8, 256 * c, ("fn", c))]

        def eslabs(e, n):
            r = []
            for tag, w in (("w1", a["moe_w1_2"][0, e]), ("w3", a["moe_w3_2"][0, e])):
                for k0 in range(2):
                    r.append(("G", (tag, e, n, k0), w[k0 * 512:(k0 + 1) * 512, n * 512:(n + 1) * 512]
                              .rearrange("(k p) n -> p k n", p=128), 4, 512))
            return r

        def dslabs(e, n):
            w = a["moe_w2_2"][0, e]
            return [("G", ("w2", e, n, j), w[n * 512 + j * 256:n * 512 + (j + 1) * 256, :]
                     .rearrange("(k p) n -> p k n", p=128), 2, 1024) for j in range(2)]

        steps = [(e, n) for e in range(NEXP) for n in range(7)]
        for i, (e, n) in enumerate(steps):
            plan += eslabs(e, n)
            if i:
                plan += dslabs(*steps[i - 1])
        plan += dslabs(*steps[-1])
        if "cut" in dbg:
            plan = plan[:dbg["cut"](plan)]

        raw_i = [0]

        def raw_view(i):
            _, _, src, nk, nc_ = plan[i]
            return raw[i % NR][:, :nk * nc_].rearrange("p (k n) -> p k n", k=nk)

        raw_free = {}

        def issue(i):
            if i >= len(plan):
                return
            sp.wait(raw_free.get(i - NR))
            dst, src, s = raw_view(i), plan[i][2], s_raw[i % NR]
            sp.eng.dma_start(dst, src).then_inc(s, 16)

        for i in range(NR):
            issue(i)

        def arrived(i):
            return (s_raw[i % NR], 16 * (i // NR + 1))

        pair_free = [[] for _ in range(NP)]
        pair_of, gcount = {}, [0]
        pair_tok = {}
        pos, ahead = [0], [0]
        mstate = {}

        def prepare(i):
            kind, tag, src, nk, w = plan[i]
            if kind == "G":
                k = gcount[0] % NP
                gcount[0] += 1
                assert pair_free[k] is not None
                n = nk * w
                r, h, l = raw[i % NR][:, :n], whi[k][:, :n], wlo[k][:, :n]
                th = act.do(lambda e: e.copy(h, r), arrived(i), pair_free[k])
                tl = dve.do(lambda e: e.tensor_tensor(l, r, h.bitcast(F), ALU.subtract), arrived(i), th, pair_free[k])
                pair_free[k] = None
                pair_of[i], pair_tok[i] = k, [th, tl]
                raw_free[i] = [th, tl]
            else:
                which, g, k0 = tag
                v = raw_view(i)
                cs = [(which, {0: 0, 1: 8, 3: 8}[which])]
                if which == 1 and g < 4:
                    cs.append((2, 16))
                toks = []
                for dest, c0 in cs:
                    if k0 == 0:
                        kk, acc, fr = MA.get()
                        mstate[dest, g] = [kk, acc, fr]
                    kk, acc, t = mstate[dest, g]
                    for j in range(4):
                        sc = csil[:, c0 + k0 * 4 + j:c0 + k0 * 4 + j + 1]
                        if k0 == 0 and j == 0:
                            t = dve.do(lambda e, sc=sc, acc=acc: e.tensor_scalar(acc[:, :], v[:, 0, :], sc, None, ALU.mult),
                                       arrived(i), t, csil_tok)
                        else:
                            t = dve.do(lambda e, sc=sc, acc=acc, j=j: e.scalar_tensor_tensor(
                                out=acc[:, :], in0=v[:, j, :], scalar=sc, in1=acc[:, :], op0=ALU.mult, op1=ALU.add),
                                arrived(i), t)
                    mstate[dest, g][2] = t
                    toks.append(t)
                raw_free[i] = toks
            issue(i + NR)

        mod_tok = {}

        def reduce_mod(i):
            which, g, k0 = plan[i][1]
            if k0 == 0:
                return
            for dest in [which] + ([2] if which == 1 and g < 4 else []):
                kk, acc, t = mstate.pop((dest, g))
                b, bank, fr = PT.get()
                for j in range(4):
                    f = lambda e, j=j, acc=acc, bank=bank: e.matmul(bank[:, j:j + 1], acc[:, j * 128:(j + 1) * 128],
                                                                    one[:, 0:1], start=True, stop=True)
                    if j < 3:
                        pe.run(f, t, fr)
                    else:
                        tp = pe.do(f)
                MA.put(kk, tp)
                bias = {0: vec("b_mod"), 1: vec("ada_b0"), 2: vec("ada_b0"), 3: vec("ada_b1")}[dest]
                td = dve.do(lambda e, g=g, bank=bank, dest=dest: e.tensor_tensor(
                    modT[dest][:, 4 * g:4 * g + 4], bank[:, 0:4], bias[:, 4 * g:4 * g + 4], ALU.add), tp, vec_tok)
                PT.put(b, td)
                mod_tok[dest, g] = td

        def advance(n):
            while ahead[0] < min(n, len(plan)):
                prepare(ahead[0])
                ahead[0] += 1

        def skip_mods():
            while pos[0] < len(plan) and plan[pos[0]][0] == "M":
                advance(pos[0] + 1 + LOOK)
                reduce_mod(pos[0])
                pos[0] += 1

        def take(tag):
            skip_mods()
            i = pos[0]
            assert plan[i][1] == tag, (plan[i][1], tag)
            advance(i + 1)
            k = pair_of[i]
            pe.wait(pair_tok[i])
            nk, w = plan[i][3], plan[i][4]
            h = whi[k][:, :nk * w].rearrange("p (k n) -> p k n", k=nk)
            l = wlo[k][:, :nk * w].rearrange("p (k n) -> p k n", k=nk)
            pos[0] += 1
            return i, h, l, nk

        def done(i, tok):
            pair_free[pair_of[i]] = [tok]
            advance(i + 1 + LOOK)
            skip_mods()

        live, pending = [], []
        LIMIT = [2]

        running = [False]

        def pump():
            if running[0] or not (live or pending):
                return False
            tick()
            return True

        Slots.pump = pump

        def tick():
            running[0] = True
            step()
            running[0] = False

        def step():
            while pending and len(live) < LIMIT[0]:
                live.append(pending.pop(0))
            for g in list(live):
                try:
                    next(g)
                except StopIteration:
                    live.remove(g)

        def drain():
            while live or pending:
                tick()

        def now(g):
            for _ in g:
                pass

        def mm3(outp, wh, wl, xh, xl, first, last, **kw):
            seq = [(wh, xh), (wh, xl), (wl, xh)]
            for n, (l, r) in enumerate(seq):
                st, sp_ = first and n == 0, last and n == 2
                pe.run(lambda e, l=l, r=r, st=st, sp_=sp_: e.matmul(outp, l, r, start=st, stop=sp_, **kw))

        def mark(fn, *t):
            return pe.do(fn, *t)

        def gemmT(tags_kts, xh, xl, xt, evac, n=S):
            k_all = sum(k for _, k in tags_kts)
            pe.wait(xt)
            b, bank, fr = PG.get()
            pe.wait(fr)
            if n == 512:
                b2, bank2, fr2 = PG.get()
                pe.wait(fr2)
            kb = 0
            for tag, _ in tags_kts:
                i, h, l, nk = take(tag)
                for m in range(2):
                    for k in range(nk):
                        kk = kb + k
                        if n == 512:
                            o = (bank, bank2)[m][:, :]
                        else:
                            o = bank[:, m * S:(m + 1) * S]
                        seq = [(h, xh), (h, xl), (l, xh)]
                        for q, (w, xx) in enumerate(seq):
                            st = kk == 0 and q == 0 and (m == 0 or n == 512)
                            sp_ = kk == k_all - 1 and q == 2
                            lastone = m == 1 and k == nk - 1 and q == 2
                            f = lambda e, w=w, xx=xx, k=k, kk=kk, m=m, st=st, sp_=sp_, o=o: e.matmul(
                                o, w[:, k, m * 128:(m + 1) * 128], xx[:, kk, :], start=st, stop=sp_,
                                skip_group_check=True)
                            if lastone:
                                t = pe.do(f)
                            else:
                                pe.run(f)
                kb += nk
                done(i, t)
            if n == 512:
                r1, r2 = evac((bank, bank2), t)
                PG.put(b, *r1)
                PG.put(b2, *r2)
            else:
                PG.put(b, *evac(bank, t))
            tick()

        def mm32(o, l, r, st=True, sp_=True, *t):
            return pe.do(lambda e: e.matmul(o, l, r, start=st, stop=sp_), *t)

        vrows = {}
        vlist = [[("norm_mix", a["norm_mix"], 8), ("norm_ffn", a["norm_ffn"], 8), ("b_mod", a["b_mod"], 48),
                  ("rcb", a["rnn_conv_b"], 8), ("rcw", a["rnn_conv_w"], 32), ("gab", a["rnn_gate_a_b"], 8),
                  ("gxb", a["rnn_gate_x_b"], 8), ("lam", a["rnn_lambda"], 8)],
                 [("ada_b0", a["ada_b_2"][0:1], 48), ("ada_b1", a["ada_b_2"][1:2], 48),
                  ("n10", a["norm1_g_2"][0:1], 8), ("n11", a["norm1_g_2"][1:2], 8),
                  ("n20", a["norm2_g_2"][0:1], 8), ("n21", a["norm2_g_2"][1:2], 8)],
                 [("fcw01", a["ffn_conv_w"][:, 0:2, :], 88), ("c", a["c"], 8), ("c2", a["c_2"], 8),
                  ("cc", a["c_ctx_2"].rearrange("(o d) -> o d", o=1), 8), ("fbo", a["fnet_b_o_2"], 8),
                  ("fing", a["final_g_2"].rearrange("(o d) -> o d", o=1), 8)],
                 [("fcw2", a["ffn_conv_w"][:, 2:3, :], 44), ("fcb", a["ffn_conv_b"], 44), ("sub", a["attn_subln_g_2"], 1),
                  ("qa", a["qnorm_a"], 0), ("ka", a["knorm_a"], 0), ("qc", a["qnorm_c"], 0), ("kc", a["knorm_c"], 0)]]

        with ExitStack() as c0:
            vn = [sb(f"vn{i}", [128, 128], F, c0) for i in range(4)]
            rnat = sb("rnat", [64, 16], F, c0)
            rows = sb("rrow", [16, 384], F, c0)
            oh = sb("oh", [64, 768], F, c0)
            bias_dram = nc.dram_tensor("bias_rows", (16, 384), F, kind="Internal")
            t_c = load("cst", [(cst[:, :], a["consts"][:, 0:384]), (one[:, :], a["consts"][:, C_ONE:C_ONE + 128])])
            pairs = []
            t_ms = [pool.do(lambda e, i=i: e.memset(vn[i][:, :], 0.0)) for i in range(4)]
            for ti, vl in enumerate(vlist):
                r0 = 0
                for name, ap, n in vl:
                    vrows[name] = (ti, r0, max(n, 1))
                    if n == 0:
                        for hh_ in range(2):
                            pairs.append((vn[ti][r0:r0 + 1, hh_ * 64:hh_ * 64 + 64], ap))
                        r0 += 1
                        continue
                    flat = ap
                    while len(flat.shape) > 2:
                        flat = flat.rearrange("a b c -> a (b c)")
                    pairs.append((vn[ti][r0:r0 + n, :], flat.rearrange("o (n p) -> (o n) p", p=128)))
                    r0 += n
                assert r0 <= 128
            t_v = load("vec", pairs, t_ms)
            t_r = load("rel", [(rnat[0:32, :], a["rel_bias"]), (oh[0:33, :], a["consts"][0:33, C_OHA:C_OHA + 768])])
            t_r1 = pool.do(lambda e: e.memset(rnat[32:64, :], 1.0))
            b, bank, fr = PT.get()
            for i in range(4):
                t = pe.do(lambda e, i=i: e.transpose(bank[:, i * 128:(i + 1) * 128], vn[i][:, :], ident), fr, t_v, t_c)
            for i in range(4):
                vec_tok = dve.do(lambda e, i=i: e.tensor_copy(vt[i][:, :], bank[:, i * 128:(i + 1) * 128]), t)
            PT.put(b, vec_tok)

            def vec(name):
                ti, r0, n = vrows[name]
                return vt[ti][:, r0:r0 + n]

            for j, nm in enumerate(("c", "c2", "cc")):
                csil_tok = act.do(lambda e, nm=nm, j=j: e.activation(csil[:, 8 * j:8 * j + 8], vec(nm), ACT.Silu), vec_tok)
            b, bank, fr = PT.get()
            b2, bank2, fr2 = PT.get()
            t1 = pe.do(lambda e: e.matmul(bank[0:16, 0:384], rnat[0:33, :], oh[0:33, 0:384], start=True, stop=True),
                       fr, t_r, t_r1)
            t2 = pe.do(lambda e: e.matmul(bank2[0:16, 0:384], rnat[0:33, :], oh[0:33, 384:768], start=True, stop=True), fr2)
            rows2 = sb("rrow2", [16, 384], F, c0)
            ta = dve.do(lambda e: e.tensor_scalar(rows[:, :], bank[0:16, 0:384], 8.0, None, ALU.mult), t1)
            tb = dve.do(lambda e: e.tensor_scalar(rows2[:, :], bank2[0:16, 0:384], 8.0, None, ALU.mult), t2)
            PT.put(b, ta)
            PT.put(b2, tb)
            t_bias = load("brow", [(bias_dram[0:8, :], rows[0:8, :]), (bias_dram[8:16, :], rows2[8:16, :])], ta, tb)

            xn = sb("xn", [128, 2, 1024], F, c0)
            t_x = load("xn", [(xn[:, tb_, :], a["x"][0, tb_ * 128:(tb_ + 1) * 128, :]) for tb_ in range(2)])
            x_tok = []

            def transpose_in(src, t_src, dst, toks=()):
                r = []
                for c in range(0, 8, 2):
                    b, bank, fr = PT.get()
                    for m in range(2):
                        for tb_ in range(2):
                            t = pe.do(lambda e, m=m, tb_=tb_, c=c, bank=bank: e.transpose(
                                bank[:, m * 256 + tb_ * 128:m * 256 + tb_ * 128 + 128],
                                src[:, tb_, (c + m) * 128:(c + m + 1) * 128], ident), fr, t_src, t_c)
                    tt = dve.do(lambda e, c=c, bank=bank: e.tensor_copy(
                        dst[:, c:c + 2, :], bank[:, :].rearrange("p (m t) -> p m t", m=2)), t, *toks)
                    PT.put(b, tt)
                    r.append(tt)
                return r
            x_tok = transpose_in(xn, t_x, X)
            init_fence = fence() + [t_bias]

        def rstd_T(src, nch, toks, width, lhs=None, npart=128):
            b, bank, fr = PT.get()
            pe.wait(fr)
            for c in range(nch):
                k, sq, fs = SQ.get()
                t = act.do(lambda e, c=c, sq=sq: e.activation(sq[:, :], src[:, c, :], ACT.Square), toks, fs)
                tp = pe.do(lambda e, c=c, sq=sq: e.matmul(bank[:, 0:S], one[:, :] if lhs is None else lhs,
                                                          sq[:, :], start=(c == 0), stop=(c == nch - 1)), t, t_c)
                SQ.put(k, tp)
            k, r, fr = RS.get()
            t = act.do(lambda e: e.activation(r[:, :], bank[:, 0:S], ACT.Ln, bias=eps_c[:, 0:1], scale=1.0 / width), tp, fr, t_eps)
            PT.put(b, t)
            t = act.do(lambda e: e.activation(r[:, :], r[:, :], ACT.Exp, scale=-0.5), t)
            return k, r, t

        def split(dst_h, dst_l, src, toks, wfree=None):
            th = act.do(lambda e: e.copy(dst_h, src), toks, wfree)
            return [th, dve.do(lambda e: e.tensor_tensor(dst_l, src, dst_h.bitcast(F), ALU.subtract), toks, wfree, th)]

        def coeff(col, g, scale, mt):
            o = nA[:, col:col + 8]
            return o, dve.do(lambda e: e.scalar_tensor_tensor(out=o, in0=scale, scalar=1.0, in1=g, op0=ALU.add, op1=ALU.mult), mt, vec_tok)

        eps_c = sb("eps_c", [128, 1])
        t_eps = pool.do(lambda e: e.memset(eps_c[:, :], EPS))
        tmp = [sb(f"tmpn{i}", [128, S]) for i in range(2)]
        TM = Slots(tmp)

        def modulate(x, xtoks, A, At, shift, st, hh, hl, wfree, sl=slice(0, S)):
            k, r, t = rstd_T(x, 8, xtoks, D)
            toks = []
            for c in range(8):
                kt, tt, ft = TM.get()
                t1 = dve.do(lambda e, c=c, tt=tt: e.scalar_tensor_tensor(out=tt[:, :], in0=x[:, c, :], scalar=A[:, c:c + 1],
                                                                         in1=r[:, :], op0=ALU.mult, op1=ALU.mult), t, At, ft)
                t2 = act.do(lambda e, c=c, tt=tt: e.activation(hh[:, c, sl], tt[:, :], ACT.Identity, bias=shift[:, c:c + 1]),
                            t1, st, wfree)
                t3 = dve.do(lambda e, c=c, tt=tt: e.scalar_tensor_tensor(out=hl[:, c, sl], in0=tt[:, :], scalar=shift[:, c:c + 1],
                                                                         in1=hh[:, c, sl].bitcast(F), op0=ALU.add, op1=ALU.subtract), t2, wfree)
                TM.put(kt, t3)
                toks = [t2, t3]
            RS.put(k, t3)
            return toks

        c1 = ctx.enter_context(ExitStack())
        HH, HL = sb("HH", [128, 8, S], R, c1), sb("HL", [128, 8, S], R, c1)
        OH, OL = sb("OH", [128, 16, S], R, c1), sb("OL", [128, 16, S], R, c1)
        o_tok = [None] * 16
        c2 = ctx.enter_context(ExitStack())
        QA = sb("QA", [128, 4, S], F, c2)
        KA = sb("KA", [128, 2, S], F, c2)
        QC, KC = sb("QC", [128, 4, S], F, c2), sb("KC", [128, 4, S], F, c2)
        VA, VC = sb("VA", [128, 2, 128], F, c2), sb("VC", [128, 2, 512], F, c2)
        BI = Slots([sb(f"bi{i}", [128, S], F, c2) for i in range(2)])
        SS = Slots([sb(f"ss{i}", [128, S], F, c2) for i in range(2)])
        PTB = Slots([sb(f"ptb{i}", [128, 384], F, c2) for i in range(2)])
        st8 = Slots([sb(f"st{i}", [128, 8], F, c2) for i in range(3)])
        ZT = Slots([sb(f"zt{i}", [128, 512], F, c2) for i in range(2)])
        snk = sb("snk", [128, 8], F, c2)
        GW = Slots([sb(f"gw{i}", [128, 2, 2, 128], F, c2) for i in range(2)])
        clam = sb("clam", [128, 48], F, c2)
        RT = [sb(f"rt{i}", [128, 2, S], F, c2) for i in range(5)]
        xpad = sb("xpad", [128, 2, S + 3], F, c2)
        t_snk = load("snk", [(snk[:, :], a["sinks"].broadcast_to([128, 8]))], init_fence)
        t_m = [pool.do(lambda e, w=w: e.memset(w[:, :, :, :], 0.0), init_fence) for w in GW.bufs]
        gsrc = [w.rearrange("(m two) c d -> two c m d", two=2) for w in (a["rnn_gate_a_w"][0], a["rnn_gate_x_w"][0])]

        def load_gates(j):
            k, gw, fr = GW.get()
            prs = [(gw[two * 64:two * 64 + 64, w, :, two * 64:two * 64 + 64], gsrc[w][two][:, 2 * j:2 * j + 2, :])
                   for w in range(2) for two in range(2)]
            return k, gw, load(f"gw{k}", prs, t_m, fr)

        L = vec("lam")
        cl = lambda i: clam[:, 8 * i:8 * i + 8]
        t = dve.do(lambda e: e.tensor_scalar(cl(1), L, -1.0, None, ALU.mult), vec_tok, init_fence)
        t = dve.do(lambda e: e.tensor_tensor(cl(1), cl(1), L, ALU.min), t)
        t = act.do(lambda e: e.activation(cl(2), cl(1), ACT.Exp), t)
        t = dve.do(lambda e: e.tensor_scalar(cl(3), cl(2), 1.0, None, ALU.add), t)
        ta = act.do(lambda e: e.activation(cl(4), cl(3), ACT.Ln), t)
        t = dve.do(lambda e: e.tensor_scalar(cl(3), cl(3), -1.0, None, ALU.add), ta)
        t = dve.do(lambda e: e.tensor_scalar(cl(5), cl(3), 0.0, None, ALU.is_equal), t)
        t = dve.do(lambda e: e.tensor_tensor(cl(4), cl(4), cl(2), ALU.mult), ta, t)
        t = dve.do(lambda e: e.tensor_tensor(cl(2), cl(2), cl(5), ALU.mult), t)
        t = dve.do(lambda e: e.tensor_tensor(cl(3), cl(3), cl(5), ALU.add), t)
        t = dve.do(lambda e: e.reciprocal(cl(3), cl(3)), t)
        t = dve.do(lambda e: e.tensor_tensor(cl(4), cl(4), cl(3), ALU.mult), t)
        t = dve.do(lambda e: e.tensor_tensor(cl(4), cl(4), cl(2), ALU.add), t)
        t = dve.do(lambda e: e.tensor_scalar(cl(5), L, -1.0, 0.0, ALU.mult, ALU.max), t)
        t = dve.do(lambda e: e.tensor_tensor(cl(4), cl(4), cl(5), ALU.add), t)
        t_lam = dve.do(lambda e: e.tensor_scalar(cl(0), cl(4), -8.0, None, ALU.mult), t)

        skip_mods()
        A0, At0 = coeff(0, vec("norm_mix"), modT[0][:, 8:16], mod_tok[0, 3])
        h_tok = modulate(X, x_tok, A0, At0, modT[0][:, 0:8], mod_tok[0, 1], HH, HL, init_fence)

        z_ready = {}

        def norm_heads(dst, gains, key):
            def ev(bank, tok):
                k, z, fz = ZT.get()
                zz = z[:, :].rearrange("p (m t) -> p m t", m=2)
                tz = act.do(lambda e: e.copy(z[:, :], bank[:, :]), tok, fz)

                def rest():
                    yield
                    for m in range(2):
                        if dst[m] is None:
                            continue
                        kr, r, tr = rstd_T(zz[:, m:m + 1, :], 1, tz, 64, lhs=bones)
                        yield
                        td = dve.do(lambda e, m=m: e.scalar_tensor_tensor(out=dst[m], in0=zz[:, m, :], scalar=gains,
                                                                          in1=r[:, :], op0=ALU.mult, op1=ALU.mult), tr, vec_tok, init_fence)
                        RS.put(kr, td)
                        z_ready.setdefault(key, []).append(td)
                    ZT.put(k, td)
                pending.append(rest())
                return [tz]
            return ev

        LIMIT[0] = 1
        for j in range(2):
            gemmT([(("z", 256 * j), 8)], HH, HL, h_tok, norm_heads([QA[:, 2 * j, :], QA[:, 2 * j + 1, :]], vec("qa"), "qa"))

        i, h, l, nk = take(("z", 512))
        b, bank, fr = PG.get()
        b2, bank2, fr2 = PG.get()
        pe.wait(fr, fr2)
        for k in range(8):
            for q, (w, xx) in enumerate([(h, HH), (h, HL), (l, HH)]):
                pe.run(lambda e, w=w, xx=xx, k=k, q=q: e.matmul(bank[:, 0:S], w[:, k, 0:128], xx[:, k, :],
                                                                 start=(k == 0 and q == 0), stop=(k == 7 and q == 2)))

        def natural(bankx, h, l, hi, lo, tbs, nks=8, cols=256):
            for n, tb_ in enumerate(tbs):
                for k in range(nks):
                    for q, (xx, w) in enumerate([(hi, h), (lo, h), (hi, l)]):
                        f = lambda e, w=w, xx=xx, k=k, q=q, n=n, tb_=tb_: e.matmul(
                            bankx[:, n * 256:n * 256 + cols], xx[:, k, tb_ * 128:(tb_ + 1) * 128], w[:, k, 0:cols],
                            start=(k == 0 and q == 0), stop=(k == nks - 1 and q == 2))
                        if n == len(tbs) - 1 and k == nks - 1 and q == 2:
                            return pe.do(f)
                        pe.run(f)

        t = natural(bank2, h, l, HH, HL, [0, 1])
        done(i, t)
        kz, z, fz = ZT.get()
        tz = act.do(lambda e: e.copy(z[:, 0:S], bank[:, 0:S]), t, fz)
        PG.put(b, tz)
        t_va = act.do(lambda e: e.copy(VA[:, :, :], bank2[:, :].rearrange("p (b n) -> p b n", b=2)[:, :, 128:256]), t, init_fence)
        PG.put(b2, t_va)

        def ka_rest():
            kr, r, tr = rstd_T(z[:, 0:S].rearrange("p (m t) -> p m t", m=1), 1, tz, 64, lhs=bones)
            yield
            td = dve.do(lambda e: e.scalar_tensor_tensor(out=z[:, S:2 * S], in0=z[:, 0:S], scalar=vec("ka"), in1=r[:, :],
                                                         op0=ALU.mult, op1=ALU.mult), tr, vec_tok)
            RS.put(kr, td)
            yield
            b, bank, fr = PT.get()
            for j in range(2):
                for r0 in (0, 64):
                    t = pe.do(lambda e: e.matmul(bank[r0:r0 + 64, j * S:(j + 1) * S], ident[:, 64 * j:64 * j + 64],
                                                 z[:, S:2 * S], start=True, stop=True), fr, td)
            t = act.do(lambda e: e.copy(KA[:, :, :], bank[:, :].rearrange("p (m t) -> p m t", m=2)), t, init_fence)
            PT.put(b, t)
            ZT.put(kz, t)
            z_ready["ka"] = [t]
        pending.append(ka_rest())
        tick()

        def attention(h, q, k, v, toks, och, swa):
            while BI.busy() or PTB.busy():
                yield
            kb, bi, fb = BI.get()
            src = bass.AP(bias_dram, h * 384, [[1, 128], [1, 256]])
            t_b = load("bi%d" % kb, [(bi[:, :], src)], fb, t_bias, init_fence)
            kp, pt, fp = PTB.get()
            for qb in (0, 1):
                nk = 128 + 128 * qb
                b, bank, fr = PT.get()
                pe.do(lambda e: e.matmul(bank[:, 0:nk], q[:, qb * 128:qb * 128 + 128], k[:, 0:nk], start=True, stop=False), fr, toks)
                t = pe.do(lambda e: e.matmul(bank[:, 0:nk], JJ[:, :], bi[:, 256 - nk:256], start=False, stop=True), t_b, t_snk)
                yield
                while SS.busy() or st8.busy():
                    yield
                ks, s, fs = SS.get()
                kq, st, fq = st8.get()
                t1 = dve.do(lambda e: e.tensor_reduce(st[:, 5:6], bank[:, 0:nk], AX, ALU.max), t, fq, init_fence)
                t1 = dve.do(lambda e: e.tensor_scalar(st[:, 0:1], st[:, 5:6], 0.125, None, ALU.mult), t1)
                if swa:
                    t1 = dve.do(lambda e: e.tensor_tensor(st[:, 0:1], st[:, 0:1], snk[:, h:h + 1], ALU.max), t1, t_snk)
                t1 = dve.do(lambda e: e.tensor_scalar(st[:, 1:2], st[:, 0:1], -1.0, None, ALU.mult), t1)
                t2 = act.do(lambda e: e.activation(s[:, 0:nk], bank[:, 0:nk], ACT.Exp, bias=st[:, 1:2], scale=0.125, accum_out=st[:, 2:3]), t1, fs, init_fence)
                PT.put(b, t2)
                if swa:
                    t3 = act.do(lambda e: e.activation(st[:, 3:4], snk[:, h:h + 1], ACT.Exp, bias=st[:, 1:2]))
                    t2 = dve.do(lambda e: e.tensor_tensor(st[:, 2:3], st[:, 2:3], st[:, 3:4], ALU.add), t3)
                t4 = dve.do(lambda e: e.reciprocal(st[:, 4:5], st[:, 2:3]), t2)
                t4 = dve.do(lambda e: e.tensor_scalar(s[:, 0:nk], s[:, 0:nk], st[:, 4:5], None, ALU.mult), t4)
                st8.put(kq, t4)
                yield
                b, bank, fr = PT.get()
                for j in range(qb + 1):
                    t = pe.do(lambda e, j=j: e.transpose(bank[:, j * 128:(j + 1) * 128], s[:, j * 128:(j + 1) * 128], ident), fr, t4)
                SS.put(ks, t)
                t5 = act.do(lambda e, qb=qb, nk=nk: e.copy(pt[:, qb * 128:qb * 128 + nk], bank[:, 0:nk]), t, fp if qb == 0 else None, init_fence)
                PT.put(b, t5)
            BI.put(kb, t4)
            yield
            b, bank, fr = PT.get()
            r0 = 64 * (h % 2)
            o = bank[r0:r0 + 64, 0:S]
            pe.do(lambda e: e.matmul(o, v[:, 0, :], pt[:, 0:S], start=True, stop=False, skip_group_check=True), fr, t5, toks)
            t = pe.do(lambda e: e.matmul(bank[r0:r0 + 64, 128:S], v[:, 1, :], pt[:, S:384], start=False, stop=True, skip_group_check=True))
            PTB.put(kp, t)
            dh, dl = OH[r0:r0 + 64, och, :], OL[r0:r0 + 64, och, :]
            th = act.do(lambda e: e.copy(dh, o), t, init_fence)
            tl = dve.do(lambda e: e.tensor_tensor(dl, o, dh.bitcast(F), ALU.subtract), th)
            PT.put(b, tl)
            o_tok[och] = (o_tok[och] or []) + [th, tl]

        def swa_tasks():
            for h in range(8):
                r0 = 64 * (h % 2)
                yield from attention(h, QA[r0:r0 + 64, h // 2, :], KA[r0:r0 + 64, h // 4, :],
                                     VA[:, :, (h // 4) * 64:(h // 4) * 64 + 64], z_ready["qa"] + z_ready["ka"] + [t_va], h // 2, True)

        for j in range(2):
            gemmT([(("z", 2816 + 256 * j), 8)], HH, HL, h_tok, norm_heads([QC[:, 2 * j, :], QC[:, 2 * j + 1, :]], vec("qc"), "qc"))
        for j in range(2):
            gemmT([(("z", 3328 + 256 * j), 8)], HH, HL, h_tok, norm_heads([KC[:, 2 * j, :], KC[:, 2 * j + 1, :]], vec("kc"), "kc"))
        t_vc = []
        for j in range(2):
            i, h, l, nk = take(("z", 3840 + 256 * j))
            b, bank, fr = PG.get()
            pe.wait(fr)
            t = natural(bank, h, l, HH, HL, [0, 1])
            done(i, t)
            tt = act.do(lambda e, j=j, bank=bank: e.copy(VC[:, :, 256 * j:256 * j + 256], bank[:, :].rearrange("p (b n) -> p b n", b=2)), t, init_fence)
            PG.put(b, tt)
            t_vc.append(tt)
            tick()
        drain()

        def moba_tasks():
            for h in range(8):
                r0 = 64 * (h % 2)
                yield from attention(8 + h, QC[r0:r0 + 64, h // 2, :], KC[r0:r0 + 64, h // 2, :],
                                     VC[:, :, h * 64:h * 64 + 64], z_ready["qc"] + z_ready["kc"] + t_vc, 12 + h // 2, False)
        LIMIT[0] = 2
        pending += [swa_tasks(), moba_tasks()]

        t_pad = dve.do(lambda e: e.memset(xpad[:, :, 0:3], 0.0), init_fence)
        rnn_prev = [init_fence]

        def tt2(o, x, y, op, *t):
            return dve.do(lambda e: e.tensor_tensor(o, x, y, op), *t)

        def rnn_xr(j):
            def ev(bank, tok):
                t = act.do(lambda e: e.copy(xpad[:, :, 3:S + 3], bank[:, :].rearrange("p (m t) -> p m t", m=2)), tok, rnn_prev[0])
                rnn_state["x"] = t
                return [t]
            return ev

        rnn_state = {}

        def rnn_yr(j):
            def ev(bank, tok):
                t = act.do(lambda e: e.copy(RT[4][:, :, :], bank[:, :].rearrange("p (m t) -> p m t", m=2)), tok, rnn_prev[0])
                rnn_state["y"] = t
                return [t]
            return ev

        rcw, rcb = vec("rcw"), vec("rcb")
        for j in range(4):
            gemmT([(("z", 768 + 256 * j), 8)], HH, HL, h_tok, rnn_xr(j))
            xc, ga, gx, aa, yy = RT
            ww = xpad[:, :, 3:S + 3]
            kgw, gw, t_gw = load_gates(j)
            tx = []
            for m in range(2):
                c = 2 * j + m
                t = dve.do(lambda e, m=m, c=c: e.tensor_scalar(xc[:, m, :], xpad[:, m, 0:S], rcw[:, c:c + 1], rcb[:, c:c + 1],
                                                               ALU.mult, ALU.add), rnn_state["x"], t_pad, rnn_prev[0])
                for k in range(1, 4):
                    t = dve.do(lambda e, m=m, c=c, k=k: e.scalar_tensor_tensor(
                        out=xc[:, m, :], in0=xpad[:, m, k:k + S], scalar=rcw[:, 8 * k + c:8 * k + c + 1], in1=xc[:, m, :],
                        op0=ALU.mult, op1=ALU.add), t)
                tx.append(t)
            gemmT([(("z", 1792 + 256 * j), 8)], HH, HL, h_tok, rnn_yr(j))
            tg = []
            for w, dst, bn in ((0, ga, "gab"), (1, gx, "gxb")):
                b, bank, fr = PT.get()
                for m in range(2):
                    c = 2 * j + m
                    t = pe.do(lambda e, m=m, c=c, w=w, bank=bank: e.matmul(bank[:, m * S:(m + 1) * S], gw[:, w, m, :], xc[:, m, :],
                                                                         start=True, stop=True), fr, tx, t_gw)
                for m in range(2):
                    c = 2 * j + m
                    t1 = dve.do(lambda e, m=m, c=c, dst=dst, bank=bank, bn=bn: e.tensor_scalar(
                        dst[:, m, :], bank[:, m * S:(m + 1) * S], vec(bn)[:, c:c + 1], -80.0, ALU.add, ALU.max), t, rnn_prev[0])
                PT.put(b, t1)
                t1 = act.do(lambda e, dst=dst: e.activation(dst[:, :, :], dst[:, :, :], ACT.Exp, scale=-1.0), t1)
                t1 = dve.do(lambda e, dst=dst: e.tensor_scalar(dst[:, :, :], dst[:, :, :], 1.0, None, ALU.add), t1)
                t1 = dve.do(lambda e, dst=dst: e.reciprocal(dst[:, :, :], dst[:, :, :]), t1)
                tg.append(t1)
            GW.put(kgw, pe.now())
            for m in range(2):
                c = 2 * j + m
                ta = act.do(lambda e, m=m, c=c: e.activation(aa[:, m, :], ga[:, m, :], ACT.Exp, scale=clam[:, c:c + 1]), tg[0], t_lam, rnn_prev[0])
            t = dve.do(lambda e: e.tensor_scalar(ww[:, :, :], aa[:, :, :], -1.0, 1.0, ALU.mult, ALU.add), ta, rnn_prev[0])
            t = dve.do(lambda e: e.scalar_tensor_tensor(out=ww[:, :, :], in0=aa[:, :, :], scalar=1.0, in1=ww[:, :, :], op0=ALU.add, op1=ALU.mult), t)
            t = dve.do(lambda e: e.tensor_scalar(ww[:, :, :], ww[:, :, :], 1e-18, None, ALU.max), t)
            t = act.do(lambda e: e.activation(ww[:, :, :], ww[:, :, :], ACT.Ln), t)
            t = act.do(lambda e: e.activation(ww[:, :, :], ww[:, :, :], ACT.Exp, scale=0.5), t)
            t = dve.do(lambda e: e.memset(ww[:, :, 0:1], 1.0), t)
            tu = tt2(gx[:, :, :], gx[:, :, :], xc[:, :, :], ALU.mult, tg[1])
            t = tt2(gx[:, :, :], gx[:, :, :], ww[:, :, :], ALU.mult, tu, t)
            for m in range(2):
                ts = dve.do(lambda e, m=m: e.tensor_tensor_scan(ww[:, m, :], aa[:, m, :], gx[:, m, :], 0.0, ALU.mult, ALU.add), t)
            ty = rnn_state["y"]
            t = tt2(ga[:, :, :], yy[:, :, :], yy[:, :, :], ALU.mult, ty, ta)
            t = dve.do(lambda e: e.tensor_scalar(ga[:, :, :], ga[:, :, :], 0.044715, 1.0, ALU.mult, ALU.add), t)
            t = tt2(ga[:, :, :], ga[:, :, :], yy[:, :, :], ALU.mult, t)
            t = dve.do(lambda e: e.tensor_scalar(ga[:, :, :], ga[:, :, :], -50.0, None, ALU.max), t)
            t = act.do(lambda e: e.activation(ga[:, :, :], ga[:, :, :], ACT.Exp, scale=-2.0 * math.sqrt(2.0 / math.pi)), t)
            t = dve.do(lambda e: e.tensor_scalar(ga[:, :, :], ga[:, :, :], 1.0, None, ALU.add), t)
            t = dve.do(lambda e: e.reciprocal(ga[:, :, :], ga[:, :, :]), t)
            t = tt2(ga[:, :, :], ga[:, :, :], yy[:, :, :], ALU.mult, t)
            t = tt2(ww[:, :, :], ww[:, :, :], ga[:, :, :], ALU.mult, t, ts)
            r = split(OH[:, 4 + 2 * j:6 + 2 * j, :], OL[:, 4 + 2 * j:6 + 2 * j, :], ww[:, :, :], t, init_fence)
            o_tok[4 + 2 * j] = o_tok[5 + 2 * j] = r
            rnn_prev[0] = fence()
        LIMIT[0] = 2
        drain()
        fz1 = fence()
        c2.close()

        c2 = ctx.enter_context(ExitStack())
        GT = sb("GT", [128, 24, S], F, c2)
        g_tok = []
        for j in range(12):
            def ev(bank, tok, j=j):
                t = act.do(lambda e: e.activation(GT[:, 2 * j:2 * j + 2, :], bank[:, :].rearrange("p (m t) -> p m t", m=2), ACT.Sigmoid), tok, fz1)
                g_tok.append(t)
                return [t]
            gemmT([(("z", 4352 + 256 * j), 8)], HH, HL, h_tok, ev)
        mtok = []
        hfree = pe.now()
        for c in range(4):
            bk = [PG.get(), PT.get(), PT.get()]
            pe.wait(*[x[2] for x in bk], o_tok)
            kb = 0
            for s_ in range(2):
                i, h, l, nk = take(("br", c))
                for m in range(2):
                    for k in range(8):
                        kk = kb + k
                        g = 0 if kk < 4 else (1 if kk < 12 else 2)
                        lo_, hi_ = ((0, 3), (4, 11), (12, 15))[g]
                        for q, (w, xx) in enumerate([(h, OH), (h, OL), (l, OH)]):
                            st = kk == lo_ and q == 0 and m == 0
                            sp_ = kk == hi_ and q == 2
                            f = lambda e, w=w, xx=xx, k=k, kk=kk, m=m, g=g, st=st, sp_=sp_, bk=bk: e.matmul(
                                bk[g][1][:, m * S:(m + 1) * S], w[:, k, m * 128:(m + 1) * 128], xx[:, kk, :],
                                start=st, stop=sp_, skip_group_check=True)
                            if m == 1 and k == 7 and q == 2:
                                t = pe.do(f)
                            else:
                                pe.run(f)
                kb += 8
                done(i, t)
            ta = None
            gs = [GT[:, 8 * g + 2 * c:8 * g + 2 * c + 2, :] for g in range(3)]
            bv = [x[1][:, :].rearrange("p (m t) -> p m t", m=2) for x in bk]
            tts = [tt2(gs[g], bv[g], gs[g], ALU.mult, t, g_tok) for g in range(3)]
            for g in range(3):
                (PG if g == 0 else PT).put(bk[g][0], tts[g])
            t1 = tt2(gs[0], gs[0], gs[1], ALU.add, tts)
            t1 = tt2(gs[0], gs[0], gs[2], ALU.add, t1)
            mtok += split(HH[:, 2 * c:2 * c + 2, :], HL[:, 2 * c:2 * c + 2, :], gs[0], t1, hfree)

        def residual(gate, gt, bias=None):
            r = []

            def mk(c):
                def ev(bank, tok):
                    for m in range(2):
                        cc = 2 * c + m
                        bo = bank[:, m * S:(m + 1) * S]
                        if bias is not None:
                            tok = dve.do(lambda e, cc=cc, bo=bo: e.tensor_scalar(bo, bo, bias[:, cc:cc + 1], None, ALU.add), tok)
                        tok = dve.do(lambda e, cc=cc, bo=bo: e.scalar_tensor_tensor(
                            out=X[:, cc, :], in0=bo, scalar=gate[:, cc:cc + 1], in1=X[:, cc, :],
                            op0=ALU.mult, op1=ALU.add), tok, gt)
                    r.append(tok)
                    return [tok]
                return ev
            return r, mk

        skip_mods()
        r, mk = residual(modT[0][:, 16:24], mod_tok[0, 5])
        for c in range(4):
            gemmT([(("out", c), 8)], HH, HL, mtok, mk(c))
        x_tok = r
        if dbg.get("stop") == "mix":
            return finish(locals())
        c2.close()
        hfree = fence()

        def silu_mul(g_ap, v_ap, buf, toks, wf):
            t = act.do(lambda e: e.activation(buf, g_ap, ACT.Silu), toks, wf)
            return t

        c2 = ctx.enter_context(ExitStack())
        c1.close()
        HH, HL = sb("HH2", [128, 8, S], R, c2), sb("HL2", [128, 8, S], R, c2)
        FH, FL = sb("FH", [128, 22, S], R, c2), sb("FL", [128, 22, S], R, c2)
        A1, At1 = coeff(8, vec("norm_ffn"), modT[0][:, 32:40], mod_tok[0, 9])
        h_tok = modulate(X, x_tok, A1, At1, modT[0][:, 24:32], mod_tok[0, 7], HH, HL, hfree)
        UP = Slots([sb(f"up{i}", [128, 2, S + 2], F, c2) for i in range(2)])
        UC = [sb(f"uc{i}", [128, 2, S], F, c2) for i in range(2)]
        tpads = [dve.do(lambda e, u=u: e.memset(u[:, :, 0:2], 0.0), hfree) for u in UP.bufs]
        cw = lambda k, c: (vec("fcw01")[:, 44 * k + c:44 * k + c + 1] if k < 2 else vec("fcw2")[:, c:c + 1])
        f_tok, uc_free = [], [hfree, hfree]

        def conv_ev(which, c):
            def ev(bank, tok):
                k_, u, fu = UP.get()
                t = act.do(lambda e: e.copy(u[:, :, 2:S + 2], bank[:, :].rearrange("p (m t) -> p m t", m=2)), tok, fu, hfree)
                for m in range(2):
                    ch = 22 * which + 2 * c + m
                    td = dve.do(lambda e, m=m, ch=ch: e.tensor_scalar(UC[which][:, m, :], u[:, m, 0:S], cw(0, ch), vec("fcb")[:, ch:ch + 1],
                                                                      ALU.mult, ALU.add), t, tpads, uc_free[which])
                    for k in (1, 2):
                        td = dve.do(lambda e, m=m, ch=ch, k=k: e.scalar_tensor_tensor(
                            out=UC[which][:, m, :], in0=u[:, m, k:k + S], scalar=cw(k, ch), in1=UC[which][:, m, :],
                            op0=ALU.mult, op1=ALU.add), td)
                UP.put(k_, td)
                if which == 1:
                    ta = act.do(lambda e: e.activation(UC[0][:, :, :], UC[0][:, :, :], ACT.Silu), td)
                    tm = tt2(UC[0][:, :, :], UC[0][:, :, :], UC[1][:, :, :], ALU.mult, ta)
                    r = split(FH[:, 2 * c:2 * c + 2, :], FL[:, 2 * c:2 * c + 2, :], UC[0][:, :, :], tm, hfree)
                    f_tok.extend(r)
                    uc_free[0], uc_free[1] = r, [tm]
                return [t]
            return ev
        for c in range(11):
            gemmT([(("ug", c), 8)], HH, HL, h_tok, conv_ev(0, c))
            gemmT([(("uv", c), 8)], HH, HL, h_tok, conv_ev(1, c))
        skip_mods()
        r, mk = residual(modT[0][:, 40:48], mod_tok[0, 11])
        for c in range(4):
            gemmT([(("dn", c), 8), (("dn", c), 8), (("dn", c), 6)], FH, FL, f_tok, mk(c))
        x_tok = r
        c2.close()
        hfree = fence()
        if dbg.get("stop") == "b1":
            return finish(locals())

        c2 = ctx.enter_context(ExitStack())
        HH, HL = sb("HH3", [128, 8, 512], R, c2), sb("HL3", [128, 8, 512], R, c2)
        c3 = ctx.enter_context(ExitStack())
        cn, cT = sb("cn", [128, 2, 1024], F, c3), sb("cT", [128, 8, S], F, c3)
        t_x = load("cn", [(cn[:, tb_, :], a["ctx_2"][0, tb_ * 128:(tb_ + 1) * 128, :]) for tb_ in range(2)], hfree)
        ct = transpose_in(cn, t_x, cT, (hfree,))
        Ac, Act_ = coeff(16, vec("n10"), modT[2][:, 8:16], mod_tok[2, 3])
        hc_tok = modulate(cT, ct, Ac, Act_, modT[2][:, 0:8], mod_tok[2, 1], HH, HL, hfree, slice(0, S))
        Ax, Axt = coeff(24, vec("n10"), modT[1][:, 8:16], mod_tok[1, 3])
        h_tok = modulate(X, x_tok, Ax, Axt, modT[1][:, 0:8], mod_tok[1, 1], HH, HL, hfree, slice(S, 2 * S)) + hc_tok
        cfree = fence()
        c3.close()
        Q2, K2 = sb("Q2", [128, 8, S], F, c2), sb("K2", [128, 8, 512], F, c2)
        V2 = sb("V2", [128, 4, 1024], F, c2)
        c3 = ctx.enter_context(ExitStack())
        cs = sb("cs", [128, 640], F, c3)
        rot = cs[:, 512:640]
        t_cs = load("cs", [(cs[:, 0:512], a["consts"][:, C_COS:C_COS + 512]), (rot, a["consts"][:, C_ROT:C_ROT + 128])], cfree)
        ZT = Slots([sb(f"zu{i}", [128, 512], F, c3) for i in range(2)])
        z_ready = {"q": [], "k": [], "v": []}

        def rope(z, c_, dst, tz, key, done_cb):
            yield
            b, bank, fr = PT.get()
            t = pe.do(lambda e: e.matmul(bank[:, 0:S], rot, z, start=True, stop=True), fr, tz, t_cs)
            yield
            t1 = tt2(dst, bank[:, 0:S], cs[:, 256:512], ALU.mult, t, t_cs, cfree)
            PT.put(b, t1)
            t2 = tt2(z, z, cs[:, 0:256], ALU.mult, t, t_cs)
            t3 = tt2(dst, dst, z, ALU.add, t1, t2)
            z_ready[key].append(t3)
            done_cb(t3)

        def q_ev(c):
            def ev(bank, tok):
                k, z, fz = ZT.get()
                tz = act.do(lambda e: e.copy(z[:, :], bank[:, :]), tok, fz, cfree)
                cnt = []

                def cb(t):
                    cnt.append(t)
                    if len(cnt) == 2:
                        ZT.put(k, *cnt)
                for m in range(2):
                    pending.append(rope(z[:, m * S:(m + 1) * S], 2 * c + m, Q2[:, 2 * c + m, :], tz, "q", cb))
                return [tz]
            return ev

        def k_ev(c):
            def ev(bks, tok):
                k, z, fz = ZT.get()
                cnt, rr = [], []

                def cb(t):
                    cnt.append(t)
                    if len(cnt) == 2:
                        ZT.put(k, *cnt)
                for m in range(2):
                    t0 = act.do(lambda e, m=m: e.copy(K2[:, 2 * c + m, 0:S], bks[m][:, 0:S]), tok, cfree)
                    tz = act.do(lambda e, m=m: e.copy(z[:, m * S:(m + 1) * S], bks[m][:, S:512]), tok, fz)
                    z_ready["k"].append(t0)
                    pending.append(rope(z[:, m * S:(m + 1) * S], 2 * c + m, K2[:, 2 * c + m, S:512], tz, "k", cb))
                    rr.append([tz])
                return rr
            return ev
        LIMIT[0] = 2
        for c in range(4):
            gemmT([(("qkv", c), 8)], HH[:, :, S:512], HL[:, :, S:512], h_tok, q_ev(c))
            tick()
        drain()
        for c in range(4):
            gemmT([(("qkv", 4 + c), 8)], HH, HL, h_tok, k_ev(c), n=512)
            drain()
        drain()
        for c in range(4):
            i, h, l, nk = take(("qkv", 8 + c))
            bb = [PG.get(), PG.get()]
            pe.wait(bb[0][2], bb[1][2])
            t = natural(bb[0][1], h, l, HH, HL, [0, 1])
            t2 = natural(bb[1][1], h, l, HH, HL, [2, 3])
            done(i, t2)
            for n in range(2):
                tt = act.do(lambda e, n=n, c=c, bb=bb: e.copy(V2[:, 2 * n:2 * n + 2, 256 * c:256 * c + 256],
                                                            bb[n][1][:, :].rearrange("p (b n) -> p b n", b=2)), (t, t2)[n], cfree)
                PG.put(bb[n][0], tt)
                z_ready["v"].append(tt)
        cfree = fence()
        c3.close()
        lq = sb("lq", [128, 4, 64], F, c2)
        lt = sb("lt", [128, 16], F, c2)
        t_l = load("lq", [(lq[:, n, :], a[nm].broadcast_to([128, 64])) for n, nm in
                          enumerate(("attn_lq1_2", "attn_lk1_2", "attn_lq2_2", "attn_lk2_2"))], cfree)
        lam_init = 0.8 - 0.6 * math.exp(-0.3 * 0)
        for n in range(2):
            t = dve.do(lambda e, n=n: e.tensor_tensor_reduce(lq[:, 2 * n, :], lq[:, 2 * n, :], lq[:, 2 * n + 1, :], 1.0, 0.0,
                                                             ALU.mult, ALU.add, lt[:, n:n + 1]), t_l, cfree)
        t = act.do(lambda e: e.activation(lt[:, 2:4], lt[:, 0:2], ACT.Exp), t)
        t_lm = dve.do(lambda e: e.scalar_tensor_tensor(out=lt[:, 4:5], in0=lt[:, 2:3], scalar=lam_init, in1=lt[:, 3:4],
                                                       op0=ALU.add, op1=ALU.subtract), t)
        LAM = lt[:, 4:5]
        t_sg = dve.do(lambda e: e.tensor_scalar(lt[:, 5:6], vec("sub"), 1.0 - lam_init, None, ALU.mult), vec_tok, t_lm)
        SUBG = lt[:, 5:6]
        hf3 = [pe.now()]
        OHH, OHL = HH, HL
        PP = Slots([sb(f"pp{i}", [128, 2, 512], F, c2) for i in range(2)])
        AT = Slots([sb(f"at{i}", [128, 4, S], F, c2) for i in range(2)])
        ST = Slots([sb(f"sr{i}", [128, 12], F, c2) for i in range(2)])
        OT = Slots([sb(f"ot{i}", [128, 1, S], F, c2) for i in range(2)])
        aready = []

        def da_head(h):
            while AT.busy():
                yield
            ka, at, fa = AT.get()
            for qb in range(2):
                while PP.busy() or ST.busy():
                    yield
                kp, pp, fp = PP.get()
                ks, s, fs = ST.get()
                tx = []
                for n in range(2):
                    r0 = 64 * n
                    b, bank, fr = PG.get()
                    t = pe.do(lambda e, r0=r0, bank=bank, qb=qb: e.matmul(bank[:, :], Q2[r0:r0 + 64, h, qb * 128:qb * 128 + 128],
                                                                         K2[r0:r0 + 64, h, :], start=True, stop=True), fr, z_ready["q"], z_ready["k"])
                    t = dve.do(lambda e, n=n, bank=bank, s=s: e.tensor_reduce(s[:, n:n + 1], bank[:, :], AX, ALU.max), t, fs, cfree)
                    t = dve.do(lambda e, n=n, s=s: e.tensor_scalar(s[:, 2 + n:3 + n], s[:, n:n + 1], -0.125, None, ALU.mult), t)
                    t = act.do(lambda e, n=n, bank=bank, s=s, pp=pp: e.activation(
                        pp[:, n, :], bank[:, :], ACT.Exp, bias=s[:, 2 + n:3 + n], scale=0.125, accum_out=s[:, 4 + n:5 + n]), t, fp, cfree)
                    PG.put(b, t)
                    tx.append(t)
                yield
                t = dve.do(lambda e, s=s: e.reciprocal(s[:, 6:8], s[:, 4:6]), tx)
                t = tt2(s[:, 8:9], s[:, 7:8], LAM, ALU.mult, t, t_lm)
                t = dve.do(lambda e, s=s, pp=pp: e.tensor_scalar(pp[:, 1, :], pp[:, 1, :], s[:, 8:9], None, ALU.mult), t)
                t = dve.do(lambda e, s=s, pp=pp: e.scalar_tensor_tensor(out=pp[:, 0, :], in0=pp[:, 0, :], scalar=s[:, 6:7], in1=pp[:, 1, :],
                                                                        op0=ALU.mult, op1=ALU.subtract), t)
                ST.put(ks, t)
                yield
                b, bank, fr = PT.get()
                for j in range(4):
                    tp = pe.do(lambda e, j=j, bank=bank, pp=pp: e.transpose(bank[:, j * 128:(j + 1) * 128], pp[:, 0, j * 128:(j + 1) * 128], ident), fr, t)
                PP.put(kp, tp)
                t = act.do(lambda e, qb=qb, bank=bank: e.copy(at[:, :, qb * 128:qb * 128 + 128], bank[:, :].rearrange("p (j q) -> p j q", j=4)),
                           tp, fa if qb == 0 else None, cfree)
                PT.put(b, t)
            yield
            b, bank, fr = PT.get()
            for j in range(4):
                tp = pe.do(lambda e, j=j: e.matmul(bank[:, 0:S], V2[:, j, h * 128:(h + 1) * 128], at[:, j, :], start=(j == 0), stop=(j == 3)), fr, t, z_ready["v"])
            AT.put(ka, tp)
            while OT.busy():
                yield
            ko, o, fo = OT.get()
            to = act.do(lambda e: e.copy(o[:, 0, :], bank[:, 0:S]), tp, fo, cfree)
            PT.put(b, to)
            yield
            kr, r, tr = rstd_T(o, 1, to, 128)
            yield
            t = dve.do(lambda e: e.scalar_tensor_tensor(out=o[:, 0, :], in0=o[:, 0, :], scalar=SUBG, in1=r[:, :], op0=ALU.mult, op1=ALU.mult), tr, t_sg)
            RS.put(kr, t)
            rr = split(OHH[:, h, 0:S], OHL[:, h, 0:S], o[:, 0, :], t, hf3[0])
            OT.put(ko, *rr)
            aready.extend(rr)
        hf3[0] = pe.now()
        LIMIT[0] = 2
        pending += [da_head(h) for h in range(8)]
        drain()
        skip_mods()
        r, mk = residual(modT[1][:, 16:24], mod_tok[1, 5])
        for c in range(4):
            gemmT([(("wo", c), 8)], HH[:, :, 0:S], HL[:, :, 0:S], aready, mk(c))
        x_tok = r
        c2.close()
        hfree = fence()
        if dbg.get("stop") == "attn":
            return finish(locals())
        c2 = ctx.enter_context(ExitStack())
        HH, HL = sb("HH4", [128, 8, S], R, c2), sb("HL4", [128, 8, S], R, c2)
        FH, FL = sb("FH4", [128, 28, S], R, c2), sb("FL4", [128, 28, S], R, c2)
        UC = Slots([sb(f"ud{i}", [128, 2, S], F, c2) for i in range(2)])
        A1, At1 = coeff(32, vec("n20"), modT[1][:, 32:40], mod_tok[1, 9])
        h_tok = modulate(X, x_tok, A1, At1, modT[1][:, 24:32], mod_tok[1, 7], HH, HL, hfree)
        f_tok = []
        cur = {}

        def f1_ev(bank, tok):
            k, u, fu = UC.get()
            t = act.do(lambda e: e.activation(u[:, :, :], bank[:, :].rearrange("p (m t) -> p m t", m=2), ACT.Silu), tok, fu, hfree)
            cur["u"] = (k, u, t)
            return [t]

        def f3_ev(c):
            def ev(bank, tok):
                k, u, tu = cur["u"]
                tm = tt2(u[:, :, :], bank[:, :].rearrange("p (m t) -> p m t", m=2), u[:, :, :], ALU.mult, tok, tu)
                r = split(FH[:, 2 * c:2 * c + 2, :], FL[:, 2 * c:2 * c + 2, :], u[:, :, :], tm, hfree)
                f_tok.extend(r)
                UC.put(k, *r)
                return [tm]
            return ev
        for c in range(14):
            gemmT([(("f1", c), 8)], HH, HL, h_tok, f1_ev)
            gemmT([(("f3", c), 8)], HH, HL, h_tok, f3_ev(c))
        skip_mods()
        r, mk = residual(modT[1][:, 40:48], mod_tok[1, 11])
        for c in range(4):
            gemmT([(("f2", c), 8), (("f2", c), 8), (("f2", c), 8), (("f2", c), 4)], FH, FL, f_tok, mk(c))
        x_tok = r
        c2.close()
        hfree = fence()
        if dbg.get("stop") == "ffn2":
            return finish(locals())

        skip_mods()
        c2 = ctx.enter_context(ExitStack())
        FX = sb("FX", [128, 8, S], F, c2)
        FN = sb("FN", [128, 2, 8, 256], F, c2)
        HH, HL = sb("HH5", [128, 8, S], R, c2), sb("HL5", [128, 8, S], R, c2)
        fcs = sb("fcs", [128, 1280], F, c2)
        t_f = load("fcs", [(fcs[:, :], a["consts"][:, C_FD:C_FD + 1280])], hfree)
        A1, At1 = coeff(40, vec("n11"), modT[3][:, 8:16], mod_tok[3, 3])

        def norm_full(dst, A, At, shift, st, toks, wf):
            k, r, t = rstd_T(X, 8, toks, D)
            o = []
            for c in range(8):
                t1 = dve.do(lambda e, c=c: e.scalar_tensor_tensor(out=dst[:, c, :], in0=X[:, c, :], scalar=A[:, c:c + 1],
                                                                  in1=r[:, :], op0=ALU.mult, op1=ALU.mult), t, At, wf)
                if shift is not None:
                    t1 = act.do(lambda e, c=c: e.activation(dst[:, c, :], dst[:, c, :], ACT.Identity, bias=shift[:, c:c + 1]), t1, st)
                o.append(t1)
            RS.put(k, dve.now())
            return o
        xt = norm_full(FX, A1, At1, modT[3][:, 0:8], mod_tok[3, 1], x_tok, hfree)
        tn = []
        for g in range(8):
            b, bank, fr = PG.get()
            for tb_ in range(2):
                t = pe.do(lambda e, g=g, tb_=tb_, bank=bank: e.matmul(bank[:, tb_ * 256:tb_ * 256 + 256], FX[:, g, tb_ * 128:tb_ * 128 + 128],
                                                                     fcs[:, 0:256], start=True, stop=True), fr, xt, t_f)
            t = act.do(lambda e, g=g, bank=bank: e.copy(FN[:, :, g, :], bank[:, :].rearrange("p (b n) -> p b n", b=2)), t, hfree)
            PG.put(b, t)
            tn.append(t)
        f_tok = []
        for g in range(0, 8, 2):
            b, bank, fr = PG.get()
            for m in range(2):
                for s_ in range(4):
                    tb_, part = s_ // 2, s_ % 2
                    t = pe.do(lambda e, g=g, m=m, tb_=tb_, part=part, s_=s_, bank=bank: e.matmul(
                        bank[:, m * S:(m + 1) * S], FN[:, tb_, g + m, part * 128:part * 128 + 128],
                        fcs[:, 256 + tb_ * 512 + part * 256:256 + tb_ * 512 + part * 256 + 256],
                        start=(s_ == 0), stop=(s_ == 3)), fr, tn)
            rr = split(HH[:, g:g + 2, :], HL[:, g:g + 2, :], bank[:, :].rearrange("p (m t) -> p m t", m=2), t, hfree)
            PG.put(b, *rr)
            f_tok += rr
        r, mk = residual(modT[3][:, 16:24], mod_tok[3, 5], vec("fbo"))
        for c in range(4):
            gemmT([(("fn", c), 8)], HH, HL, f_tok, mk(c))
        x_tok = r
        c2.close()
        hfree = fence()
        if dbg.get("stop") == "fnet":
            return finish(locals())

        c2 = ctx.enter_context(ExitStack())
        TH, TL = sb("TH", [128, 2, 1024], R, c2), sb("TL", [128, 2, 1024], R, c2)
        MO = sb("MO", [128, 8, S], F, c2)
        misc = sb("misc", [128, 264], F, c2)
        RO = sb("RO", [128, 2, 96], F, c2)
        RK = sb("RK", [128, 2, 8], F, c2)
        CN = sb("CN", [128, 64], F, c2)
        OV = sb("OV", [128, 2, 8], F, c2)
        CI = sb("CI", [128, 4], I32, c2)
        c3 = ctx.enter_context(ExitStack())
        H2 = sb("H2", [128, 8, S], F, c3)
        rw = sb("rw", [128, 8, 8], F, c3)
        A1, At1 = coeff(48, vec("n21"), modT[3][:, 32:40], mod_tok[3, 9])
        xt = norm_full(H2, A1, At1, modT[3][:, 24:32], mod_tok[3, 7], x_tok, hfree)
        t_rw = load("rw", [(rw[:, :, :], a["moe_router_2"][0].rearrange("(k p) e -> p k e", p=128))], hfree)
        t_mi = load("misc", [(misc[:, 0:264], a["consts"][:, C_TRI:C_TRI + 264])], hfree)
        tri, iota, eix = misc[:, 0:128], misc[:, 128:256], misc[:, 256:264]
        tok_t = []
        for tb_ in range(2):
            for c in range(0, 8, 4):
                b, bank, fr = PG.get()
                for j in range(4):
                    t = pe.do(lambda e, j=j, c=c, tb_=tb_, bank=bank: e.transpose(bank[:, j * 128:(j + 1) * 128],
                                                                                H2[:, c + j, tb_ * 128:tb_ * 128 + 128], ident), fr, xt)
                rr = split(TH[:, tb_, c * 128:c * 128 + 512], TL[:, tb_, c * 128:c * 128 + 512], bank[:, :], t, hfree)
                PG.put(b, *rr)
                tok_t += rr
        ro = lambda tb_, i, n=8: RO[:, tb_, 8 * i:8 * i + n]
        tm = []
        for tb_ in range(2):
            b, bank, fr = PT.get()
            for k in range(8):
                t = pe.do(lambda e, k=k, tb_=tb_, bank=bank: e.matmul(bank[:, 0:8], H2[:, k, tb_ * 128:tb_ * 128 + 128], rw[:, k, :],
                                                                     start=(k == 0), stop=(k == 7)), fr, xt, t_rw)
            lg, eq1, s1, eq2, s2, l2, mk_, gt_, ex = (ro(tb_, i) for i in range(9))
            sc = RO[:, tb_, 72:96]
            t = dve.do(lambda e: e.tensor_copy(lg, bank[:, 0:8]), t, hfree)
            PT.put(b, t)

            def top(lg, eq, sel, v, t):
                t = dve.do(lambda e: e.tensor_reduce(v, lg, AX, ALU.max), t)
                t = dve.do(lambda e: e.tensor_scalar(eq, lg, v, None, ALU.is_equal), t)
                t = tt2(eq, eq, eix, ALU.mult, t, t_mi)
                t = dve.do(lambda e: e.tensor_reduce(sc[:, 7:8], eq, AX, ALU.max), t)
                return dve.do(lambda e: e.tensor_scalar(sel, eq, sc[:, 7:8], None, ALU.is_equal), t)
            t = top(lg, eq1, s1, sc[:, 0:1], t)
            t = dve.do(lambda e: e.tensor_scalar(l2, s1, -3.0e38, None, ALU.mult), t)
            t = dve.do(lambda e: e.tensor_scalar(eq2, s1, -1.0, 1.0, ALU.mult, ALU.add), t)
            t = tt2(eq2, eq2, lg, ALU.mult, t)
            t = tt2(l2, l2, eq2, ALU.add, t)
            t = top(l2, eq2, s2, sc[:, 1:2], t)
            t = tt2(mk_, s1, s2, ALU.add, t)
            t = tt2(sc[:, 2:3], sc[:, 1:2], sc[:, 0:1], ALU.subtract, t)
            t = act.do(lambda e: e.activation(sc[:, 3:4], sc[:, 2:3], ACT.Exp), t)
            t = dve.do(lambda e: e.tensor_scalar(sc[:, 4:5], sc[:, 3:4], 1.0, None, ALU.add), t)
            t = dve.do(lambda e: e.reciprocal(sc[:, 4:5], sc[:, 4:5]), t)
            t = tt2(sc[:, 5:6], sc[:, 3:4], sc[:, 4:5], ALU.mult, t)
            t = dve.do(lambda e: e.tensor_scalar(gt_, s1, sc[:, 4:5], None, ALU.mult), t)
            t = dve.do(lambda e: e.scalar_tensor_tensor(out=gt_, in0=s2, scalar=sc[:, 5:6], in1=gt_, op0=ALU.mult, op1=ALU.add), t)
            tm.append(t)
        tr = []
        for tb_ in range(2):
            b, bank, fr = PT.get()
            if tb_ == 1:
                pe.do(lambda e, bank=bank: e.matmul(bank[:, 0:8], one[:, :], ro(0, 6), start=True, stop=False), fr, tm)
            t = pe.do(lambda e, tb_=tb_, bank=bank: e.matmul(bank[:, 0:8], tri, ro(tb_, 6), start=(tb_ == 0), stop=True), fr, tm, t_mi)
            t = dve.do(lambda e, tb_=tb_, bank=bank: e.tensor_copy(RK[:, tb_, :], bank[:, 0:8]), t, hfree)
            PT.put(b, t)
            t = tt2(RK[:, tb_, :], RK[:, tb_, :], ro(tb_, 6), ALU.mult, t)
            t = dve.do(lambda e, tb_=tb_: e.tensor_scalar(ro(tb_, 8), ro(tb_, 6), 1e4, -1e4, ALU.mult, ALU.add), t)
            tr.append(tt2(RK[:, tb_, :], RK[:, tb_, :], ro(tb_, 8), ALU.add, t))
        b, bank, fr = PT.get()
        pe.do(lambda e: e.matmul(bank[:, 0:8], one[:, :], ro(0, 6), start=True, stop=False), fr, tm)
        t = pe.do(lambda e: e.matmul(bank[:, 0:8], one[:, :], ro(1, 6), start=False, stop=True))
        t_cn = dve.do(lambda e: e.tensor_copy(CN[:, 0:8], bank[:, 0:8]), t, hfree)
        PT.put(b, t_cn)
        t = dve.do(lambda e: e.tensor_scalar(CN[:, 8:16], CN[:, 0:8], float(CAP), None, ALU.is_gt), t_cn)
        t = dve.do(lambda e: e.memset(CN[:, 56:64], 1.0), hfree)
        t = dve.do(lambda e: e.tensor_tensor_scan(CN[:, 16:24], CN[:, 56:64], CN[:, 8:16], 0.0, ALU.mult, ALU.add), t)
        t_ov = [dve.do(lambda e: e.tensor_copy(CN[:, 48:49], CN[:, 23:24]), t)]
        for j in range(3):
            sj = CN[:, 24 + 8 * j:32 + 8 * j]
            t1 = dve.do(lambda e: e.tensor_scalar(sj, CN[:, 16:24], float(j + 1), None, ALU.is_equal), t)
            t1 = tt2(sj, sj, CN[:, 8:16], ALU.mult, t1)
            t1 = dve.do(lambda e: e.tensor_tensor_reduce(CN[:, 56:64], sj, eix, 1.0, 0.0, ALU.mult, ALU.add, CN[:, 49 + j:50 + j]), t1, t_ov)
            t1 = dve.do(lambda e: e.tensor_scalar(CN[:, 49 + j:50 + j], CN[:, 49 + j:50 + j], -1.0, 8.0, ALU.mult, ALU.add), t1)
            t1 = dve.do(lambda e: e.tensor_scalar(CN[:, 49 + j:50 + j], CN[:, 49 + j:50 + j], 7.0, None, ALU.min), t1)
            for tb_ in range(2):
                t1 = dve.do(lambda e: e.tensor_tensor_reduce(CN[:, 56:64], sj, RK[:, tb_, :], 1.0, -float(CAP), ALU.mult, ALU.add,
                                                             OV[:, tb_, j:j + 1]), t1, tr, hfree)
                t1 = dve.do(lambda e: e.tensor_tensor_reduce(CN[:, 56:64], sj, ro(tb_, 7), 1.0, 0.0, ALU.mult, ALU.add,
                                                             OV[:, tb_, 4 + j:5 + j]), t1, tm)
            t_ov.append(t1)
        t_ov.append(dve.do(lambda e: e.memset(OV[:, :, 3:4], -1.0), hfree))
        t_ci = dve.do(lambda e: e.tensor_copy(CI[:, :], CN[:, 48:52]), t_ov)
        t_mo = dve.do(lambda e: e.memset(MO[:, :, :], 0.0), hfree)
        mfree = fence()
        c3.close()
        XH = Slots([sb(f"xh{i}", [128, 8, 256], R, c2) for i in range(2)])
        XL = [sb(f"xl{i}", [128, 8, 256], R, c2) for i in range(2)]
        PB = Slots([sb(f"pb{i}", [128, 2, 256], R, c2) for i in range(2)])
        PTT = Slots([sb(f"ptt{i}", [128, 2, 256], R, c2) for i in range(3)])
        GS = Slots([sb(f"gsl{i}", [128, 2], F, c2) for i in range(3)])
        HB = Slots([sb(f"hb{i}", [128, 512], F, c2) for i in range(2)])
        TT = Slots([sb(f"tth{i}", [128, 4, 128], R, c2) for i in range(2)])
        TTL = [sb(f"ttl{i}", [128, 4, 128], R, c2) for i in range(2)]
        YH, YL = sb("YH", [128, 1024], R, c2), sb("YL", [128, 1024], R, c2)
        YB = (banks[6], banks[7])
        ytok = PT.free[2] + PT.free[3]
        assert len(PT.order) == 4
        freeT = [PT.free[0], PT.free[1]]
        PT = Slots(banks[4:6])
        PT.free = freeT

        def gather(cols, rk, off, gate, m0):
            k_, pb, fp = PB.get()
            kt_, ptt, ft = PTT.get()
            kg_, gsl, fg = GS.get()
            tb = []
            for n in range(2):
                for tb_ in range(2):
                    rc = rk(n, tb_)
                    tb.append(dve.do(lambda e, n=n, tb_=tb_, rc=rc: e.tensor_scalar(
                        pb[:, tb_, n * 128:(n + 1) * 128], iota, rc, None, ALU.is_equal), fp, m0, t_mi, mfree))
            kx, xh, fx = XH.get()
            xl = XL[kx]
            tx = []
            for c in range(8):
                for (src, dst) in ((TH, xh), (TL, xl)):
                    if dst is xh:
                        b, bank, fr = PG.get()
                    o = bank[:, 0:256] if dst is xh else bank[:, 256:512]
                    for tb_ in range(2):
                        t = pe.do(lambda e, c=c, tb_=tb_, src=src, o=o: e.matmul(o, src[:, tb_, c * 128:(c + 1) * 128], pb[:, tb_, :],
                                                                                start=(tb_ == 0), stop=(tb_ == 1)), fr, tb, tok_t)
                t1 = act.do(lambda e, c=c, bank=bank: e.copy(xh[:, c, :], bank[:, 0:256]), t, fx, mfree)
                t2 = act.do(lambda e, c=c, bank=bank: e.copy(xl[:, c, :], bank[:, 256:512]), t)
                PG.put(b, t2)
                tx.append(t2)
            b, bank, fr = PT.get()
            for n in range(2):
                for tb_ in range(2):
                    t = pe.do(lambda e, n=n, tb_=tb_, bank=bank: e.transpose(
                        bank[:, n * 256 + tb_ * 128:n * 256 + tb_ * 128 + 128], pb[:, tb_, n * 128:(n + 1) * 128].bitcast(F), ident), fr, tb)
            t = act.do(lambda e, bank=bank: e.copy(ptt[:, :, :], bank[:, :].rearrange("p (n t) -> p n t", n=2)), t, ft, mfree)
            PT.put(b, t)
            b, bank, fr = PT.get()
            for n in range(2):
                for tb_ in range(2):
                    gc = gate(n, tb_)
                    tg = pe.do(lambda e, n=n, tb_=tb_, bank=bank, gc=gc: e.matmul(
                        bank[:, n:n + 1], pb[:, tb_, n * 128:(n + 1) * 128].bitcast(F), gc, start=(tb_ == 0), stop=(tb_ == 1)), fr, tb)
            PB.put(k_, tg)
            tg = dve.do(lambda e, bank=bank: e.tensor_copy(gsl[:, :], bank[:, 0:2]), tg, fg, mfree)
            PT.put(b, tg)
            return dict(kx=kx, xh=xh, xl=xl, tx=tx, kt=kt_, ptt=ptt, tp=t, kg=kg_, gsl=gsl, tg=tg)

        def up(G, n_in, tags):
            res = []
            for w in range(2):
                b, bank, fr = PG.get()
                pe.wait(fr, G["tx"])
                for k0 in range(2):
                    i, h, l, nk = take(tags[2 * w + k0])
                    for k in range(4):
                        kk = 4 * k0 + k
                        xs, ls = G["xh"][:, kk, n_in * 128:(n_in + 1) * 128], G["xl"][:, kk, n_in * 128:(n_in + 1) * 128]
                        for q, (x_, w_) in enumerate([(xs, h), (ls, h), (xs, l)]):
                            f = lambda e, x_=x_, w_=w_, k=k, kk=kk, q=q, bank=bank: e.matmul(
                                bank[:, :], x_, w_[:, k, :], start=(kk == 0 and q == 0), stop=(kk == 7 and q == 2))
                            if k == 3 and q == 2:
                                t = pe.do(f)
                            else:
                                pe.run(f)
                    done(i, t)
                res.append((b, bank, t))
            kh, hb, fh = HB.get()
            t1 = act.do(lambda e: e.activation(hb[:, :], res[0][1][:, :], ACT.Silu), res[0][2], fh, mfree)
            PG.put(res[0][0], t1)
            t2 = tt2(hb[:, :], res[1][1][:, :], hb[:, :], ALU.mult, t1, res[1][2])
            PG.put(res[1][0], t2)
            return kh, hb, t2

        def turn(kh, hb, th):
            b, bank, fr = PT.get()
            for j in range(4):
                t = pe.do(lambda e, j=j, bank=bank: e.transpose(bank[:, j * 128:(j + 1) * 128], hb[:, j * 128:(j + 1) * 128], ident), fr, th)
            HB.put(kh, t)
            kt, tt_, ft = TT.get()
            v = bank[:, :].rearrange("p (j t) -> p j t", j=4)
            rr = split(tt_[:, :, :], TTL[kt][:, :, :], v, t, [ft, mfree])
            PT.put(b, *rr)
            return kt, tt_, rr

        def down(kt, tt_, rr, n, tags, yfree):
            pe.wait(rr, yfree)
            for j in range(2):
                i, h, l, nk = take(tags[j])
                for k in range(2):
                    kk = 2 * j + k
                    for half in range(2):
                        for q, (x_, w_) in enumerate([(tt_, h), (TTL[kt], h), (tt_, l)]):
                            f = lambda e, x_=x_, w_=w_, k=k, kk=kk, q=q, half=half: e.matmul(
                                YB[half][:, :], x_[:, kk, :], w_[:, k, half * 512:(half + 1) * 512],
                                start=(n == 0 and kk == 0 and q == 0), stop=(n == 6 and kk == 3 and q == 2), skip_group_check=True)
                            if k == 1 and half == 1 and q == 2:
                                t = pe.do(f)
                            else:
                                pe.run(f)
                done(i, t)
            TT.put(kt, t)
            return t

        state = {"yfree": ytok, "ys": [], "mo": [t_mo]}

        def collect(G, n_in, t):
            gs = G["gsl"][:, n_in:n_in + 1]
            tl = []
            for half in range(2):
                sl = slice(half * 512, half * 512 + 512)
                th = act.do(lambda e, half=half, sl=sl: e.activation(YH[:, sl], YB[half][:, :], ACT.Copy, scale=gs), t, G["tg"], state["ys"], mfree)
                tl.append(dve.do(lambda e, half=half, sl=sl: e.scalar_tensor_tensor(
                    out=YL[:, sl], in0=YB[half][:, :], scalar=gs, in1=YH[:, sl].bitcast(F), op0=ALU.mult, op1=ALU.subtract), th, state["ys"], mfree))
            state["yfree"] = tl
            return tl + [th]

        def scatter(G, n_in, ty):
            for c in range(0, 8, 2):
                b, bank, fr = PG.get()
                for m in range(2):
                    for q, y in enumerate((YH, YL)):
                        t = pe.do(lambda e, c=c, m=m, q=q, y=y, bank=bank: e.matmul(
                            bank[:, m * S:(m + 1) * S], y[:, (c + m) * 128:(c + m + 1) * 128], G["ptt"][:, n_in, :],
                            start=(q == 0), stop=(q == 1)), fr, ty, G["tp"])
                tv = tt2(MO[:, c:c + 2, :], bank[:, :].rearrange("p (m t) -> p m t", m=2), MO[:, c:c + 2, :], ALU.add, t, state["mo"])
                PG.put(b, tv)
            state["ys"] = [t]
            return t

        def etags(e, n):
            return [(tag, e, n, k0) for tag in ("w1", "w3") for k0 in range(2)]

        def dtags(e, n):
            return [("w2", e, n, j) for j in range(2)]

        def run_experts(order, gathers, extra=False):
            prev = None
            late = None

            def finish_step(p):
                (e, n), (kt, tt_, rr) = p
                return down(kt, tt_, rr, n, dtags(e, n), state["yfree"] if n == 0 else None)
            for (e, n) in order:
                G = gathers[e // 2]
                h = up(G, e % 2, etags(e, n))
                if prev is not None:
                    (pe_, pn), t_ = prev
                    t = finish_step(prev)
                    if pn == 6:
                        Gp = gathers[pe_ // 2]
                        late = (Gp, pe_ % 2, collect(Gp, pe_ % 2, t), pe_)
                if n == 1 and late is not None:
                    t = scatter(*late[:3])
                    release(late, t, gathers)
                    late = None
                if n == 3 and e % 2 == 0 and e + 2 < NEXP and not extra:
                    gathers[e // 2 + 1] = gather(None, *gargs(e // 2 + 1))
                prev = ((e, n), turn(*h))
            t = finish_step(prev)
            (pe_, pn), _ = prev
            Gp = gathers[pe_ // 2]
            ty = collect(Gp, pe_ % 2, t)
            t = scatter(Gp, pe_ % 2, ty)
            release((Gp, pe_ % 2, ty, pe_), t, gathers)

        def release(late, t, gathers):
            G, n_in, _, e = late
            if e % 2 == 1:
                XH.put(G["kx"], pe.now())
                PTT.put(G["kt"], pe.now())
                GS.put(G["kg"], dve.now(), act.now())

        def gargs(p):
            return (lambda n, tb_: RK[:, tb_, 2 * p + n:2 * p + n + 1], 0,
                    lambda n, tb_: ro(tb_, 7)[:, 2 * p + n:2 * p + n + 1], tr + tm)
        gathers = {0: gather(None, *gargs(0))}
        run_experts(steps, gathers)

        for q in (pe, act, dve, pool, sp):
            q.wait(fence(), t_ci)
        main = (pe, act, dve)
        n_over = nc.values_load(CI[0:1, 0:1], min_val=0, max_val=3)
        pe, act, dve = (Queue(q.eng, sem("s_over_" + n)) for q, n in zip(main, ("pe", "act", "dve")))
        s_raw = [sem(f"s_over_raw{i}") for i in range(NR)]
        plan, raw_free = [], {}
        pos[0] = ahead[0] = gcount[0] = 0
        pair_free = [[] for _ in range(NP)]
        for ring in (PG, PT, XH, PB, PTT, GS, HB, TT):
            assert len(ring.order) == len(ring.bufs)
            ring.free = [[] for _ in ring.bufs]
        state = {"yfree": [], "ys": [], "mo": []}
        ovt = lambda n, tb_, j, o: OV[:, tb_, o + j:o + j + 1] if n == 0 else OV[:, tb_, 3:4]
        for j in range(3):
            with nc.If(n_over > j):
                ex = nc.sync.value_load(CI[0:1, 1 + j:2 + j], min_val=0, max_val=7)
                first = len(plan)
                eu = [a[f"moe_w{w}_2"] for w in (1, 3)]
                for n in range(8):
                    if n < 7:
                        for tag, w in (("w1", eu[0]), ("w3", eu[1])):
                            for k0 in range(2):
                                src = w[0, bass.ds(ex, 1), k0 * 512:(k0 + 1) * 512, n * 512:(n + 1) * 512]
                                plan.append(("G", (tag, 0, n, k0), src.rearrange("a (k p) n -> p (a k) n", p=128), 4, 512))
                    if n:
                        for k0 in range(2):
                            r0 = (n - 1) * 512 + k0 * 256
                            src = a["moe_w2_2"][0, bass.ds(ex, 1), r0:r0 + 256, :]
                            plan.append(("G", ("w2", 0, n - 1, k0), src.rearrange("a (k p) n -> p (a k) n", p=128), 2, 1024))
                for i in range(first, first + NR):
                    issue(i)
                G = gather(None, lambda n, tb_: ovt(n, tb_, j, 0), 0, lambda n, tb_: ovt(n, tb_, j, 4), None)
                run_experts([(0, n) for n in range(7)], {0: G}, extra=True)
                XH.put(G["kx"], pe.now())
                PTT.put(G["kt"], pe.now())
                GS.put(G["kg"], dve.now(), act.now())
                for q in (pe, act, dve, pool, sp):
                    q.wait([pe.now(), act.now(), dve.now()])
            for q in (pe, act, dve, pool, sp):
                q.eng.wait_ge(t_ci[0], t_ci[1])
        pe, act, dve = main
        for ring in (PG, PT, TM, SQ, RS):
            ring.free = [[] for _ in ring.bufs]

        tx = []
        for c in range(8):
            tx.append(dve.do(lambda e, c=c: e.scalar_tensor_tensor(out=X[:, c, :], in0=MO[:, c, :], scalar=modT[3][:, 40 + c:41 + c],
                                                                   in1=X[:, c, :], op0=ALU.mult, op1=ALU.add), dve.now(), mod_tok[3, 11]))
        x_tok = tx
        fin = norm_full(X, vec("fing"), vec_tok, None, None, tx, None)
        c2.close()
        x_tok = fin
        return finish(locals())


def finish(v):
    nc, pe, act, dve, pool, sp = (v[k] for k in ("nc", "pe", "act", "dve", "pool", "sp"))
    PT, X, ident, load, fence, out = (v[k] for k in ("PT", "X", "ident", "load", "fence", "out"))
    f = fence()
    c = ExitStack()
    o = v["sb"]("onat", [128, 2, 1024], F, c)
    with c:
        toks = []
        for tb in range(2):
            for c4 in range(0, 8, 4):
                b, bank, fr = PT.get()
                for j in range(4):
                    t = pe.do(lambda e, j=j, c4=c4, tb=tb, bank=bank: e.transpose(
                        bank[:, j * 128:(j + 1) * 128], X[:, c4 + j, tb * 128:tb * 128 + 128], ident), fr, v["x_tok"])
                t = dve.do(lambda e, tb=tb, c4=c4, bank=bank: e.tensor_copy(o[:, tb, c4 * 128:c4 * 128 + 512], bank[:, :]), t, f)
                PT.put(b, t)
                toks.append(t)
        t_out = load("out", [(out[0, tb * 128:(tb + 1) * 128, :], o[:, tb, :]) for tb in range(2)], toks, q=sp)
        sp.wait(t_out)


_USED = ["x", "c", "w_mod", "b_mod", "norm_mix", "norm_ffn", "w_in", "qnorm_a", "knorm_a", "sinks", "rnn_conv_w",
         "rnn_conv_b", "rnn_gate_a_w", "rnn_gate_a_b", "rnn_gate_x_w", "rnn_gate_x_b", "rnn_lambda", "qnorm_c",
         "knorm_c", "rel_bias", "w_branch", "w_out", "w_up", "ffn_conv_w", "ffn_conv_b", "w_down", "c_2", "ctx_2",
         "c_ctx_2", "ada_w_2", "ada_b_2", "norm1_g_2", "norm2_g_2", "attn_w_qkv_2", "attn_lq1_2", "attn_lk1_2",
         "attn_lq2_2", "attn_lk2_2", "attn_subln_g_2", "attn_w_o_2", "fnet_w_o_2", "fnet_b_o_2", "ff_w1_2",
         "ff_w3_2", "ff_w2_2", "moe_router_2", "moe_w1_2", "moe_w3_2", "moe_w2_2", "final_g_2"]


def kernel(**inputs):
    import concourse.bacc as bacc
    from concourse.bass_utils import run_bass_kernel_spmd

    nc = bacc.Bacc("TRN2", target_bir_lowering=False, num_devices=1)
    arrays, aps = {}, {}
    for name in _USED:
        v = np.ascontiguousarray(inputs[name])
        arrays[f"in_{name}"] = v
        aps[name] = nc.dram_tensor(f"in_{name}", v.shape, mybir.dt.from_np(v.dtype), kind="ExternalInput").ap()
    v = constants()
    arrays["in_consts"] = v
    aps["consts"] = nc.dram_tensor("in_consts", v.shape, F, kind="ExternalInput").ap()
    out = nc.dram_tensor("out_0", (1, S, D), F, kind="ExternalOutput").ap()
    build(nc, aps, out)
    r = run_bass_kernel_spmd(nc, [arrays], core_ids=[0])
    return r.results[0]["out_0"]
```

```python
import math
from contextlib import ExitStack

import numpy as np
import concourse.bass as bass
from concourse import mybir
from concourse.alu_op_type import AluOpType as ALU

F = mybir.dt.float32
R = mybir.dt.float32r
I32 = mybir.dt.int32
ACT = mybir.ActivationFunctionType
AX = mybir.AxisListType.X

D = 1024
S = 256
EPS = 1e-6
NEG = -1e30
D_IN = 7424
FF1 = 2816
FF2 = 3584
NEXP = 8

NR = 4
NX = 1
NP = 3
LOOK = 2
CAP = 128

C_ID, C_BO, C_J, C_ROT = 0, 128, 256, 512
C_COS, C_SIN, C_FD, C_FL = 640, 896, 1152, 1408
C_OHA, C_OHC, C_TRI, C_IOTA, C_EIDX, C_ONE = 2432, 2816, 3200, 3328, 3456, 3464
C_END = 3592


def t5_bucket(d):
    d = max(d, 0)
    if d < 16:
        return d
    f = np.float32
    lr = np.log(f(d) / f(16)) / f(math.log(2048 / 16))
    return min(16 + int(f(lr * f(16))), 31)


def constants():
    c = np.zeros((128, C_END), np.float32)
    p = np.arange(128)
    c[:, C_ID:C_ID + 128] = np.eye(128)
    c[:, C_BO:C_BO + 128] = (p[:, None] // 64 == p[None, :] // 64)
    for m in range(128):
        half = (m // 16) % 2
        c[m + 16 if half == 0 else m - 16, C_ROT + m] = -1.0 if half == 0 else 1.0
    tok = np.arange(S, dtype=np.float32)
    row, col = np.floor(tok / 64), np.mod(tok, 64)
    freqs = (np.float32(10000.0) ** (-np.arange(16, dtype=np.float32) / np.float32(16))).astype(np.float32)
    for m in range(128):
        d = m % 64
        ang = (row if d < 32 else col) * freqs[d % 16]
        c[m, C_COS:C_COS + S] = np.cos(ang.astype(np.float32))
        c[m, C_SIN:C_SIN + S] = np.sin(ang.astype(np.float32))
    w = 2 * np.pi * np.outer(p, p) / 128
    c[:, C_FD:C_FD + 128] = np.cos(w) / math.sqrt(128)
    c[:, C_FD + 128:C_FD + 256] = np.sin(w) / math.sqrt(128)
    for tb in range(2):
        w = 2 * np.pi * np.outer(p + 128 * tb, np.arange(S)) / S
        c[:, C_FL + tb * 512:C_FL + tb * 512 + 256] = np.cos(w) / math.sqrt(S)
        c[:, C_FL + tb * 512 + 256:C_FL + tb * 512 + 512] = -np.sin(w) / math.sqrt(S)
    for t in range(384):
        diff = 255 - t
        b = t5_bucket(diff)
        c[b, C_OHA + t] = 1.0
        c[b, C_OHC + t] = 1.0
        c[32, C_OHA + t] = 0.0 if 0 <= diff < 128 else NEG
        c[32, C_OHC + t] = 0.0 if diff >= 0 else NEG
    c[:, C_TRI:C_TRI + 128] = (p[:, None] < p[None, :])
    c[:, C_IOTA:C_IOTA + 128] = p[None, :]
    c[:, C_EIDX:C_EIDX + 8] = 8 - np.arange(8)
    c[:, C_ONE:C_ONE + 128] = 1.0
    c[:, C_J:C_J + 128] = np.eye(128)[::-1]
    return c


class Queue:

    def __init__(self, eng, sem):
        self.eng, self.sem, self.n, self.seen = eng, sem, 0, {}

    def wait(self, *toks):
        for t in toks:
            if t is None:
                continue
            if isinstance(t, list):
                self.wait(*t)
                continue
            sem, val = t
            if self.seen.get(id(sem), 0) < val:
                self.seen[id(sem)] = val
                self.eng.wait_ge(sem, val)

    def do(self, fn, *toks):
        self.wait(*toks)
        self.n += 1
        fn(self.eng).then_inc(self.sem, 1)
        return (self.sem, self.n)

    def run(self, fn, *toks):
        self.wait(*toks)
        fn(self.eng)

    def now(self):
        return (self.sem, self.n)


class Chunks(list):
    pass


class Slots:

    pump = None

    def __init__(self, bufs):
        self.bufs, self.free, self.order = bufs, [[] for _ in bufs], list(range(len(bufs)))

    def busy(self):
        return not self.order

    def get(self):
        while self.busy() and Slots.pump():
            pass
        assert self.order, "every slot is in use"
        k = self.order.pop(0)
        return k, self.bufs[k], self.free[k]

    def put(self, k, *toks):
        assert k not in self.order
        self.free[k] = list(toks)
        self.order.append(k)


def build(nc, a, out, dbg=None):
    ctx = ExitStack()
    dbg = dbg or {}

    def sb(name, shape, dt=F, c=ctx):
        return c.enter_context(nc.sbuf_tensor(name, shape, dt))

    def sem(name):
        return ctx.enter_context(nc.semaphore(name))

    with ctx:
        pe, act, dve, pool, sp = (Queue(g, sem("s_" + n)) for n, g in (
            ("pe", nc.tensor), ("act", nc.scalar), ("dve", nc.vector), ("pool", nc.gpsimd), ("sp", nc.sync)))

        def fence():
            return [pe.now(), act.now(), dve.now(), pool.now()]

        raw = [sb(f"raw{i}", [128, 2048]) for i in range(NR)]
        whi = [sb(f"whi{i}", [128, 2048], R) for i in range(NP)]
        wlo = [sb(f"wlo{i}", [128, 2048], R) for i in range(NP)]
        X = sb("X", [128, 8, S])
        cst = sb("cst", [128, 384])
        one = sb("one", [128, 128])
        vt = [sb(f"vt{i}", [128, 128]) for i in range(4)]
        modT = [sb("mod_m", [128, 48]), sb("mod_a0", [128, 48]), sb("mod_c0", [128, 16]), sb("mod_a1", [128, 48])]
        macc = [sb(f"macc{i}", [128, 512]) for i in range(4)]
        eps_c = sb("eps_c", [128, 1])
        csil = sb("csil", [128, 24])
        nA = sb("nA", [128, 64])
        sqb = [sb(f"sqb{i}", [128, 512]) for i in range(3)]
        rst = [sb(f"rst{i}", [128, 512]) for i in range(2)]
        banks = [ctx.enter_context(nc.psum_tensor(f"bk{i}", [128, 512], F)) for i in range(8)]
        PG = PT = Slots(banks)
        MA = Slots(macc)
        SQ = Slots(sqb)
        RS = Slots(rst)
        s_raw = [sem(f"s_raw{i}") for i in range(NR + NX)]
        ident, bones, JJ = cst[:, C_ID:C_ID + 128], cst[:, C_BO:C_BO + 128], cst[:, C_J:C_J + 128]

        dma_sems = {}

        def load(name, pairs, *toks, q=pool):
            s = dma_sems.setdefault(name, [None, 0])
            if s[0] is None:
                s[0] = sem("d_" + name)
            q.wait(*toks)
            for o, i in pairs:
                s[1] += 16
                q.eng.dma_start(o, i).then_inc(s[0], 16)
            return (s[0], s[1])

        plan = []

        def gslabs(w, kts, c0, tag):
            r = []
            for k0 in range(0, kts, 8):
                nk = min(8, kts - k0)
                src = w[k0 * 128:(k0 + nk) * 128, c0:c0 + 256].rearrange("(k p) n -> p k n", p=128)
                r.append(("G", tag, src, nk, 256))
            return r

        def mslabs(w, g, which):
            return [("M", (which, g, k0), w[k0 * 512:(k0 + 1) * 512, g * 512:(g + 1) * 512]
                     .rearrange("(k p) n -> p k n", p=128), 4, 512) for k0 in range(2)]

        def mix(gs, ms):
            o, j = [], 0
            for i, g in enumerate(gs):
                o.append(g)
                while j < len(ms) and j < (i + 1) * len(ms) / len(gs):
                    o.append(ms[j])
                    j += 1
            return o + ms[j:]

        wmod, ada = a["w_mod"][0], a["ada_w_2"]
        win, wbr, wout, wup, wdn = a["w_in"][0], a["w_branch"][0], a["w_out"][0], a["w_up"][0], a["w_down"][0]
        wqkv, wo2, fwo = a["attn_w_qkv_2"][0], a["attn_w_o_2"][0], a["fnet_w_o_2"][0]
        f1, f3, f2 = a["ff_w1_2"][0], a["ff_w3_2"][0], a["ff_w2_2"][0]
        z_cols = [0, 256, 512, 2816, 3072, 3328, 3584, 3840, 4096]
        for j in range(4):
            z_cols += [768 + 256 * j, 1792 + 256 * j]
        gcols = lambda cs: [4352 + 1024 * g + 256 * c for c in cs for g in range(3)]
        zs = lambda cols: [s for c in cols for s in gslabs(win, 8, c, ("z", c))]
        m0 = [s for g in range(4, 12) for s in mslabs(wmod, g, 0)]
        m1 = [s for g in range(12) for s in mslabs(ada[0], g, 1)]
        m3 = [s for g in range(12) for s in mslabs(ada[1], g, 3)]
        for g in (0, 1, 2, 3):
            plan += mslabs(wmod, g, 0)
        plan += mix(zs(z_cols[:9]), m0[:6])
        plan += zs(z_cols[9:] + gcols((0, 1)))
        bs = [s for c in range(4) for s in gslabs(wbr, 16, 256 * c, ("br", c))]
        bs += [s for c in range(4) for s in gslabs(wout, 8, 256 * c, ("out", c))]
        plan += mix(zs(gcols((2, 3))) + bs[:-2], m0[6:] + m1[:8]) + bs[-2:]
        us = [s for c in range(11) for s in gslabs(wup, 8, 256 * c, ("ug", c)) + gslabs(wup, 8, FF1 + 256 * c, ("uv", c))]
        ds_ = [s for c in range(4) for s in gslabs(wdn, 22, 256 * c, ("dn", c))]
        plan += us
        plan += mix(ds_, m1[8:14])
        q2 = [s for c in range(4) for j in (4 + c, 8 + c, c) for s in gslabs(wqkv, 8, 256 * j, ("qkv", j))]
        q2 += [s for c in range(4) for s in gslabs(wo2, 8, 256 * c, ("wo", c))]
        plan += mix(q2, m1[14:])
        ff = [s for c in range(14) for s in gslabs(f1, 8, 256 * c, ("f1", c)) + gslabs(f3, 8, 256 * c, ("f3", c))]
        ff += [s for c in range(4) for s in gslabs(f2, 28, 256 * c, ("f2", c))]
        plan += mix(ff, m3)
        plan += [s for c in range(4) for s in gslabs(fwo, 8, 256 * c, ("fn", c))]
        first_moe = [len(plan)]

        def eslabs(e, n):
            r = []
            for tag, w in (("w1", a["moe_w1_2"][0, e]), ("w3", a["moe_w3_2"][0, e])):
                for k0 in range(2):
                    r.append(("G", (tag, e, n, k0), w[k0 * 512:(k0 + 1) * 512, n * 512:(n + 1) * 512]
                              .rearrange("(k p) n -> p k n", p=128), 4, 512))
            return r

        def dslabs(e, n):
            w = a["moe_w2_2"][0, e]
            return [("G", ("w2", e, n, j), w[n * 512 + j * 256:n * 512 + (j + 1) * 256, :]
                     .rearrange("(k p) n -> p k n", p=128), 2, 1024) for j in range(2)]

        steps = [(e, n) for e in range(NEXP) for n in range(7)]
        for i, (e, n) in enumerate(steps):
            plan += eslabs(e, n)
            if i:
                plan += dslabs(*steps[i - 1])
        plan += dslabs(*steps[-1])
        if "cut" in dbg:
            plan = plan[:dbg["cut"](plan)]

        where, used, wide, nxt, raw_free = [], {}, [None], [0], {}

        def place(i):
            while len(where) <= i:
                j = len(where)
                s = j % NR if j < first_moe[0] else (j - first_moe[0]) % (NR + NX)
                if j >= first_moe[0] and s < NR:
                    s = (s + first_moe[0]) % NR
                c, p = used.get(s, (0, None))
                where.append((s, c + 1, p))
                used[s] = (c + 1, j)
            return where[i]

        def raw_view(i):
            _, _, src, nk, nc_ = plan[i]
            return raw[place(i)[0]][:, :nk * nc_].rearrange("p (k n) -> p k n", k=nk)

        def issue():
            while nxt[0] < len(plan):
                i = nxt[0]
                s, _, p = place(i)
                if (s >= NR and wide[0] is None) or (p is not None and p not in raw_free):
                    return
                sp.wait(raw_free[p] if p is not None else (wide[0] if s >= NR else None))
                sp.eng.dma_start(raw_view(i), plan[i][2]).then_inc(s_raw[s], 16)
                nxt[0] += 1

        def arrived(i):
            s, c, _ = place(i)
            return (s_raw[s], 16 * c)

        pair_free = [[] for _ in range(NP)]
        pair_of, gcount = {}, [0]
        pair_tok = {}
        pos, ahead = [0], [0]
        mstate = {}

        def prepare(i):
            kind, tag, src, nk, w = plan[i]
            if kind == "G":
                k = gcount[0] % NP
                gcount[0] += 1
                assert pair_free[k] is not None
                n = nk * w
                r, h, l = raw[place(i)[0]][:, :n], whi[k][:, :n], wlo[k][:, :n]
                th = act.do(lambda e: e.copy(h, r), arrived(i), pair_free[k])
                tl = dve.do(lambda e: e.tensor_tensor(l, r, h.bitcast(F), ALU.subtract), arrived(i), th, pair_free[k])
                pair_free[k] = None
                pair_of[i], pair_tok[i] = k, [th, tl]
                raw_free[i] = [th, tl]
            else:
                which, g, k0 = tag
                v = raw_view(i)
                cs = [(which, {0: 0, 1: 8, 3: 8}[which])]
                if which == 1 and g < 4:
                    cs.append((2, 16))
                toks = []
                for dest, c0 in cs:
                    if k0 == 0:
                        kk, acc, fr = MA.get()
                        mstate[dest, g] = [kk, acc, fr]
                    kk, acc, t = mstate[dest, g]
                    for j in range(4):
                        sc = csil[:, c0 + k0 * 4 + j:c0 + k0 * 4 + j + 1]
                        if k0 == 0 and j == 0:
                            t = dve.do(lambda e, sc=sc, acc=acc: e.tensor_scalar(acc[:, :], v[:, 0, :], sc, None, ALU.mult),
                                       arrived(i), t, csil_tok)
                        else:
                            t = dve.do(lambda e, sc=sc, acc=acc, j=j: e.scalar_tensor_tensor(
                                out=acc[:, :], in0=v[:, j, :], scalar=sc, in1=acc[:, :], op0=ALU.mult, op1=ALU.add),
                                arrived(i), t)
                    mstate[dest, g][2] = t
                    toks.append(t)
                raw_free[i] = toks
            issue()

        mod_tok = {}

        def reduce_mod(i):
            which, g, k0 = plan[i][1]
            if k0 == 0:
                return
            for dest in [which] + ([2] if which == 1 and g < 4 else []):
                kk, acc, t = mstate.pop((dest, g))
                b, bank, fr = PT.get()
                for j in range(4):
                    f = lambda e, j=j, acc=acc, bank=bank: e.matmul(bank[:, j:j + 1], acc[:, j * 128:(j + 1) * 128],
                                                                    one[:, 0:1], start=True, stop=True)
                    if j < 3:
                        pe.run(f, t, fr, t_c)
                    else:
                        tp = pe.do(f)
                MA.put(kk, tp)
                bias = {0: vec("b_mod"), 1: vec("ada_b0"), 2: vec("ada_b0"), 3: vec("ada_b1")}[dest]
                td = dve.do(lambda e, g=g, bank=bank, dest=dest: e.tensor_tensor(
                    modT[dest][:, 4 * g:4 * g + 4], bank[:, 0:4], bias[:, 4 * g:4 * g + 4], ALU.add), tp, vec_tok)
                PT.put(b, td)
                mod_tok[dest, g] = td

        def advance(n):
            while ahead[0] < min(n, len(plan)):
                prepare(ahead[0])
                ahead[0] += 1

        def skip_mods():
            while pos[0] < len(plan) and plan[pos[0]][0] == "M":
                advance(pos[0] + 1 + LOOK)
                reduce_mod(pos[0])
                pos[0] += 1

        def take(tag):
            skip_mods()
            i = pos[0]
            assert plan[i][1] == tag, (plan[i][1], tag)
            advance(i + 1)
            k = pair_of[i]
            pe.wait(pair_tok[i])
            nk, w = plan[i][3], plan[i][4]
            h = whi[k][:, :nk * w].rearrange("p (k n) -> p k n", k=nk)
            l = wlo[k][:, :nk * w].rearrange("p (k n) -> p k n", k=nk)
            pos[0] += 1
            return i, h, l, nk

        def done(i, tok):
            pair_free[pair_of[i]] = [tok]
            advance(i + 1 + LOOK)
            skip_mods()

        live, pending = [], []
        LIMIT = [2]

        running = [False]

        def pump():
            if running[0] or not (live or pending):
                return False
            tick()
            return True

        Slots.pump = pump

        def tick():
            running[0] = True
            step()
            running[0] = False

        RATE = [2]

        def step():
            while pending and len(live) < LIMIT[0]:
                live.append(pending.pop(0))
            for _ in range(min(RATE[0], len(live))):
                g = live.pop(0)
                try:
                    next(g)
                    live.append(g)
                except StopIteration:
                    pass
                while pending and len(live) < LIMIT[0]:
                    live.append(pending.pop(0))

        def drain():
            while live or pending:
                tick()

        def now(g):
            for _ in g:
                pass

        def mm3(outp, wh, wl, xh, xl, first, last, **kw):
            seq = [(wh, xh), (wh, xl), (wl, xh)]
            for n, (l, r) in enumerate(seq):
                st, sp_ = first and n == 0, last and n == 2
                pe.run(lambda e, l=l, r=r, st=st, sp_=sp_: e.matmul(outp, l, r, start=st, stop=sp_, **kw))

        def mark(fn, *t):
            return pe.do(fn, *t)

        def step_wait(xt, kk):
            if isinstance(xt, Chunks):
                pe.wait(xt[kk])

        def gemmT(tags_kts, xh, xl, xt, evac, two=None, keep=False):
            k_all = sum(k for _, k in tags_kts)
            if not isinstance(xt, Chunks):
                pe.wait(xt)
            b, bank, fr = PG.get()
            pe.wait(fr)
            if two:
                b2, bank2, fr2 = PG.get()
                pe.wait(fr2)
                jobs = [(two[0], two[1], two[2], m, (bank, bank2)[m][:, 0:S], True) for m in range(2)]
                jobs += [(xh, xl, xt, m, (bank, bank2)[m][:, S:512], False) for m in range(2)]
            else:
                jobs = [(xh, xl, xt, m, bank[:, m * S:(m + 1) * S], m == 0) for m in range(2)]
            kb = 0
            for n_, (tag, _) in enumerate(tags_kts):
                i, h, l, nk = take(tag)
                for n, (hi, lo, tk, m, o, first) in enumerate(jobs):
                    for k in range(nk):
                        kk = kb + k
                        step_wait(tk, kk)
                        for q, (w, xx) in enumerate([(h, hi), (h, lo), (l, hi)]):
                            st = kk == 0 and q == 0 and first
                            sp_ = kk == k_all - 1 and q == 2
                            f = lambda e, w=w, xx=xx, k=k, kk=kk, m=m, st=st, sp_=sp_, o=o: e.matmul(
                                o, w[:, k, m * 128:(m + 1) * 128], xx[:, kk, :], start=st, stop=sp_,
                                skip_group_check=True)
                            if n == len(jobs) - 1 and k == nk - 1 and q == 2:
                                t = pe.do(f)
                            else:
                                pe.run(f)
                    if n < len(jobs) - 1:
                        tick()
                kb += nk
                done(i, t)
                if n_ < len(tags_kts) - 1:
                    tick()
            if two:
                r1, r2 = evac((bank, bank2), t)
                PG.put(b, *r1)
                PG.put(b2, *r2)
            else:
                if keep:
                    evac(bank, t, b)
                else:
                    PG.put(b, *evac(bank, t))
            tick()

        def mm32(o, l, r, st=True, sp_=True, *t):
            return pe.do(lambda e: e.matmul(o, l, r, start=st, stop=sp_), *t)

        vrows = {}
        vlist = [[("norm_mix", a["norm_mix"], 8), ("norm_ffn", a["norm_ffn"], 8), ("b_mod", a["b_mod"], 48),
                  ("rcb", a["rnn_conv_b"], 8), ("rcw", a["rnn_conv_w"], 32), ("gab", a["rnn_gate_a_b"], 8),
                  ("gxb", a["rnn_gate_x_b"], 8), ("lam", a["rnn_lambda"], 8)],
                 [("ada_b0", a["ada_b_2"][0:1], 48), ("ada_b1", a["ada_b_2"][1:2], 48),
                  ("n10", a["norm1_g_2"][0:1], 8), ("n11", a["norm1_g_2"][1:2], 8),
                  ("n20", a["norm2_g_2"][0:1], 8), ("n21", a["norm2_g_2"][1:2], 8)],
                 [("fcw01", a["ffn_conv_w"][:, 0:2, :], 88), ("fbo", a["fnet_b_o_2"], 8),
                  ("fing", a["final_g_2"].rearrange("(o d) -> o d", o=1), 8)],
                 [("fcw2", a["ffn_conv_w"][:, 2:3, :], 44), ("fcb", a["ffn_conv_b"], 44), ("sub", a["attn_subln_g_2"], 1),
                  ("qa", a["qnorm_a"], 0), ("ka", a["knorm_a"], 0), ("qc", a["qnorm_c"], 0), ("kc", a["knorm_c"], 0)]]

        with ExitStack() as c0:
            vn = [sb(f"vn{i}", [128, 128], F, c0) for i in range(4)]
            rnat = sb("rnat", [64, 16], F, c0)
            rows = sb("rrow", [16, 384], F, c0)
            oh = sb("oh", [64, 768], F, c0)
            bias_dram = nc.dram_tensor("bias_rows", (16, 384), F, kind="Internal")
            crow = sb("crow", [24, 128], F, c0)
            t_cr = load("crow", [(crow[8 * n:8 * n + 8, :], ap) for n, ap in enumerate((
                a["c"].rearrange("o (n p) -> (o n) p", p=128), a["c_2"].rearrange("o (n p) -> (o n) p", p=128),
                a["c_ctx_2"].rearrange("(n p) -> n p", p=128)))], q=sp)
            t_c = load("cst", [(cst[:, :], a["consts"][:, 0:384]), (one[:, :], a["consts"][:, C_ONE:C_ONE + 128])], q=act)
            issue()
            b, bank, fr = PT.get()
            t = pe.do(lambda e: e.transpose(bank[:, 0:24], crow[:, :], ident[0:24, 0:24]), t_cr, t_c)
            pairs = []
            t_ms = [dve.do(lambda e, i=i: e.memset(vn[i][:, :], 0.0)) for i in range(4)]
            for ti, vl in enumerate(vlist):
                r0 = 0
                for name, ap, n in vl:
                    vrows[name] = (ti, r0, max(n, 1))
                    if n == 0:
                        for hh_ in range(2):
                            pairs.append((vn[ti][r0:r0 + 1, hh_ * 64:hh_ * 64 + 64], ap))
                        r0 += 1
                        continue
                    flat = ap
                    while len(flat.shape) > 2:
                        flat = flat.rearrange("a b c -> a (b c)")
                    pairs.append((vn[ti][r0:r0 + n, :], flat.rearrange("o (n p) -> (o n) p", p=128)))
                    r0 += n
                assert r0 <= 128
            csil_tok = act.do(lambda e: e.activation(csil[:, :], bank[:, 0:24], ACT.Silu), t)
            PT.put(b, csil_tok)
            xn = sb("xn", [128, 2, 1024], F, c0)
            t_x = load("xn", [(xn[:, tb_, :], a["x"][0, tb_ * 128:(tb_ + 1) * 128, :]) for tb_ in range(2)], q=act)
            t_v = load("vec", pairs[:12], t_ms, q=act)
            t_v2 = load("vec2", pairs[12:], t_ms)
            t_r = load("rel", [(rnat[0:32, :], a["rel_bias"]), (oh[0:33, :], a["consts"][0:33, C_OHA:C_OHA + 768])])
            t_r1 = pool.do(lambda e: e.memset(rnat[32:64, :], 1.0))
            t_eps = dve.do(lambda e: e.memset(eps_c[:, :], EPS))

            def vec(name):
                ti, r0, n = vrows[name]
                return vt[ti][:, r0:r0 + n]

            x_tok = []

            def transpose_in(src, t_src, dst, toks=()):
                r = Chunks()
                for c in range(0, 8, 2):
                    b, bank, fr = PT.get()
                    for m in range(2):
                        for tb_ in range(2):
                            t = pe.do(lambda e, m=m, tb_=tb_, c=c, bank=bank: e.transpose(
                                bank[:, m * 256 + tb_ * 128:m * 256 + tb_ * 128 + 128],
                                src[:, tb_, (c + m) * 128:(c + m + 1) * 128], ident), fr, t_src, t_c)
                    tt = act.do(lambda e, c=c, bank=bank: e.copy(
                        dst[:, c:c + 2, :], bank[:, :].rearrange("p (m t) -> p m t", m=2)), t, *toks)
                    PT.put(b, tt)
                    r += [[tt], [tt]]
                    yield r

            class Stats:

                def __init__(self):
                    self.b, self.bank, self.fr = PT.get()
                    self.n, self.q = 0, []

                def flush(self, last=False):
                    k, sq, t = self.q.pop(0)
                    for m in range(2):
                        st, sp_ = self.n == 0 and m == 0, last and m == 1
                        t = pe.do(lambda e, m=m, st=st, sp_=sp_, sq=sq: e.matmul(self.bank[:, 0:S], one[:, :], sq[:, m * S:(m + 1) * S],
                                                                          start=st, stop=sp_), t, self.fr, t_c)
                    SQ.put(k, t)
                    self.n += 1
                    return t

                def add(self, src, toks):
                    if len(self.q) > 1:
                        self.flush()
                    k, sq, fs = SQ.get()
                    t = act.do(lambda e: e.activation(sq[:, :].rearrange("p (m t) -> p m t", m=2), src, ACT.Square), toks, fs)
                    self.q.append((k, sq, t))

                def close(self, width):
                    while self.q:
                        t = self.flush(len(self.q) == 1)
                    k, r, fr = RS.get()
                    t = act.do(lambda e: e.activation(r[:, 0:S], self.bank[:, 0:S], ACT.Ln, bias=eps_c[:, 0:1], scale=1.0 / width), t, fr, t_eps)
                    PT.put(self.b, t)
                    return k, r, act.do(lambda e: e.activation(r[:, 0:S], r[:, 0:S], ACT.Exp, scale=-0.5), t)

            xst = Stats()
            for r in transpose_in(xn, t_x, X):
                c = len(r) - 2
                xst.add(X[:, c:c + 2, :], r[-1])
            x_tok = r
            b, bank, fr = PT.get()
            for i in range(4):
                t = pe.do(lambda e, i=i: e.transpose(bank[:, i * 128:(i + 1) * 128], vn[i][:, :], ident), fr, t_v, t_v2, t_c)
            for i in range(4):
                vec_tok = act.do(lambda e, i=i: e.copy(vt[i][:, :], bank[:, i * 128:(i + 1) * 128]), t)
            PT.put(b, vec_tok)
            xrs = xst.close(D)
            skip_mods()
            b, bank, fr = PT.get()
            b2, bank2, fr2 = PT.get()
            t1 = pe.do(lambda e: e.matmul(bank[0:16, 0:384], rnat[0:33, :], oh[0:33, 0:384], start=True, stop=True),
                       fr, t_r, t_r1)
            t2 = pe.do(lambda e: e.matmul(bank2[0:16, 0:384], rnat[0:33, :], oh[0:33, 384:768], start=True, stop=True), fr2)
            rows2 = sb("rrow2", [16, 384], F, c0)
            ta = act.do(lambda e: e.activation(rows[:, :], bank[0:16, 0:384], ACT.Copy, scale=8.0), t1)
            tb = act.do(lambda e: e.activation(rows2[:, :], bank2[0:16, 0:384], ACT.Copy, scale=8.0), t2)
            PT.put(b, ta)
            PT.put(b2, tb)
            t_bias = load("brow", [(bias_dram[0:8, :], rows[0:8, :]), (bias_dram[8:16, :], rows2[8:16, :])], ta, tb)
            init_fence = fence() + [t_bias]

        def split(dst_h, dst_l, src, toks, wfree=None):
            th = act.do(lambda e: e.copy(dst_h, src), toks, wfree)
            return [th, dve.do(lambda e: e.tensor_tensor(dst_l, src, dst_h.bitcast(F), ALU.subtract), toks, wfree, th)]

        def coeff(col, g, scale, mt):
            o = nA[:, col:col + 8]
            return o, dve.do(lambda e: e.scalar_tensor_tensor(out=o, in0=scale, scalar=1.0, in1=g, op0=ALU.add, op1=ALU.mult), mt, vec_tok)

        def modulate(x, rs, xtoks, A, At, shift, st, hh, hl, wfree):
            k, r, tr = rs
            r_ = r[:, 0:S]
            toks, q = Chunks(), []

            def low(c, kt, tt, t2s):
                for m, t2 in enumerate(t2s):
                    t3 = dve.do(lambda e, m=m: e.scalar_tensor_tensor(
                        out=hl[:, c + m, :], in0=tt[:, m * S:(m + 1) * S], scalar=shift[:, c + m:c + m + 1],
                        in1=hh[:, c + m, :].bitcast(F), op0=ALU.add, op1=ALU.subtract), t2, wfree)
                    toks.append([t2, t3])
                SQ.put(kt, t3)
            for c in range(0, 8, 2):
                kt, tt, ft = SQ.get()
                t2s = []
                for m in range(2):
                    t1 = dve.do(lambda e, c=c, tt=tt, m=m: e.scalar_tensor_tensor(
                        out=tt[:, m * S:(m + 1) * S], in0=x[:, c + m, :], scalar=A[:, c + m:c + m + 1],
                        in1=r_, op0=ALU.mult, op1=ALU.mult), tr, At, ft, xtoks)
                    t2s.append(act.do(lambda e, c=c, tt=tt, m=m: e.activation(
                        hh[:, c + m, :], tt[:, m * S:(m + 1) * S], ACT.Identity, bias=shift[:, c + m:c + m + 1]), t1, st, wfree))
                q.append((c, kt, tt, t2s))
                if len(q) > 1:
                    low(*q.pop(0))
            low(*q.pop(0))
            RS.put(k, t1)
            return toks

        c1 = ctx.enter_context(ExitStack())
        HH, HL = sb("HH", [128, 8, S], R, c1), sb("HL", [128, 8, S], R, c1)
        O = sb("O", [128, 16, S], F, c1)
        QA, QC = O[:, 0:4, :], O[:, 12:16, :]
        GT1 = sb("GT1", [128, 3, 4, S], F, c1)
        o_tok = [[] for _ in range(16)]
        c2 = ctx.enter_context(ExitStack())
        KA, KC = sb("KA", [128, 2, S], F, c2), sb("KC", [128, 4, S], F, c2)
        VA, VC = sb("VA", [128, 2, 128], F, c2), sb("VC", [128, 2, 512], F, c2)
        BI = Slots([sb(f"bi{i}", [128, S], F, c2) for i in range(4)])
        SS = Slots([sb(f"ss{i}", [128, 384], F, c2) for i in range(3)])
        PTB = Slots([sb(f"ptb{i}", [128, 384], F, c2) for i in range(3)])
        st8 = Slots([sb(f"st{i}", [128, 16], F, c2) for i in range(4)])
        snk = sb("snk", [128, 16], F, c2)
        GW = Slots([sb(f"gw{i}", [128, 2, 2, 128], F, c2) for i in range(2)])
        clam = sb("clam", [128, 48], F, c2)
        RT = Slots([[sb(f"rt{i}_{n}", [128, 2, S], F, c2) for n in range(5)] for i in range(2)])
        t_snk = load("snk", [(snk[:, 0:8], a["sinks"].broadcast_to([128, 8]))], init_fence)
        t_snk = dve.do(lambda e: e.tensor_scalar(snk[:, 8:16], snk[:, 0:8], -1.0, None, ALU.mult), t_snk)
        t_m = [pool.do(lambda e, w=w: e.memset(w[:, :, :, :], 0.0), init_fence) for w in GW.bufs]
        gsrc = [w.rearrange("(m two) c d -> two c m d", two=2) for w in (a["rnn_gate_a_w"][0], a["rnn_gate_x_w"][0])]

        def load_gates(j):
            k, gw, fr = GW.get()
            prs = [(gw[two * 64:two * 64 + 64, w, :, two * 64:two * 64 + 64], gsrc[w][two][:, 2 * j:2 * j + 2, :])
                   for w in range(2) for two in range(2)]
            return k, gw, load(f"gw{k}", prs, t_m, fr)

        L = vec("lam")
        cl = lambda i: clam[:, 8 * i:8 * i + 8]
        t = dve.do(lambda e: e.tensor_scalar(cl(1), L, -1.0, None, ALU.mult), vec_tok, init_fence)
        t = dve.do(lambda e: e.tensor_tensor(cl(1), cl(1), L, ALU.min), t)
        t = act.do(lambda e: e.activation(cl(2), cl(1), ACT.Exp), t)
        t = dve.do(lambda e: e.tensor_scalar(cl(3), cl(2), 1.0, None, ALU.add), t)
        ta = act.do(lambda e: e.activation(cl(4), cl(3), ACT.Ln), t)
        t = dve.do(lambda e: e.tensor_scalar(cl(3), cl(3), -1.0, None, ALU.add), ta)
        t = dve.do(lambda e: e.tensor_scalar(cl(5), cl(3), 0.0, None, ALU.is_equal), t)
        t = dve.do(lambda e: e.tensor_tensor(cl(4), cl(4), cl(2), ALU.mult), ta, t)
        t = dve.do(lambda e: e.tensor_tensor(cl(2), cl(2), cl(5), ALU.mult), t)
        t = dve.do(lambda e: e.tensor_tensor(cl(3), cl(3), cl(5), ALU.add), t)
        t = dve.do(lambda e: e.reciprocal(cl(3), cl(3)), t)
        t = dve.do(lambda e: e.tensor_tensor(cl(4), cl(4), cl(3), ALU.mult), t)
        t = dve.do(lambda e: e.tensor_tensor(cl(4), cl(4), cl(2), ALU.add), t)
        t = dve.do(lambda e: e.tensor_scalar(cl(5), L, -1.0, 0.0, ALU.mult, ALU.max), t)
        t = dve.do(lambda e: e.tensor_tensor(cl(4), cl(4), cl(5), ALU.add), t)
        t_lam = dve.do(lambda e: e.tensor_scalar(cl(0), cl(4), -8.0, None, ALU.mult), t)

        A0, At0 = coeff(0, vec("norm_mix"), modT[0][:, 8:16], mod_tok[0, 3])
        h_tok = modulate(X, xrs, x_tok, A0, At0, modT[0][:, 0:8], mod_tok[0, 1], HH, HL, init_fence)

        z_ready = {}

        def norm_pair(bank, b, tok, dst, gains, n=512):
            while SQ.busy() or RS.busy():
                yield
            k, sq, fs = SQ.get()
            t = act.do(lambda e: e.activation(sq[:, 0:n], bank[:, 0:n], ACT.Square), tok, fs)
            yield
            while PT.busy() or RS.busy():
                yield
            b2, bank2, fr2 = PT.get()
            t = pe.do(lambda e: e.matmul(bank2[:, 0:n], bones, sq[:, 0:n], start=True, stop=True), t, fr2)
            SQ.put(k, t)
            kr, r, fr = RS.get()
            t = act.do(lambda e: e.activation(r[:, 0:n], bank2[:, 0:n], ACT.Ln, bias=eps_c[:, 0:1], scale=1.0 / 64), t, fr, t_eps)
            PT.put(b2, t)
            t = act.do(lambda e: e.activation(r[:, 0:n], r[:, 0:n], ACT.Exp, scale=-0.5), t)
            td = dve.do(lambda e: e.scalar_tensor_tensor(out=dst, in0=bank[:, 0:n], scalar=gains,
                                                         in1=r[:, 0:n], op0=ALU.mult, op1=ALU.mult), t, vec_tok, init_fence)
            RS.put(kr, td)
            PT.put(b, td)
            return td

        def norm_heads(dst, gains, key):
            def ev(bank, tok, b):
                def rest():
                    z_ready.setdefault(key, []).append((yield from norm_pair(bank, b, tok, dst, gains)))
                pending.append(rest())
            return ev

        LIMIT[0] = 3
        for j in range(2):
            gemmT([(("z", 256 * j), 8)], HH, HL, h_tok, norm_heads(QA[:, 2 * j:2 * j + 2, :].rearrange("p m t -> p (m t)"), vec("qa"), "qa"), keep=True)

        i, h, l, nk = take(("z", 512))
        b, bank, fr = PG.get()
        b2, bank2, fr2 = PG.get()
        pe.wait(fr, fr2)
        for k in range(8):
            for q, (w, xx) in enumerate([(h, HH), (h, HL), (l, HH)]):
                pe.run(lambda e, w=w, xx=xx, k=k, q=q: e.matmul(bank[:, 0:S], w[:, k, 0:128], xx[:, k, :],
                                                                 start=(k == 0 and q == 0), stop=(k == 7 and q == 2)))

        def natural(bankx, h, l, hi, lo, tbs, nks=8, cols=256):
            for n, tb_ in enumerate(tbs):
                for k in range(nks):
                    for q, (xx, w) in enumerate([(hi, h), (lo, h), (hi, l)]):
                        f = lambda e, w=w, xx=xx, k=k, q=q, n=n, tb_=tb_: e.matmul(
                            bankx[:, n * 256:n * 256 + cols], xx[:, k, tb_ * 128:(tb_ + 1) * 128], w[:, k, 0:cols],
                            start=(k == 0 and q == 0), stop=(k == nks - 1 and q == 2))
                        if n == len(tbs) - 1 and k == nks - 1 and q == 2:
                            return pe.do(f)
                        pe.run(f)

        t = natural(bank2, h, l, HH, HL, [0, 1])
        done(i, t)
        t_va = act.do(lambda e: e.copy(VA[:, :, :], bank2[:, :].rearrange("p (b n) -> p b n", b=2)[:, :, 128:256]), t, init_fence)
        PG.put(b2, t_va)

        def ka_rest(b, bank, tok):
            kr, r, fr = RT.get()
            z = r[0].rearrange("p m t -> p (m t)")[:, 0:S]
            td = yield from norm_pair(bank, b, tok, z, vec("ka"), S)
            yield
            while PT.busy():
                yield
            b, bank, fr = PT.get()
            for j in range(2):
                for r0 in (0, 64):
                    t = pe.do(lambda e, j=j, r0=r0: e.matmul(bank[r0:r0 + 64, j * S:(j + 1) * S], ident[:, 64 * j:64 * j + 64],
                                                             z, start=True, stop=True), fr, td)
            t = act.do(lambda e: e.copy(KA[:, :, :], bank[:, :].rearrange("p (m t) -> p m t", m=2)), t, init_fence)
            PT.put(b, t)
            RT.put(kr, t)
            z_ready["ka"] = [t]
        pending.append(ka_rest(b, bank, t))
        tick()

        def load_bias(h):
            kb, bi, fb = BI.get()
            src = bass.AP(bias_dram, h * 384, [[1, 128], [1, 256]])
            return kb, bi, load("bi%d" % kb, [(bi[:, :], src)], fb, t_bias, init_fence)

        def attention(h, q, k, v, toks, och, swa):
            while BI.busy():
                yield
            kb, bi, t_b = load_bias(h)
            yield
            while PT.busy() or SS.busy() or PTB.busy() or st8.busy():
                yield
            b, bank, fr = PT.get()
            spans = [(0, 128), (128, 256)]
            for qb, (o0, nk) in enumerate(spans):
                o = bank[:, o0:o0 + nk]
                pe.run(lambda e: e.matmul(o, q[:, qb * 128:qb * 128 + 128], k[:, 0:nk], start=True, stop=False), fr, toks)
                t = pe.do(lambda e: e.matmul(o, JJ[:, :], bi[:, 256 - nk:256], start=False, stop=True), t_b, t_snk)
            BI.put(kb, t)
            ks, s, fs = SS.get()
            kq, st, fq = st8.get()
            for qb, (o0, nk) in enumerate(spans):
                t1 = dve.do(lambda e: e.tensor_reduce(st[:, qb:qb + 1], bank[:, o0:o0 + nk], AX, ALU.max), t, fq, init_fence)
            if swa:
                t1 = dve.do(lambda e: e.tensor_scalar(st[:, 2:4], st[:, 0:2], -0.125, snk[:, 8 + h:9 + h], ALU.mult, ALU.min), t1, t_snk)
            else:
                t1 = dve.do(lambda e: e.tensor_scalar(st[:, 2:4], st[:, 0:2], -0.125, None, ALU.mult), t1)
            for qb, (o0, nk) in enumerate(spans):
                t2 = act.do(lambda e: e.activation(s[:, o0:o0 + nk], bank[:, o0:o0 + nk], ACT.Exp, bias=st[:, 2 + qb:3 + qb], scale=0.125,
                                                   accum_out=st[:, 4 + qb:5 + qb]), t1, fs, init_fence)
            PT.put(b, t2)
            if swa:
                t3 = act.do(lambda e: e.activation(st[:, 6:8], st[:, 2:4], ACT.Exp, bias=snk[:, h:h + 1]), t_snk)
                t2 = dve.do(lambda e: e.tensor_tensor(st[:, 4:6], st[:, 4:6], st[:, 6:8], ALU.add), t3)
            t4 = dve.do(lambda e: e.reciprocal(st[:, 8:10], st[:, 4:6]), t2)
            for qb, (o0, nk) in enumerate(spans):
                t5 = dve.do(lambda e: e.tensor_scalar(s[:, o0:o0 + nk], s[:, o0:o0 + nk], st[:, 8 + qb:9 + qb], None, ALU.mult), t4)
            st8.put(kq, t5)
            yield
            while PT.busy():
                yield
            b, bank, fr = PT.get()
            for j in range(3):
                t = pe.do(lambda e, j=j: e.transpose(bank[:, j * 128:(j + 1) * 128], s[:, j * 128:(j + 1) * 128], ident), fr, t5)
            SS.put(ks, t)
            kp, pt, fp = PTB.get()
            t5 = act.do(lambda e: e.copy(pt[:, :], bank[:, 0:384]), t, fp, init_fence)
            PT.put(b, t5)
            yield
            while PT.busy():
                yield
            b, bank, fr = PT.get()
            r0 = 64 * (h % 2)
            o = bank[r0:r0 + 64, 0:S]
            pe.run(lambda e: e.matmul(o, v[:, 0, :], pt[:, 0:S], start=True, stop=False, skip_group_check=True), fr, t5, toks)
            t = pe.do(lambda e: e.matmul(bank[r0:r0 + 64, 128:S], v[:, 1, :], pt[:, S:384], start=False, stop=True, skip_group_check=True))
            PTB.put(kp, t)
            th = act.do(lambda e: e.copy(O[r0:r0 + 64, och, :], o), t)
            PT.put(b, th)
            o_tok[och].append(th)

        def swa(h):
            r0 = 64 * (h % 2)
            while "ka" not in z_ready or len(z_ready.get("qa", ())) < 2:
                yield
            yield from attention(h, QA[r0:r0 + 64, h // 2, :], KA[r0:r0 + 64, h // 4, :],
                                 VA[:, :, (h // 4) * 64:(h // 4) * 64 + 64], z_ready["qa"] + z_ready["ka"] + [t_va], h // 2, True)

        for j in range(2):
            gemmT([(("z", 2816 + 256 * j), 8)], HH, HL, h_tok, norm_heads(QC[:, 2 * j:2 * j + 2, :].rearrange("p m t -> p (m t)"), vec("qc"), "qc"), keep=True)
        pending += [swa(h) for h in range(0, 4)]
        LIMIT[0] = 4
        for j in range(2):
            gemmT([(("z", 3328 + 256 * j), 8)], HH, HL, h_tok, norm_heads(KC[:, 2 * j:2 * j + 2, :].rearrange("p m t -> p (m t)"), vec("kc"), "kc"), keep=True)
        pending += [swa(h) for h in range(4, 8)]
        t_vc = []
        for j in range(2):
            i, h, l, nk = take(("z", 3840 + 256 * j))
            b, bank, fr = PG.get()
            pe.wait(fr)
            t = natural(bank, h, l, HH, HL, [0, 1])
            done(i, t)
            tt = act.do(lambda e, j=j, bank=bank: e.copy(VC[:, :, 256 * j:256 * j + 256], bank[:, :].rearrange("p (b n) -> p b n", b=2)), t, init_fence)
            PG.put(b, tt)
            t_vc.append(tt)
            tick()

        def moba(h):
            r0 = 64 * (h % 2)
            while len(z_ready.get("qc", ())) < 2 or len(z_ready.get("kc", ())) < 2:
                yield
            yield from attention(8 + h, QC[r0:r0 + 64, h // 2, :], KC[r0:r0 + 64, h // 2, :],
                                 VC[:, :, h * 64:h * 64 + 64], z_ready["qc"] + z_ready["kc"] + t_vc, 12 + h // 2, False)
        pending += [moba(h) for h in range(8)]

        def tt2(o, x, y, op, *t):
            return dve.do(lambda e: e.tensor_tensor(o, x, y, op), *t)

        rcw, rcb = vec("rcw"), vec("rcb")
        def rnn_xr(j, kr, rt, fr):
            def ev(bank, tok):
                for m in range(2):
                    c = 2 * j + m
                    t = act.do(lambda e: e.activation(rt[0][:, m, :], bank[:, m * S:(m + 1) * S], ACT.Identity,
                                                      bias=rcb[:, c:c + 1], scale=rcw[:, 24 + c:25 + c]), tok, fr, init_fence, vec_tok)
                for k in (2, 1, 0):
                    for m in range(2):
                        c, d = 2 * j + m, 3 - k
                        t = dve.do(lambda e: e.scalar_tensor_tensor(
                            out=rt[0][:, m, d:S], in0=bank[:, m * S:(m + 1) * S - d], scalar=rcw[:, 8 * k + c:8 * k + c + 1],
                            in1=rt[0][:, m, d:S], op0=ALU.mult, op1=ALU.add), t, dve.now() if m == 0 else None)
                rnn_x[j] = [t]
                return [t]
            return ev

        def rnn_yr(j):
            def ev(bank, tok):
                t = act.do(lambda e: e.copy(O[:, 4 + 2 * j:6 + 2 * j, :], bank[:, :].rearrange("p (m t) -> p m t", m=2)), tok, init_fence)
                rnn_y[j] = [t]
                return [t]
            return ev
        rnn_x, rnn_y = {}, {}

        def rnn(j, kr, rt, fr, kgw, gw, t_gw):
            xc, ga, gx, ww, gl = rt
            yy = O[:, 4 + 2 * j:6 + 2 * j, :]
            t = tt2(gl[:, :, :], yy, yy, ALU.mult, rnn_y[j], fr, init_fence)
            t = dve.do(lambda e: e.tensor_scalar(gl[:, :, :], gl[:, :, :], 0.044715, 1.0, ALU.mult, ALU.add), t)
            t_gl = tt2(gl[:, :, :], gl[:, :, :], yy, ALU.mult, t)
            bks = []
            for w in range(2):
                while PT.busy():
                    yield
                b, bank, f = PT.get()
                for m in range(2):
                    t = pe.do(lambda e: e.matmul(bank[:, m * S:(m + 1) * S], gw[:, w, m, :], xc[:, m, :],
                                                 start=True, stop=True), f, rnn_x[j], t_gw)
                bks.append((b, bank, t))
            GW.put(kgw, t)
            t_gate = []
            for (b, bank, t), dst, bn in zip(bks, (ga, gx), ("gab", "gxb")):
                for m in range(2):
                    c = 2 * j + m
                    t = act.do(lambda e: e.activation(dst[:, m, :], bank[:, m * S:(m + 1) * S], ACT.Sigmoid, bias=vec(bn)[:, c:c + 1]),
                               t, fr, init_fence, vec_tok)
                PT.put(b, t)
                t_gate.append(t)
            tg = act.do(lambda e: e.activation(gl[:, :, :], gl[:, :, :], ACT.Sigmoid, scale=2.0 * math.sqrt(2.0 / math.pi)), t_gl)
            for m in range(2):
                c = 2 * j + m
                ta = act.do(lambda e: e.activation(ga[:, m, :], ga[:, m, :], ACT.Exp, scale=clam[:, c:c + 1]), t_gate[0], t_lam)
            tu = tt2(gx[:, :, :], gx[:, :, :], xc[:, :, :], ALU.mult, t_gate[1])
            tg = tt2(gl[:, :, :], gl[:, :, :], yy, ALU.mult, tg)
            yield
            t = dve.do(lambda e: e.tensor_scalar(ww[:, :, :], ga[:, :, :], -1.0, 1.0, ALU.mult, ALU.add), ta, fr, init_fence)
            t = dve.do(lambda e: e.scalar_tensor_tensor(out=ww[:, :, :], in0=ga[:, :, :], scalar=1.0, in1=ww[:, :, :], op0=ALU.add, op1=ALU.mult), t)
            t = dve.do(lambda e: e.tensor_scalar(ww[:, :, :], ww[:, :, :], 1e-18, None, ALU.max), t)
            t = act.do(lambda e: e.activation(ww[:, :, :], ww[:, :, :], ACT.Ln), t)
            t = act.do(lambda e: e.activation(ww[:, :, :], ww[:, :, :], ACT.Exp, scale=0.5), t)
            yield
            t = dve.do(lambda e: e.memset(ww[:, :, 0:1], 1.0), t)
            t = tt2(gx[:, :, :], gx[:, :, :], ww[:, :, :], ALU.mult, tu, t)
            for m in range(2):
                ts = dve.do(lambda e: e.tensor_tensor_scan(ww[:, m, :], ga[:, m, :], gx[:, m, :], 0.0, ALU.mult, ALU.add), t)
            t = tt2(yy, ww[:, :, :], gl[:, :, :], ALU.mult, tg, ts)
            o_tok[4 + 2 * j] = o_tok[5 + 2 * j] = [t]
            RT.put(kr, t)

        for j in range(4):
            RTj = RT.get()
            gwj = load_gates(j)
            gemmT([(("z", 768 + 256 * j), 8)], HH, HL, h_tok, rnn_xr(j, *RTj))
            gemmT([(("z", 1792 + 256 * j), 8)], HH, HL, h_tok, rnn_yr(j))
            pending.insert(0, rnn(j, *RTj, *gwj))

        def gate_ev(dst, wf):
            def ev(bank, tok):
                t = act.do(lambda e: e.copy(dst, bank[:, :].rearrange("p (m t) -> p m t", m=2)), tok, wf)
                g_raw.append(t)
                return [t]
            return ev
        g_raw = []
        for c in range(2):
            for g in range(3):
                gemmT([(("z", 4352 + 1024 * g + 256 * c), 8)], HH, HL, h_tok, gate_ev(GT1[:, g, 2 * c:2 * c + 2, :], init_fence))
        drain()
        fz1 = fence()
        c2.close()

        c2 = ctx.enter_context(ExitStack())
        GT2 = sb("GT2", [128, 3, 4, S], F, c2)
        OH, OL = sb("OH", [128, 16, S], R, c2), sb("OL", [128, 16, S], R, c2)
        g_tok = [act.do(lambda e: e.activation(GT1[:, :, :, :], GT1[:, :, :, :], ACT.Sigmoid), g_raw)]
        oh_tok = Chunks([None] * 16)
        for c in (4, 6, 8, 10, 0, 2, 12, 14):
            oh_tok[c] = oh_tok[c + 1] = split(OH[:, c:c + 2, :], OL[:, c:c + 2, :], O[:, c:c + 2, :], [o_tok[c], o_tok[c + 1]], fz1)
        for c in range(2):
            for g in range(3):
                def ev(bank, tok):
                    t = act.do(lambda e: e.activation(GT2[:, g, 2 * c:2 * c + 2, :], bank[:, :].rearrange("p (m t) -> p m t", m=2), ACT.Sigmoid), tok, fz1)
                    g_tok.append(t)
                    return [t]
                gemmT([(("z", 4352 + 1024 * g + 256 * (c + 2)), 8)], HH, HL, h_tok, ev)
        mtok = Chunks()
        hfree = pe.now()
        for c in range(4):
            bk = [PG.get(), PG.get(), PG.get()]
            pe.wait(*[x[2] for x in bk], oh_tok)
            kb = 0
            for s_ in range(2):
                i, h, l, nk = take(("br", c))
                for m in range(2):
                    for k in range(8):
                        kk = kb + k
                        g = 0 if kk < 4 else (1 if kk < 12 else 2)
                        lo_, hi_ = ((0, 3), (4, 11), (12, 15))[g]
                        for q, (w, xx) in enumerate([(h, OH), (h, OL), (l, OH)]):
                            st = kk == lo_ and q == 0 and m == 0
                            sp_ = kk == hi_ and q == 2
                            f = lambda e, w=w, xx=xx, k=k, kk=kk, m=m, g=g, st=st, sp_=sp_, bk=bk: e.matmul(
                                bk[g][1][:, m * S:(m + 1) * S], w[:, k, m * 128:(m + 1) * 128], xx[:, kk, :],
                                start=st, stop=sp_, skip_group_check=True)
                            if m == 1 and k == 7 and q == 2:
                                t = pe.do(f)
                            else:
                                pe.run(f)
                kb += 8
                done(i, t)
            G_, c_ = (GT1, 2 * c) if c < 2 else (GT2, 2 * c - 4)
            gs = [G_[:, g, c_:c_ + 2, :] for g in range(3)]
            bv = [x[1][:, :].rearrange("p (m t) -> p m t", m=2) for x in bk]
            tts = [tt2(gs[g], bv[g], gs[g], ALU.mult, t, g_tok) for g in range(3)]
            for g in range(3):
                PG.put(bk[g][0], tts[g])
            t1 = tt2(gs[0], gs[0], gs[1], ALU.add, tts)
            t1 = tt2(gs[0], gs[0], gs[2], ALU.add, t1)
            t1 = split(HH[:, 2 * c:2 * c + 2, :], HL[:, 2 * c:2 * c + 2, :], gs[0], t1, hfree)
            mtok += [t1, t1]

        def residual(gate, gt):
            r, st_ = Chunks(), Stats()

            def mk(c):
                def ev(bank, tok):
                    for m in range(2):
                        cc = 2 * c + m
                        tk = dve.do(lambda e, cc=cc, m=m: e.scalar_tensor_tensor(
                            out=X[:, cc, :], in0=bank[:, m * S:(m + 1) * S], scalar=gate[:, cc:cc + 1], in1=X[:, cc, :],
                            op0=ALU.mult, op1=ALU.add), tok, gt)
                    r.extend([[tk], [tk]])
                    st_.add(X[:, 2 * c:2 * c + 2, :], tk)
                    return [tk]
                return ev
            return r, mk, st_

        skip_mods()
        r, mk, xst = residual(modT[0][:, 16:24], mod_tok[0, 5])
        for c in range(4):
            gemmT([(("out", c), 8)], HH, HL, mtok, mk(c))
        x_tok, xrs = r, xst.close(D)
        if dbg.get("stop") == "mix":
            return finish(locals())
        c2.close()
        hfree = fence()

        c1.close()
        c1 = ctx.enter_context(ExitStack())
        HHc, HLc = sb("HHc", [128, 8, S], R, c1), sb("HLc", [128, 8, S], R, c1)
        HH, HL = sb("HH2", [128, 8, S], R, c1), sb("HL2", [128, 8, S], R, c1)
        c2 = ctx.enter_context(ExitStack())
        FH, FL = sb("FH", [128, 22, S], R, c2), sb("FL", [128, 22, S], R, c2)
        A1, At1 = coeff(8, vec("norm_ffn"), modT[0][:, 32:40], mod_tok[0, 9])
        h_tok = modulate(X, xrs, x_tok, A1, At1, modT[0][:, 24:32], mod_tok[0, 7], HH, HL, hfree)
        UC = Slots([sb(f"uc{i}", [128, 2, S], F, c2) for i in range(3)])
        cw = lambda k, c: (vec("fcw01")[:, 44 * k + c:44 * k + c + 1] if k < 2 else vec("fcw2")[:, c:c + 1])
        f_tok, cur = Chunks(), {}

        def conv_ev(which, c):
            def ev(bank, tok):
                k_, u, fu = UC.get()
                for m in range(2):
                    ch = 22 * which + 2 * c + m
                    t = act.do(lambda e: e.activation(u[:, m, :], bank[:, m * S:(m + 1) * S], ACT.Identity,
                                                      bias=vec("fcb")[:, ch:ch + 1], scale=cw(2, ch)), tok, fu, hfree)
                for k in (1, 0):
                    for m in range(2):
                        ch, d = 22 * which + 2 * c + m, 2 - k
                        t = dve.do(lambda e: e.scalar_tensor_tensor(
                            out=u[:, m, d:S], in0=bank[:, m * S:(m + 1) * S - d], scalar=cw(k, ch), in1=u[:, m, d:S],
                            op0=ALU.mult, op1=ALU.add), t)
                if which == 0:
                    ta = act.do(lambda e: e.activation(u[:, :, :], u[:, :, :], ACT.Silu), t)
                    cur["g"] = (k_, u, ta)
                else:
                    kg, g, ta = cur["g"]
                    tm = tt2(u[:, :, :], u[:, :, :], g[:, :, :], ALU.mult, ta, t)
                    r = split(FH[:, 2 * c:2 * c + 2, :], FL[:, 2 * c:2 * c + 2, :], u[:, :, :], tm, hfree)
                    f_tok.extend([r, r])
                    UC.put(kg, tm)
                    UC.put(k_, *r)
                return [t]
            return ev

        c3 = ctx.enter_context(ExitStack())
        cn, cT = sb("cn", [128, 1, 1024], F, c3), sb("cT", [128, 8, S], F, c3)

        def context():
            ct = Chunks([[] for _ in range(8)])
            wf = hfree
            for tb_ in range(2):
                t_x = load("cn", [(cn[:, 0, :], a["ctx_2"][0, tb_ * 128:(tb_ + 1) * 128, :])], wf)
                yield
                yield
                for c in range(0, 8, 4):
                    while PT.busy():
                        yield
                    b, bank, fr = PT.get()
                    for j in range(4):
                        t = pe.do(lambda e: e.transpose(bank[:, j * 128:(j + 1) * 128], cn[:, 0, (c + j) * 128:(c + j + 1) * 128], ident), fr, t_x)
                    wf = t
                    t = act.do(lambda e: e.copy(cT[:, c:c + 4, tb_ * 128:tb_ * 128 + 128], bank[:, :].rearrange("p (j t) -> p j t", j=4)), t, hfree)
                    PT.put(b, t)
                    for j in range(4):
                        ct[c + j].append(t)
                    yield
            while PT.busy():
                yield
            st_ = Stats()
            for c in range(0, 8, 2):
                while SQ.busy():
                    yield
                st_.add(cT[:, c:c + 2, :], ct[c])
                yield
            while RS.busy():
                yield
            Ac, Act_ = coeff(16, vec("n10"), modT[2][:, 8:16], mod_tok[2, 3])
            rs = st_.close(D)
            yield
            while len(SQ.order) < 3:
                yield
            ctx_tok.extend(modulate(cT, rs, ct, Ac, Act_, modT[2][:, 0:8], mod_tok[2, 1], HHc, HLc, hfree))
        ctx_tok = Chunks()
        pending.append(context())
        for c in range(11):
            gemmT([(("ug", c), 8)], HH, HL, h_tok, conv_ev(0, c))
            gemmT([(("uv", c), 8)], HH, HL, h_tok, conv_ev(1, c))
        skip_mods()
        r, mk, xst = residual(modT[0][:, 40:48], mod_tok[0, 11])
        for c in range(4):
            gemmT([(("dn", c), 8), (("dn", c), 8), (("dn", c), 6)], FH, FL, f_tok, mk(c))
        drain()
        x_tok, xrs = r, xst.close(D)
        c3.close()
        c2.close()
        hfree = fence()
        if dbg.get("stop") == "b1":
            return finish(locals())

        c2 = ctx.enter_context(ExitStack())
        Ax, Axt = coeff(24, vec("n10"), modT[1][:, 8:16], mod_tok[1, 3])
        h_tok = modulate(X, xrs, x_tok, Ax, Axt, modT[1][:, 0:8], mod_tok[1, 1], HH, HL, hfree)
        Q2, K2 = sb("Q2", [128, 8, S], F, c2), sb("K2", [128, 8, 512], F, c2)
        V2 = sb("V2", [128, 4, 1024], F, c2)
        cs = sb("cs", [128, 640], F, c2)
        rot = cs[:, 512:640]
        cfree = hfree
        t_cs = load("cs", [(cs[:, 0:512], a["consts"][:, C_COS:C_COS + 512]), (rot, a["consts"][:, C_ROT:C_ROT + 128])], cfree)
        z_ready = {}

        def rope(c, dst, tz, key):
            while PT.busy() or SQ.busy():
                yield
            b, bank, fr = PT.get()
            k, z, fz = SQ.get()
            zz = z[:, :].rearrange("p (m t) -> p m t", m=2)
            for m in range(2):
                t = pe.do(lambda e: e.matmul(bank[:, m * S:(m + 1) * S], rot, dst[:, m, :], start=True, stop=True), fr, tz, t_cs)
            for m in range(2):
                t1 = tt2(z[:, m * S:(m + 1) * S], bank[:, m * S:(m + 1) * S], cs[:, 256:512], ALU.mult, t, t_cs, fz)
            PT.put(b, t1)
            for m in range(2):
                t2 = tt2(dst[:, m, :], dst[:, m, :], cs[:, 0:256], ALU.mult, t, t_cs)
            t3 = tt2(dst, dst, zz, ALU.add, t1, t2)
            SQ.put(k, t3)
            z_ready[key, c] = t3

        def q_ev(c):
            def ev(bank, tok):
                tz = act.do(lambda e: e.copy(Q2[:, 2 * c:2 * c + 2, :], bank[:, :].rearrange("p (m t) -> p m t", m=2)), tok, cfree)
                pending.append(rope(c, Q2[:, 2 * c:2 * c + 2, :], tz, "q"))
                return [tz]
            return ev

        def k_ev(c):
            def ev(bks, tok):
                tz = [act.do(lambda e: e.copy(K2[:, 2 * c + m, :], bks[m][:, :]), tok, cfree) for m in range(2)]
                pending.append(rope(c, K2[:, 2 * c:2 * c + 2, S:512], tz, "k"))
                return [tz[0:1], tz[1:2]]
            return ev

        lq = sb("lq", [128, 4, 64], F, c2)
        lt = sb("lt", [128, 16], F, c2)
        t_l = load("lq", [(lq[:, n, :], a[nm].broadcast_to([128, 64])) for n, nm in
                          enumerate(("attn_lq1_2", "attn_lk1_2", "attn_lq2_2", "attn_lk2_2"))], cfree)
        lam_init = 0.8 - 0.6 * math.exp(-0.3 * 0)
        for n in range(2):
            t = dve.do(lambda e, n=n: e.tensor_tensor_reduce(lq[:, 2 * n, :], lq[:, 2 * n, :], lq[:, 2 * n + 1, :], 1.0, 0.0,
                                                             ALU.mult, ALU.add, lt[:, n:n + 1]), t_l, cfree)
        t = act.do(lambda e: e.activation(lt[:, 2:4], lt[:, 0:2], ACT.Exp), t)
        t_lm = dve.do(lambda e: e.scalar_tensor_tensor(out=lt[:, 4:5], in0=lt[:, 2:3], scalar=lam_init, in1=lt[:, 3:4],
                                                       op0=ALU.add, op1=ALU.subtract), t)
        LAM = lt[:, 4:5]
        t_sg = dve.do(lambda e: e.tensor_scalar(lt[:, 5:6], vec("sub"), 1.0 - lam_init, None, ALU.mult), vec_tok, t_lm)
        SUBG = lt[:, 5:6]
        PP = Slots([sb(f"pp{i}", [128, 2, 512], F, c2) for i in range(2)])
        AT = Slots([sb(f"at{i}", [128, 4, S], F, c2) for i in range(2)])
        ST = Slots([sb(f"sr{i}", [128, 12], F, c2) for i in range(2)])
        a_tok = [None] * 8

        def da_head(h):
            while ("q", h // 2) not in z_ready or ("k", h // 2) not in z_ready or AT.busy():
                yield
            ka, at, fa = AT.get()
            tq = [z_ready["q", h // 2], z_ready["k", h // 2]]
            for qb in range(2):
                while PP.busy() or ST.busy() or len(PT.order) < 2:
                    yield
                kp, pp, fp = PP.get()
                ks, s, fs = ST.get()
                bks = []
                for n in range(2):
                    r0 = 64 * n
                    b, bank, fr = PT.get()
                    t = pe.do(lambda e: e.matmul(bank[:, :], Q2[r0:r0 + 64, h, qb * 128:qb * 128 + 128],
                                                 K2[r0:r0 + 64, h, :], start=True, stop=True), fr, tq)
                    t = dve.do(lambda e: e.tensor_reduce(s[:, n:n + 1], bank[:, :], AX, ALU.max), t, fs, cfree)
                    bks.append((b, bank))
                t = dve.do(lambda e: e.tensor_scalar(s[:, 2:4], s[:, 0:2], -0.125, None, ALU.mult), t)
                for n, (b, bank) in enumerate(bks):
                    te = act.do(lambda e: e.activation(pp[:, n, :], bank[:, :], ACT.Exp, bias=s[:, 2 + n:3 + n], scale=0.125,
                                                       accum_out=s[:, 4 + n:5 + n]), t, fp, cfree)
                    PT.put(b, te)
                yield
                t = dve.do(lambda e: e.reciprocal(s[:, 6:8], s[:, 4:6]), te)
                t = tt2(s[:, 8:9], s[:, 7:8], LAM, ALU.mult, t, t_lm)
                t = dve.do(lambda e: e.tensor_scalar(pp[:, 1, :], pp[:, 1, :], s[:, 8:9], None, ALU.mult), t)
                t = dve.do(lambda e: e.scalar_tensor_tensor(out=pp[:, 0, :], in0=pp[:, 0, :], scalar=s[:, 6:7], in1=pp[:, 1, :],
                                                            op0=ALU.mult, op1=ALU.subtract), t)
                ST.put(ks, t)
                yield
                while PT.busy():
                    yield
                b, bank, fr = PT.get()
                for j in range(4):
                    tp = pe.do(lambda e: e.transpose(bank[:, j * 128:(j + 1) * 128], pp[:, 0, j * 128:(j + 1) * 128], ident), fr, t)
                PP.put(kp, tp)
                t = act.do(lambda e: e.copy(at[:, :, qb * 128:qb * 128 + 128], bank[:, :].rearrange("p (j q) -> p j q", j=4)),
                           tp, fa if qb == 0 else None, cfree)
                PT.put(b, t)
            yield
            while PT.busy():
                yield
            b, bank, fr = PT.get()
            for j in range(4):
                tp = pe.do(lambda e: e.matmul(bank[:, 0:S], V2[:, j, h * 128:(h + 1) * 128], at[:, j, :], start=(j == 0), stop=(j == 3)),
                           fr, t, z_ready["v", h // 2])
            AT.put(ka, tp)
            while SQ.busy():
                yield
            k, sq, fs = SQ.get()
            ts = act.do(lambda e: e.activation(sq[:, 0:S], bank[:, 0:S], ACT.Square), tp, fs)
            to = act.do(lambda e: e.copy(Q2[:, h, :], bank[:, 0:S]), tp)
            PT.put(b, to)
            yield
            while PT.busy() or RS.busy():
                yield
            b, bank, fr = PT.get()
            tp = pe.do(lambda e: e.matmul(bank[:, 0:S], one[:, :], sq[:, 0:S], start=True, stop=True), ts, fr)
            SQ.put(k, tp)
            kr, r, fr = RS.get()
            t = act.do(lambda e: e.activation(r[:, 0:S], bank[:, 0:S], ACT.Ln, bias=eps_c[:, 0:1], scale=1.0 / 128), tp, fr)
            PT.put(b, t)
            t = act.do(lambda e: e.activation(r[:, 0:S], r[:, 0:S], ACT.Exp, scale=-0.5), t)
            t = dve.do(lambda e: e.scalar_tensor_tensor(out=Q2[:, h, :], in0=Q2[:, h, :], scalar=SUBG, in1=r[:, 0:S], op0=ALU.mult, op1=ALU.mult), t, t_sg, to)
            RS.put(kr, t)
            a_tok[h] = [t]

        LIMIT[0], RATE[0] = 4, 2
        for c in range(4):
            gemmT([(("qkv", 4 + c), 8)], HH, HL, h_tok, k_ev(c), two=(HHc, HLc, ctx_tok))
            i, h, l, nk = take(("qkv", 8 + c))
            bb = [PG.get(), PG.get()]
            pe.wait(bb[0][2], bb[1][2])
            t = natural(bb[0][1], h, l, HHc, HLc, [0, 1])
            tick()
            t2 = natural(bb[1][1], h, l, HH, HL, [0, 1])
            done(i, t2)
            z_ready["v", c] = []
            for n in range(2):
                tt = act.do(lambda e: e.copy(V2[:, 2 * n:2 * n + 2, 256 * c:256 * c + 256],
                                             bb[n][1][:, :].rearrange("p (b n) -> p b n", b=2)), (t, t2)[n], cfree)
                PG.put(bb[n][0], tt)
                z_ready["v", c].append(tt)
            tick()
            gemmT([(("qkv", c), 8)], HH, HL, h_tok, q_ev(c))
            pending += [da_head(2 * c), da_head(2 * c + 1)]
        hf3 = pe.now()
        drain()
        aready = Chunks()
        for c in range(0, 8, 2):
            r = split(HH[:, c:c + 2, :], HL[:, c:c + 2, :], Q2[:, c:c + 2, :], [a_tok[c], a_tok[c + 1]], hf3)
            aready += [r, r]
        r, mk, xst = residual(modT[1][:, 16:24], mod_tok[1, 5])
        for c in range(4):
            gemmT([(("wo", c), 8)], HH, HL, aready, mk(c))
        x_tok, xrs = r, xst.close(D)
        c2.close()
        c1.close()
        hfree = fence()
        if dbg.get("stop") == "attn":
            return finish(locals())
        c2 = ctx.enter_context(ExitStack())
        HH, HL = sb("HH4", [128, 8, S], R, c2), sb("HL4", [128, 8, S], R, c2)
        FH, FL = sb("FH4", [128, 28, S], R, c2), sb("FL4", [128, 28, S], R, c2)
        UC = Slots([sb(f"ud{i}", [128, 2, S], F, c2) for i in range(2)])
        A1, At1 = coeff(32, vec("n20"), modT[1][:, 32:40], mod_tok[1, 9])
        h_tok = modulate(X, xrs, x_tok, A1, At1, modT[1][:, 24:32], mod_tok[1, 7], HH, HL, hfree)
        f_tok, cur = Chunks(), {}

        def f1_ev(bank, tok):
            k, u, fu = UC.get()
            t = act.do(lambda e: e.activation(u[:, :, :], bank[:, :].rearrange("p (m t) -> p m t", m=2), ACT.Silu), tok, fu, hfree)
            cur["u"] = (k, u, t)
            return [t]

        def f3_ev(c):
            def ev(bank, tok):
                k, u, tu = cur["u"]
                tm = tt2(u[:, :, :], bank[:, :].rearrange("p (m t) -> p m t", m=2), u[:, :, :], ALU.mult, tok, tu)
                r = split(FH[:, 2 * c:2 * c + 2, :], FL[:, 2 * c:2 * c + 2, :], u[:, :, :], tm, hfree)
                f_tok.extend([r, r])
                UC.put(k, *r)
                return [tm]
            return ev
        for c in range(14):
            gemmT([(("f1", c), 8)], HH, HL, h_tok, f1_ev)
            gemmT([(("f3", c), 8)], HH, HL, h_tok, f3_ev(c))
        skip_mods()
        r, mk, xst = residual(modT[1][:, 40:48], mod_tok[1, 11])
        for c in range(4):
            gemmT([(("f2", c), 8), (("f2", c), 8), (("f2", c), 8), (("f2", c), 4)], FH, FL, f_tok, mk(c))
        x_tok, xrs = r, xst.close(D)
        c2.close()
        hfree = fence()
        if dbg.get("stop") == "ffn2":
            return finish(locals())

        skip_mods()
        c2 = ctx.enter_context(ExitStack())
        FX = sb("FX", [128, 8, S], F, c2)
        FN = sb("FN", [128, 2, 8, 256], F, c2)
        HH, HL = sb("HH5", [128, 8, S], R, c2), sb("HL5", [128, 8, S], R, c2)
        fcs = sb("fcs", [128, 1280], F, c2)
        t_f = load("fcs", [(fcs[:, :], a["consts"][:, C_FD:C_FD + 1280])], hfree)
        A1, At1 = coeff(40, vec("n11"), modT[3][:, 8:16], mod_tok[3, 3])

        def norm_full(dst, rs, A, At, shift, st, toks, wf):
            k, r, t = rs
            o = Chunks()
            for c in range(8):
                t1 = dve.do(lambda e, c=c: e.scalar_tensor_tensor(out=dst[:, c, :], in0=X[:, c, :], scalar=A[:, c:c + 1],
                                                                  in1=r[:, 0:S], op0=ALU.mult, op1=ALU.mult), t, toks, At, wf)
                if shift is not None:
                    t1 = act.do(lambda e, c=c: e.activation(dst[:, c, :], dst[:, c, :], ACT.Identity, bias=shift[:, c:c + 1]), t1, st)
                o.append([t1])
            RS.put(k, dve.now())
            return o
        xt = norm_full(FX, xrs, A1, At1, modT[3][:, 0:8], mod_tok[3, 1], x_tok, hfree)
        gb = nA[:, 56:64]
        t_gb = tt2(gb, modT[3][:, 16:24], vec("fbo"), ALU.mult, mod_tok[3, 5], vec_tok)
        for c in range(8):
            t_gb = dve.do(lambda e: e.tensor_scalar(X[:, c, :], X[:, c, :], gb[:, c:c + 1], None, ALU.add), t_gb, xt)
        tn = []
        for g in range(8):
            b, bank, fr = PG.get()
            for tb_ in range(2):
                t = pe.do(lambda e, g=g, tb_=tb_, bank=bank: e.matmul(bank[:, tb_ * 256:tb_ * 256 + 256], FX[:, g, tb_ * 128:tb_ * 128 + 128],
                                                                     fcs[:, 0:256], start=True, stop=True), fr, xt[g], t_f)
            t = act.do(lambda e, g=g, bank=bank: e.copy(FN[:, :, g, :], bank[:, :].rearrange("p (b n) -> p b n", b=2)), t, hfree)
            PG.put(b, t)
            tn.append(t)
        f_tok = Chunks()
        for g in range(0, 8, 2):
            b, bank, fr = PG.get()
            for m in range(2):
                for s_ in range(4):
                    tb_, part = s_ // 2, s_ % 2
                    t = pe.do(lambda e, g=g, m=m, tb_=tb_, part=part, s_=s_, bank=bank: e.matmul(
                        bank[:, m * S:(m + 1) * S], FN[:, tb_, g + m, part * 128:part * 128 + 128],
                        fcs[:, 256 + tb_ * 512 + part * 256:256 + tb_ * 512 + part * 256 + 256],
                        start=(s_ == 0), stop=(s_ == 3)), fr, tn)
            rr = split(HH[:, g:g + 2, :], HL[:, g:g + 2, :], bank[:, :].rearrange("p (m t) -> p m t", m=2), t, hfree)
            PG.put(b, *rr)
            f_tok += [rr, rr]
        r, mk, xst = residual(modT[3][:, 16:24], [mod_tok[3, 5], t_gb])
        for c in range(4):
            gemmT([(("fn", c), 8)], HH, HL, f_tok, mk(c))
        x_tok, xrs = r, xst.close(D)
        c2.close()
        hfree = fence()
        if dbg.get("stop") == "fnet":
            return finish(locals())

        c2 = ctx.enter_context(ExitStack())
        TH, TL = sb("TH", [128, 2, 1024], R, c2), sb("TL", [128, 2, 1024], R, c2)
        MO = sb("MO", [128, 8, S], F, c2)
        misc = sb("misc", [128, 264], F, c2)
        RO = sb("RO", [128, 2, 96], F, c2)
        RK = sb("RK", [128, 2, 8], F, c2)
        CN = sb("CN", [128, 64], F, c2)
        OV = sb("OV", [128, 2, 8], F, c2)
        CI = sb("CI", [128, 4], I32, c2)
        raw += [sb(f"raw{NR + i}", [128, 2048], F, c2) for i in range(NX)]
        wide[0] = hfree
        issue()
        c3 = ctx.enter_context(ExitStack())
        H2 = sb("H2", [128, 8, S], F, c3)
        rw = sb("rw", [128, 8, 8], F, c3)
        A1, At1 = coeff(48, vec("n21"), modT[3][:, 32:40], mod_tok[3, 9])
        xt = norm_full(H2, xrs, A1, At1, modT[3][:, 24:32], mod_tok[3, 7], x_tok, hfree)
        t_rw = load("rw", [(rw[:, :, :], a["moe_router_2"][0].rearrange("(k p) e -> p k e", p=128))], hfree)
        t_mi = load("misc", [(misc[:, 0:264], a["consts"][:, C_TRI:C_TRI + 264])], hfree)
        tri, iota, eix = misc[:, 0:128], misc[:, 128:256], misc[:, 256:264]
        tok_t = []
        for tb_ in range(2):
            for c in range(0, 8, 4):
                b, bank, fr = PG.get()
                for j in range(4):
                    t = pe.do(lambda e, j=j, c=c, tb_=tb_, bank=bank: e.transpose(bank[:, j * 128:(j + 1) * 128],
                                                                                H2[:, c + j, tb_ * 128:tb_ * 128 + 128], ident), fr, xt)
                rr = split(TH[:, tb_, c * 128:c * 128 + 512], TL[:, tb_, c * 128:c * 128 + 512], bank[:, :], t, hfree)
                PG.put(b, *rr)
                tok_t += rr
        ro = lambda tb_, i, n=8: RO[:, tb_, 8 * i:8 * i + n]
        tm = []
        for tb_ in range(2):
            b, bank, fr = PT.get()
            for k in range(8):
                t = pe.do(lambda e, k=k, tb_=tb_, bank=bank: e.matmul(bank[:, 0:8], H2[:, k, tb_ * 128:tb_ * 128 + 128], rw[:, k, :],
                                                                     start=(k == 0), stop=(k == 7)), fr, xt, t_rw)
            lg, eq1, s1, eq2, s2, l2, mk_, gt_, ex = (ro(tb_, i) for i in range(9))
            sc = RO[:, tb_, 72:96]
            t = dve.do(lambda e: e.tensor_copy(lg, bank[:, 0:8]), t, hfree)
            PT.put(b, t)

            def top(lg, eq, sel, v, t):
                t = dve.do(lambda e: e.tensor_reduce(v, lg, AX, ALU.max), t)
                t = dve.do(lambda e: e.tensor_scalar(eq, lg, v, None, ALU.is_equal), t)
                t = tt2(eq, eq, eix, ALU.mult, t, t_mi)
                t = dve.do(lambda e: e.tensor_reduce(sc[:, 7:8], eq, AX, ALU.max), t)
                return dve.do(lambda e: e.tensor_scalar(sel, eq, sc[:, 7:8], None, ALU.is_equal), t)
            t = top(lg, eq1, s1, sc[:, 0:1], t)
            t = dve.do(lambda e: e.tensor_scalar(l2, s1, -3.0e38, None, ALU.mult), t)
            t = dve.do(lambda e: e.tensor_scalar(eq2, s1, -1.0, 1.0, ALU.mult, ALU.add), t)
            t = tt2(eq2, eq2, lg, ALU.mult, t)
            t = tt2(l2, l2, eq2, ALU.add, t)
            t = top(l2, eq2, s2, sc[:, 1:2], t)
            t = tt2(mk_, s1, s2, ALU.add, t)
            t = tt2(sc[:, 2:3], sc[:, 1:2], sc[:, 0:1], ALU.subtract, t)
            t = act.do(lambda e: e.activation(sc[:, 3:4], sc[:, 2:3], ACT.Exp), t)
            t = dve.do(lambda e: e.tensor_scalar(sc[:, 4:5], sc[:, 3:4], 1.0, None, ALU.add), t)
            t = dve.do(lambda e: e.reciprocal(sc[:, 4:5], sc[:, 4:5]), t)
            t = tt2(sc[:, 5:6], sc[:, 3:4], sc[:, 4:5], ALU.mult, t)
            t = dve.do(lambda e: e.tensor_scalar(gt_, s1, sc[:, 4:5], None, ALU.mult), t)
            t = dve.do(lambda e: e.scalar_tensor_tensor(out=gt_, in0=s2, scalar=sc[:, 5:6], in1=gt_, op0=ALU.mult, op1=ALU.add), t)
            tm.append(t)
        tr = []
        for tb_ in range(2):
            b, bank, fr = PT.get()
            if tb_ == 1:
                pe.do(lambda e, bank=bank: e.matmul(bank[:, 0:8], one[:, :], ro(0, 6), start=True, stop=False), fr, tm)
            t = pe.do(lambda e, tb_=tb_, bank=bank: e.matmul(bank[:, 0:8], tri, ro(tb_, 6), start=(tb_ == 0), stop=True), fr, tm, t_mi)
            t = dve.do(lambda e, tb_=tb_, bank=bank: e.tensor_copy(RK[:, tb_, :], bank[:, 0:8]), t, hfree)
            PT.put(b, t)
            t = tt2(RK[:, tb_, :], RK[:, tb_, :], ro(tb_, 6), ALU.mult, t)
            t = dve.do(lambda e, tb_=tb_: e.tensor_scalar(ro(tb_, 8), ro(tb_, 6), 1e4, -1e4, ALU.mult, ALU.add), t)
            tr.append(tt2(RK[:, tb_, :], RK[:, tb_, :], ro(tb_, 8), ALU.add, t))
        b, bank, fr = PT.get()
        pe.do(lambda e: e.matmul(bank[:, 0:8], one[:, :], ro(0, 6), start=True, stop=False), fr, tm)
        t = pe.do(lambda e: e.matmul(bank[:, 0:8], one[:, :], ro(1, 6), start=False, stop=True))
        t_cn = dve.do(lambda e: e.tensor_copy(CN[:, 0:8], bank[:, 0:8]), t, hfree)
        PT.put(b, t_cn)
        t = dve.do(lambda e: e.tensor_scalar(CN[:, 8:16], CN[:, 0:8], float(CAP), None, ALU.is_gt), t_cn)
        t = dve.do(lambda e: e.memset(CN[:, 56:64], 1.0), hfree)
        t = dve.do(lambda e: e.tensor_tensor_scan(CN[:, 16:24], CN[:, 56:64], CN[:, 8:16], 0.0, ALU.mult, ALU.add), t)
        t_ov = [dve.do(lambda e: e.tensor_copy(CN[:, 48:49], CN[:, 23:24]), t)]
        for j in range(3):
            sj = CN[:, 24 + 8 * j:32 + 8 * j]
            t1 = dve.do(lambda e: e.tensor_scalar(sj, CN[:, 16:24], float(j + 1), None, ALU.is_equal), t)
            t1 = tt2(sj, sj, CN[:, 8:16], ALU.mult, t1)
            t1 = dve.do(lambda e: e.tensor_tensor_reduce(CN[:, 56:64], sj, eix, 1.0, 0.0, ALU.mult, ALU.add, CN[:, 49 + j:50 + j]), t1, t_ov)
            t1 = dve.do(lambda e: e.tensor_scalar(CN[:, 49 + j:50 + j], CN[:, 49 + j:50 + j], -1.0, 8.0, ALU.mult, ALU.add), t1)
            t1 = dve.do(lambda e: e.tensor_scalar(CN[:, 49 + j:50 + j], CN[:, 49 + j:50 + j], 7.0, None, ALU.min), t1)
            for tb_ in range(2):
                t1 = dve.do(lambda e: e.tensor_tensor_reduce(CN[:, 56:64], sj, RK[:, tb_, :], 1.0, -float(CAP), ALU.mult, ALU.add,
                                                             OV[:, tb_, j:j + 1]), t1, tr, hfree)
                t1 = dve.do(lambda e: e.tensor_tensor_reduce(CN[:, 56:64], sj, ro(tb_, 7), 1.0, 0.0, ALU.mult, ALU.add,
                                                             OV[:, tb_, 4 + j:5 + j]), t1, tm)
            t_ov.append(t1)
        t_ov.append(dve.do(lambda e: e.memset(OV[:, :, 3:4], -1.0), hfree))
        t_ci = dve.do(lambda e: e.tensor_copy(CI[:, :], CN[:, 48:52]), t_ov)
        t_mo = dve.do(lambda e: e.memset(MO[:, :, :], 0.0), hfree)
        mfree = fence()
        c3.close()
        XH = Slots([sb(f"xh{i}", [128, 8, 256], R, c2) for i in range(2)])
        XL = [sb(f"xl{i}", [128, 8, 256], R, c2) for i in range(2)]
        PB = Slots([sb(f"pb{i}", [128, 2, 256], R, c2) for i in range(2)])
        PTT = Slots([sb(f"ptt{i}", [128, 2, 256], R, c2) for i in range(3)])
        GS = Slots([sb(f"gsl{i}", [128, 2], F, c2) for i in range(3)])
        HB = Slots([sb(f"hb{i}", [128, 512], F, c2) for i in range(2)])
        TT = Slots([sb(f"tth{i}", [128, 4, 128], R, c2) for i in range(2)])
        TTL = [sb(f"ttl{i}", [128, 4, 128], R, c2) for i in range(2)]
        YH, YL = sb("YH", [128, 1024], R, c2), sb("YL", [128, 1024], R, c2)
        YB = (banks[6], banks[7])
        ytok = PT.free[6] + PT.free[7]
        assert len(PT.order) == 8
        fb = PT.free
        PG, PT = Slots(banks[0:4]), Slots(banks[4:6])
        PG.free, PT.free = fb[0:4], fb[4:6]

        def gather(cols, rk, off, gate, m0):
            k_, pb, fp = PB.get()
            kt_, ptt, ft = PTT.get()
            kg_, gsl, fg = GS.get()
            tb = []
            for n in range(2):
                for tb_ in range(2):
                    rc = rk(n, tb_)
                    tb.append(dve.do(lambda e, n=n, tb_=tb_, rc=rc: e.tensor_scalar(
                        pb[:, tb_, n * 128:(n + 1) * 128], iota, rc, None, ALU.is_equal), fp, m0, t_mi, mfree))
            kx, xh, fx = XH.get()
            xl = XL[kx]
            tx = []
            for c in range(8):
                for (src, dst) in ((TH, xh), (TL, xl)):
                    if dst is xh:
                        b, bank, fr = PG.get()
                    o = bank[:, 0:256] if dst is xh else bank[:, 256:512]
                    for tb_ in range(2):
                        t = pe.do(lambda e, c=c, tb_=tb_, src=src, o=o: e.matmul(o, src[:, tb_, c * 128:(c + 1) * 128], pb[:, tb_, :],
                                                                                start=(tb_ == 0), stop=(tb_ == 1)), fr, tb, tok_t)
                t1 = act.do(lambda e, c=c, bank=bank: e.copy(xh[:, c, :], bank[:, 0:256]), t, fx, mfree)
                t2 = act.do(lambda e, c=c, bank=bank: e.copy(xl[:, c, :], bank[:, 256:512]), t)
                PG.put(b, t2)
                tx.append(t2)
            b, bank, fr = PT.get()
            for n in range(2):
                for tb_ in range(2):
                    t = pe.do(lambda e, n=n, tb_=tb_, bank=bank: e.transpose(
                        bank[:, n * 256 + tb_ * 128:n * 256 + tb_ * 128 + 128], pb[:, tb_, n * 128:(n + 1) * 128].bitcast(F), ident), fr, tb)
            t = act.do(lambda e, bank=bank: e.copy(ptt[:, :, :], bank[:, :].rearrange("p (n t) -> p n t", n=2)), t, ft, mfree)
            PT.put(b, t)
            b, bank, fr = PT.get()
            for n in range(2):
                for tb_ in range(2):
                    gc = gate(n, tb_)
                    tg = pe.do(lambda e, n=n, tb_=tb_, bank=bank, gc=gc: e.matmul(
                        bank[:, n:n + 1], pb[:, tb_, n * 128:(n + 1) * 128].bitcast(F), gc, start=(tb_ == 0), stop=(tb_ == 1)), fr, tb)
            PB.put(k_, tg)
            tg = dve.do(lambda e, bank=bank: e.tensor_copy(gsl[:, :], bank[:, 0:2]), tg, fg, mfree)
            PT.put(b, tg)
            return dict(kx=kx, xh=xh, xl=xl, tx=tx, kt=kt_, ptt=ptt, tp=t, kg=kg_, gsl=gsl, tg=tg)

        def up(G, n_in, tags):
            res = []
            for w in range(2):
                b, bank, fr = PG.get()
                pe.wait(fr, G["tx"])
                for k0 in range(2):
                    i, h, l, nk = take(tags[2 * w + k0])
                    for k in range(4):
                        kk = 4 * k0 + k
                        xs, ls = G["xh"][:, kk, n_in * 128:(n_in + 1) * 128], G["xl"][:, kk, n_in * 128:(n_in + 1) * 128]
                        for q, (x_, w_) in enumerate([(xs, h), (ls, h), (xs, l)]):
                            f = lambda e, x_=x_, w_=w_, k=k, kk=kk, q=q, bank=bank: e.matmul(
                                bank[:, :], x_, w_[:, k, :], start=(kk == 0 and q == 0), stop=(kk == 7 and q == 2))
                            if k == 3 and q == 2:
                                t = pe.do(f)
                            else:
                                pe.run(f)
                    done(i, t)
                res.append((b, bank, t))
            kh, hb, fh = HB.get()
            t1 = act.do(lambda e: e.activation(hb[:, :], res[0][1][:, :], ACT.Silu), res[0][2], fh, mfree)
            PG.put(res[0][0], t1)
            t2 = tt2(hb[:, :], res[1][1][:, :], hb[:, :], ALU.mult, t1, res[1][2])
            PG.put(res[1][0], t2)
            return kh, hb, t2

        def turn(kh, hb, th):
            b, bank, fr = PT.get()
            for j in range(4):
                t = pe.do(lambda e, j=j, bank=bank: e.transpose(bank[:, j * 128:(j + 1) * 128], hb[:, j * 128:(j + 1) * 128], ident), fr, th)
            HB.put(kh, t)
            kt, tt_, ft = TT.get()
            v = bank[:, :].rearrange("p (j t) -> p j t", j=4)
            rr = split(tt_[:, :, :], TTL[kt][:, :, :], v, t, [ft, mfree])
            PT.put(b, *rr)
            return kt, tt_, rr

        def down(kt, tt_, rr, n, tags, yfree):
            pe.wait(rr, yfree)
            for j in range(2):
                i, h, l, nk = take(tags[j])
                for k in range(2):
                    kk = 2 * j + k
                    for half in range(2):
                        for q, (x_, w_) in enumerate([(tt_, h), (TTL[kt], h), (tt_, l)]):
                            f = lambda e, x_=x_, w_=w_, k=k, kk=kk, q=q, half=half: e.matmul(
                                YB[half][:, :], x_[:, kk, :], w_[:, k, half * 512:(half + 1) * 512],
                                start=(n == 0 and kk == 0 and q == 0), stop=(n == 6 and kk == 3 and q == 2), skip_group_check=True)
                            if k == 1 and half == 1 and q == 2:
                                t = pe.do(f)
                            else:
                                pe.run(f)
                done(i, t)
            TT.put(kt, t)
            return t

        state = {"yfree": ytok, "ys": [], "mo": [t_mo]}

        def collect(G, n_in, t):
            gs = G["gsl"][:, n_in:n_in + 1]
            tl = []
            for half in range(2):
                sl = slice(half * 512, half * 512 + 512)
                th = act.do(lambda e, half=half, sl=sl: e.activation(YH[:, sl], YB[half][:, :], ACT.Copy, scale=gs), t, G["tg"], state["ys"], mfree)
                tl.append(dve.do(lambda e, half=half, sl=sl: e.scalar_tensor_tensor(
                    out=YL[:, sl], in0=YB[half][:, :], scalar=gs, in1=YH[:, sl].bitcast(F), op0=ALU.mult, op1=ALU.subtract), th, state["ys"], mfree))
            state["yfree"] = tl
            return tl + [th]

        def scatter(G, n_in, ty):
            for c in range(0, 8, 2):
                b, bank, fr = PG.get()
                for m in range(2):
                    for q, y in enumerate((YH, YL)):
                        t = pe.do(lambda e, c=c, m=m, q=q, y=y, bank=bank: e.matmul(
                            bank[:, m * S:(m + 1) * S], y[:, (c + m) * 128:(c + m + 1) * 128], G["ptt"][:, n_in, :],
                            start=(q == 0), stop=(q == 1)), fr, ty, G["tp"])
                tv = tt2(MO[:, c:c + 2, :], bank[:, :].rearrange("p (m t) -> p m t", m=2), MO[:, c:c + 2, :], ALU.add, t, state["mo"])
                PG.put(b, tv)
            state["ys"] = [t]
            return t

        def etags(e, n):
            return [(tag, e, n, k0) for tag in ("w1", "w3") for k0 in range(2)]

        def dtags(e, n):
            return [("w2", e, n, j) for j in range(2)]

        def run_experts(order, gathers, extra=False):
            prev = None
            late = None

            def finish_step(p):
                (e, n), (kt, tt_, rr) = p
                return down(kt, tt_, rr, n, dtags(e, n), state["yfree"] if n == 0 else None)
            for (e, n) in order:
                G = gathers[e // 2]
                h = up(G, e % 2, etags(e, n))
                if prev is not None:
                    (pe_, pn), t_ = prev
                    t = finish_step(prev)
                    if pn == 6:
                        Gp = gathers[pe_ // 2]
                        late = (Gp, pe_ % 2, collect(Gp, pe_ % 2, t), pe_)
                if n == 1 and late is not None:
                    t = scatter(*late[:3])
                    release(late, t, gathers)
                    late = None
                if n == 3 and e % 2 == 0 and e + 2 < NEXP and not extra:
                    gathers[e // 2 + 1] = gather(None, *gargs(e // 2 + 1))
                prev = ((e, n), turn(*h))
            t = finish_step(prev)
            (pe_, pn), _ = prev
            Gp = gathers[pe_ // 2]
            ty = collect(Gp, pe_ % 2, t)
            t = scatter(Gp, pe_ % 2, ty)
            release((Gp, pe_ % 2, ty, pe_), t, gathers)

        def release(late, t, gathers):
            G, n_in, _, e = late
            if e % 2 == 1:
                XH.put(G["kx"], pe.now())
                PTT.put(G["kt"], pe.now())
                GS.put(G["kg"], dve.now(), act.now())

        def gargs(p):
            return (lambda n, tb_: RK[:, tb_, 2 * p + n:2 * p + n + 1], 0,
                    lambda n, tb_: ro(tb_, 7)[:, 2 * p + n:2 * p + n + 1], tr + tm)
        gathers = {0: gather(None, *gargs(0))}
        run_experts(steps, gathers)

        for q in (pe, act, dve, pool, sp):
            q.wait(fence(), t_ci)
        main = (pe, act, dve)
        n_over = nc.values_load(CI[0:1, 0:1], min_val=0, max_val=3)
        pe, act, dve = (Queue(q.eng, sem("s_over_" + n)) for q, n in zip(main, ("pe", "act", "dve")))
        s_raw = [sem(f"s_over_raw{i}") for i in range(NR + NX)]
        plan, raw_free, where, used = [], {}, [], {}
        wide[0], nxt[0], first_moe[0] = [], 0, 0
        pos[0] = ahead[0] = gcount[0] = 0
        pair_free = [[] for _ in range(NP)]
        for ring in (PG, PT, XH, PB, PTT, GS, HB, TT):
            assert len(ring.order) == len(ring.bufs)
            ring.free = [[] for _ in ring.bufs]
        state = {"yfree": [], "ys": [], "mo": []}
        ovt = lambda n, tb_, j, o: OV[:, tb_, o + j:o + j + 1] if n == 0 else OV[:, tb_, 3:4]
        for j in range(3):
            with nc.If(n_over > j):
                ex = nc.sync.value_load(CI[0:1, 1 + j:2 + j], min_val=0, max_val=7)
                eu = [a[f"moe_w{w}_2"] for w in (1, 3)]
                for n in range(8):
                    if n < 7:
                        for tag, w in (("w1", eu[0]), ("w3", eu[1])):
                            for k0 in range(2):
                                src = w[0, bass.ds(ex, 1), k0 * 512:(k0 + 1) * 512, n * 512:(n + 1) * 512]
                                plan.append(("G", (tag, 0, n, k0), src.rearrange("a (k p) n -> p (a k) n", p=128), 4, 512))
                    if n:
                        for k0 in range(2):
                            r0 = (n - 1) * 512 + k0 * 256
                            src = a["moe_w2_2"][0, bass.ds(ex, 1), r0:r0 + 256, :]
                            plan.append(("G", ("w2", 0, n - 1, k0), src.rearrange("a (k p) n -> p (a k) n", p=128), 2, 1024))
                issue()
                G = gather(None, lambda n, tb_: ovt(n, tb_, j, 0), 0, lambda n, tb_: ovt(n, tb_, j, 4), None)
                run_experts([(0, n) for n in range(7)], {0: G}, extra=True)
                XH.put(G["kx"], pe.now())
                PTT.put(G["kt"], pe.now())
                GS.put(G["kg"], dve.now(), act.now())
                for q in (pe, act, dve, pool, sp):
                    q.wait([pe.now(), act.now(), dve.now()])
            for q in (pe, act, dve, pool, sp):
                q.eng.wait_ge(t_ci[0], t_ci[1])
        pe, act, dve = main
        for ring in (PG, PT, SQ, RS):
            ring.free = [[] for _ in ring.bufs]

        xst, tx = Stats(), []
        for c in range(8):
            tx.append(dve.do(lambda e, c=c: e.scalar_tensor_tensor(out=X[:, c, :], in0=MO[:, c, :], scalar=modT[3][:, 40 + c:41 + c],
                                                                   in1=X[:, c, :], op0=ALU.mult, op1=ALU.add), dve.now(), mod_tok[3, 11]))
            if c % 2:
                xst.add(X[:, c - 1:c + 1, :], tx[c])
        xrs = xst.close(D)
        fin = norm_full(X, xrs, vec("fing"), vec_tok, None, None, tx, None)
        c2.close()
        x_tok = fin
        return finish(locals())


def finish(v):
    nc, pe, act, dve, pool, sp = (v[k] for k in ("nc", "pe", "act", "dve", "pool", "sp"))
    PT, X, ident, load, fence, out = (v[k] for k in ("PT", "X", "ident", "load", "fence", "out"))
    f = fence()
    c = ExitStack()
    o = v["sb"]("onat", [128, 2, 1024], F, c)
    with c:
        toks = []
        for tb in range(2):
            for c4 in range(0, 8, 4):
                b, bank, fr = PT.get()
                for j in range(4):
                    t = pe.do(lambda e, j=j, c4=c4, tb=tb, bank=bank: e.transpose(
                        bank[:, j * 128:(j + 1) * 128], X[:, c4 + j, tb * 128:tb * 128 + 128], ident), fr, v["x_tok"])
                t = dve.do(lambda e, tb=tb, c4=c4, bank=bank: e.tensor_copy(o[:, tb, c4 * 128:c4 * 128 + 512], bank[:, :]), t, f)
                PT.put(b, t)
                toks.append(t)
        t_out = load("out", [(out[0, tb * 128:(tb + 1) * 128, :], o[:, tb, :]) for tb in range(2)], toks, q=sp)
        sp.wait(t_out)


_USED = ["x", "c", "w_mod", "b_mod", "norm_mix", "norm_ffn", "w_in", "qnorm_a", "knorm_a", "sinks", "rnn_conv_w",
         "rnn_conv_b", "rnn_gate_a_w", "rnn_gate_a_b", "rnn_gate_x_w", "rnn_gate_x_b", "rnn_lambda", "qnorm_c",
         "knorm_c", "rel_bias", "w_branch", "w_out", "w_up", "ffn_conv_w", "ffn_conv_b", "w_down", "c_2", "ctx_2",
         "c_ctx_2", "ada_w_2", "ada_b_2", "norm1_g_2", "norm2_g_2", "attn_w_qkv_2", "attn_lq1_2", "attn_lk1_2",
         "attn_lq2_2", "attn_lk2_2", "attn_subln_g_2", "attn_w_o_2", "fnet_w_o_2", "fnet_b_o_2", "ff_w1_2",
         "ff_w3_2", "ff_w2_2", "moe_router_2", "moe_w1_2", "moe_w3_2", "moe_w2_2", "final_g_2"]


def kernel(**inputs):
    import concourse.bacc as bacc
    from concourse.bass_utils import run_bass_kernel_spmd

    nc = bacc.Bacc("TRN2", target_bir_lowering=False, num_devices=1)
    arrays, aps = {}, {}
    for name in _USED:
        v = np.ascontiguousarray(inputs[name])
        arrays[f"in_{name}"] = v
        aps[name] = nc.dram_tensor(f"in_{name}", v.shape, mybir.dt.from_np(v.dtype), kind="ExternalInput").ap()
    v = constants()
    arrays["in_consts"] = v
    aps["consts"] = nc.dram_tensor("in_consts", v.shape, F, kind="ExternalInput").ap()
    out = nc.dram_tensor("out_0", (1, S, D), F, kind="ExternalOutput").ap()
    build(nc, aps, out)
    r = run_bass_kernel_spmd(nc, [arrays], core_ids=[0])
    return r.results[0]["out_0"]
```

```python
import math
from contextlib import ExitStack

import numpy as np
import concourse.bass as bass
from concourse import mybir
from concourse.alu_op_type import AluOpType as ALU

F = mybir.dt.float32
R = mybir.dt.float32r
I32 = mybir.dt.int32
ACT = mybir.ActivationFunctionType
AX = mybir.AxisListType.X

D = 1024
S = 256
EPS = 1e-6
NEG = -1e30
D_IN = 7424
FF1 = 2816
FF2 = 3584
NEXP = 8

NR = 4
NX = 2
NP = 3
LOOK = 2
CAP = 128

C_ID, C_BO, C_J, C_ROT = 0, 128, 256, 512
C_COS, C_SIN, C_FD, C_FL = 640, 896, 1152, 1408
C_OHA, C_OHC, C_TRI, C_IOTA, C_EIDX, C_ONE = 2432, 2816, 3200, 3328, 3456, 3464
C_END = 3592


def t5_bucket(d):
    d = max(d, 0)
    if d < 16:
        return d
    f = np.float32
    lr = np.log(f(d) / f(16)) / f(math.log(2048 / 16))
    return min(16 + int(f(lr * f(16))), 31)


def constants():
    c = np.zeros((128, C_END), np.float32)
    p = np.arange(128)
    c[:, C_ID:C_ID + 128] = np.eye(128)
    c[:, C_BO:C_BO + 128] = (p[:, None] // 64 == p[None, :] // 64)
    for m in range(128):
        half = (m // 16) % 2
        c[m + 16 if half == 0 else m - 16, C_ROT + m] = -1.0 if half == 0 else 1.0
    tok = np.arange(S, dtype=np.float32)
    row, col = np.floor(tok / 64), np.mod(tok, 64)
    freqs = (np.float32(10000.0) ** (-np.arange(16, dtype=np.float32) / np.float32(16))).astype(np.float32)
    for m in range(128):
        d = m % 64
        ang = (row if d < 32 else col) * freqs[d % 16]
        c[m, C_COS:C_COS + S] = np.cos(ang.astype(np.float32))
        c[m, C_SIN:C_SIN + S] = np.sin(ang.astype(np.float32))
    w = 2 * np.pi * np.outer(p, p) / 128
    c[:, C_FD:C_FD + 128] = np.cos(w) / math.sqrt(128)
    c[:, C_FD + 128:C_FD + 256] = np.sin(w) / math.sqrt(128)
    for tb in range(2):
        w = 2 * np.pi * np.outer(p + 128 * tb, np.arange(S)) / S
        c[:, C_FL + tb * 512:C_FL + tb * 512 + 256] = np.cos(w) / math.sqrt(S)
        c[:, C_FL + tb * 512 + 256:C_FL + tb * 512 + 512] = -np.sin(w) / math.sqrt(S)
    for t in range(384):
        diff = 255 - t
        b = t5_bucket(diff)
        c[b, C_OHA + t] = 1.0
        c[b, C_OHC + t] = 1.0
        c[32, C_OHA + t] = 0.0 if 0 <= diff < 128 else NEG
        c[32, C_OHC + t] = 0.0 if diff >= 0 else NEG
    c[:, C_TRI:C_TRI + 128] = (p[:, None] < p[None, :])
    c[:, C_IOTA:C_IOTA + 128] = p[None, :]
    c[:, C_EIDX:C_EIDX + 8] = 8 - np.arange(8)
    c[:, C_ONE:C_ONE + 128] = 1.0
    c[:, C_J:C_J + 128] = np.eye(128)[::-1]
    return c


class Queue:

    def __init__(self, eng, sem):
        self.eng, self.sem, self.n, self.seen = eng, sem, 0, {}

    def wait(self, *toks):
        for t in toks:
            if t is None:
                continue
            if isinstance(t, list):
                self.wait(*t)
                continue
            sem, val = t
            if self.seen.get(id(sem), 0) < val:
                self.seen[id(sem)] = val
                self.eng.wait_ge(sem, val)

    def do(self, fn, *toks):
        self.wait(*toks)
        self.n += 1
        fn(self.eng).then_inc(self.sem, 1)
        return (self.sem, self.n)

    def run(self, fn, *toks):
        self.wait(*toks)
        fn(self.eng)

    def now(self):
        return (self.sem, self.n)


class Chunks(list):
    pass


class Slots:

    pump = None

    def __init__(self, bufs):
        self.bufs, self.free, self.order = bufs, [[] for _ in bufs], list(range(len(bufs)))

    def busy(self):
        return not self.order

    def get(self):
        while self.busy() and Slots.pump():
            pass
        assert self.order, "every slot is in use"
        k = self.order.pop(0)
        return k, self.bufs[k], self.free[k]

    def put(self, k, *toks):
        assert k not in self.order
        self.free[k] = list(toks)
        self.order.append(k)


def build(nc, a, out):
    ctx = ExitStack()

    def sb(name, shape, dt=F, c=ctx):
        return c.enter_context(nc.sbuf_tensor(name, shape, dt))

    def sem(name):
        return ctx.enter_context(nc.semaphore(name))

    with ctx:
        pe, act, dve, pool, sp = (Queue(g, sem("s_" + n)) for n, g in (
            ("pe", nc.tensor), ("act", nc.scalar), ("dve", nc.vector), ("pool", nc.gpsimd), ("sp", nc.sync)))

        def fence():
            return [pe.now(), act.now(), dve.now(), pool.now()]

        raw = [sb(f"raw{i}", [128, 2048]) for i in range(NR)]
        whi = [sb(f"whi{i}", [128, 2048], R) for i in range(NP)]
        wlo = [sb(f"wlo{i}", [128, 2048], R) for i in range(NP)]
        X = sb("X", [128, 8, S])
        cst = sb("cst", [128, 384])
        one = sb("one", [128, 128])
        vt = [sb(f"vt{i}", [128, 128]) for i in range(4)]
        modT = [sb("mod_m", [128, 48]), sb("mod_a0", [128, 48]), sb("mod_c0", [128, 16]), sb("mod_a1", [128, 48])]
        macc = [sb(f"macc{i}", [128, 512]) for i in range(4)]
        eps_c = sb("eps_c", [128, 1])
        csil = sb("csil", [128, 24])
        nA = sb("nA", [128, 64])
        sqb = [sb(f"sqb{i}", [128, 512]) for i in range(3)]
        rst = [sb(f"rst{i}", [128, 512]) for i in range(2)]
        banks = [ctx.enter_context(nc.psum_tensor(f"bk{i}", [128, 512], F)) for i in range(8)]
        PG = PT = Slots(banks)
        MA = Slots(macc)
        SQ = Slots(sqb)
        RS = Slots(rst)
        s_raw = [sem(f"s_raw{i}") for i in range(NR + NX)]
        ident, bones, JJ = cst[:, C_ID:C_ID + 128], cst[:, C_BO:C_BO + 128], cst[:, C_J:C_J + 128]

        dma_sems = {}

        def load(name, pairs, *toks, q=pool):
            s = dma_sems.setdefault(name, [None, 0])
            if s[0] is None:
                s[0] = sem("d_" + name)
            q.wait(*toks)
            for o, i in pairs:
                s[1] += 16
                q.eng.dma_start(o, i).then_inc(s[0], 16)
            return (s[0], s[1])

        plan = []

        def gslabs(w, kts, c0, tag):
            r = []
            for k0 in range(0, kts, 8):
                nk = min(8, kts - k0)
                src = w[k0 * 128:(k0 + nk) * 128, c0:c0 + 256].rearrange("(k p) n -> p k n", p=128)
                r.append(("G", tag, src, nk, 256))
            return r

        def mslabs(w, g, which):
            return [("M", (which, g, k0), w[k0 * 512:(k0 + 1) * 512, g * 512:(g + 1) * 512]
                     .rearrange("(k p) n -> p k n", p=128), 4, 512) for k0 in range(2)]

        def mix(gs, ms):
            o, j = [], 0
            for i, g in enumerate(gs):
                o.append(g)
                while j < len(ms) and j < (i + 1) * len(ms) / len(gs):
                    o.append(ms[j])
                    j += 1
            return o + ms[j:]

        wmod, ada = a["w_mod"][0], a["ada_w_2"]
        win, wbr, wout, wup, wdn = a["w_in"][0], a["w_branch"][0], a["w_out"][0], a["w_up"][0], a["w_down"][0]
        wqkv, wo2, fwo = a["attn_w_qkv_2"][0], a["attn_w_o_2"][0], a["fnet_w_o_2"][0]
        f1, f3, f2 = a["ff_w1_2"][0], a["ff_w3_2"][0], a["ff_w2_2"][0]
        z_cols = [0, 256, 512, 2816, 3072, 3328, 3584, 3840, 4096]
        for j in range(4):
            z_cols += [768 + 256 * j, 1792 + 256 * j]
        gcols = lambda cs: [4352 + 1024 * g + 256 * c for c in cs for g in range(3)]
        zs = lambda cols: [s for c in cols for s in gslabs(win, 8, c, ("z", c))]
        m0 = [s for g in range(4, 12) for s in mslabs(wmod, g, 0)]
        m1 = [s for g in range(12) for s in mslabs(ada[0], g, 1)]
        m3 = [s for g in range(12) for s in mslabs(ada[1], g, 3)]
        for g in (0, 1, 2, 3):
            plan += mslabs(wmod, g, 0)
        plan += mix(zs(z_cols[:9]), m0[:8])
        plan += mix(zs(z_cols[9:] + gcols((0, 1))), m0[8:])
        bs = [s for c in range(4) for s in gslabs(wbr, 16, 256 * c, ("br", c))]
        bs += [s for c in range(4) for s in gslabs(wout, 8, 256 * c, ("out", c))]
        plan += mix(zs(gcols((2, 3))) + bs[:-2], m1[:4]) + bs[-2:]
        us = [s for c in range(11) for s in gslabs(wup, 8, 256 * c, ("ug", c)) + gslabs(wup, 8, FF1 + 256 * c, ("uv", c))]
        ds_ = [s for c in range(4) for s in gslabs(wdn, 22, 256 * c, ("dn", c))]
        plan += mix(us, m1[4:6])
        plan += m1[6:8] + mix(ds_, m1[8:12])
        q2 = [s for c in range(4) for j in (4 + c, c, 8 + c) for s in gslabs(wqkv, 8, 256 * j, ("qkv", j))]
        q2 += [s for c in range(4) for s in gslabs(wo2, 8, 256 * c, ("wo", c))]
        plan += mix(q2, m1[12:] + m3[:4])
        ff = [s for c in range(14) for s in gslabs(f1, 8, 256 * c, ("f1", c)) + gslabs(f3, 8, 256 * c, ("f3", c))]
        ff += [s for c in range(4) for s in gslabs(f2, 28, 256 * c, ("f2", c))]
        plan += mix(ff, m3[4:])
        plan += [s for c in range(4) for s in gslabs(fwo, 8, 256 * c, ("fn", c))]
        first_moe = [len(plan)]

        def eslabs(e, n):
            r = []
            for tag, w in (("w1", a["moe_w1_2"][0, e]), ("w3", a["moe_w3_2"][0, e])):
                for k0 in range(2):
                    r.append(("G", (tag, e, n, k0), w[k0 * 512:(k0 + 1) * 512, n * 512:(n + 1) * 512]
                              .rearrange("(k p) n -> p k n", p=128), 4, 512))
            return r

        def dslabs(e, n):
            w = a["moe_w2_2"][0, e]
            return [("G", ("w2", e, n, j), w[n * 512 + j * 256:n * 512 + (j + 1) * 256, :]
                     .rearrange("(k p) n -> p k n", p=128), 2, 1024) for j in range(2)]

        steps = [(e, n) for e in range(NEXP) for n in range(7)]
        for i, (e, n) in enumerate(steps):
            plan += eslabs(e, n)
            if i:
                plan += dslabs(*steps[i - 1])
        plan += dslabs(*steps[-1])

        where, used, wide, nxt, raw_free = [], {}, [None], [0], {}

        def place(i):
            while len(where) <= i:
                j = len(where)
                s = j % NR if j < first_moe[0] else (j - first_moe[0]) % (NR + NX)
                if j >= first_moe[0] and s < NR:
                    s = (s + first_moe[0]) % NR
                c, p = used.get(s, (0, None))
                where.append((s, c + 1, p))
                used[s] = (c + 1, j)
            return where[i]

        def raw_view(i):
            _, _, src, nk, nc_ = plan[i]
            return raw[place(i)[0]][:, :nk * nc_].rearrange("p (k n) -> p k n", k=nk)

        def issue():
            while nxt[0] < len(plan):
                i = nxt[0]
                s, _, p = place(i)
                if (s >= NR and wide[0] is None) or (p is not None and p not in raw_free):
                    return
                sp.wait(raw_free[p] if p is not None else (wide[0] if s >= NR else None))
                sp.eng.dma_start(raw_view(i), plan[i][2]).then_inc(s_raw[s], 16)
                nxt[0] += 1

        def arrived(i):
            s, c, _ = place(i)
            return (s_raw[s], 16 * c)

        pair_free = [[] for _ in range(NP)]
        pair_of, gcount, taken = {}, [0], [0]
        pair_tok = {}
        pos, ahead = [0], [0]
        mstate = {}

        lows, moe = [], [False]

        def flush_lows():
            while lows:
                lows.pop(0)()

        def prepare(i):
            kind, tag, src, nk, w = plan[i]
            if nxt[0] <= i:
                flush_lows()
                assert nxt[0] > i
            if kind == "G":
                k = gcount[0] % NP
                gcount[0] += 1
                assert pair_free[k] is not None
                n = nk * w
                r, h, l = raw[place(i)[0]][:, :n], whi[k][:, :n], wlo[k][:, :n]
                th = act.do(lambda e: e.copy(h, r), arrived(i), pair_free[k])
                pf, pair_free[k] = pair_free[k], None
                pair_of[i] = k

                def low():
                    tl = dve.do(lambda e: e.tensor_tensor(l, r, h.bitcast(F), ALU.subtract), arrived(i), th, pf)
                    pair_tok[i] = raw_free[i] = [th, tl]
                    issue()
                lows.append(low)
                if moe[0]:
                    flush_lows()
                return
            else:
                which, g, k0 = tag
                v = raw_view(i)
                cs = [(which, {0: 0, 1: 8, 3: 8}[which])]
                if which == 1 and g < 4:
                    cs.append((2, 16))
                toks = []
                for dest, c0 in cs:
                    if k0 == 0:
                        kk, acc, fr = MA.get()
                        mstate[dest, g] = [kk, acc, fr]
                    kk, acc, t = mstate[dest, g]
                    for j in range(4):
                        sc = csil[:, c0 + k0 * 4 + j:c0 + k0 * 4 + j + 1]
                        if k0 == 0 and j == 0:
                            t = dve.do(lambda e, sc=sc, acc=acc: e.tensor_scalar(acc[:, :], v[:, 0, :], sc, None, ALU.mult),
                                       arrived(i), t, csil_tok)
                        else:
                            t = dve.do(lambda e, sc=sc, acc=acc, j=j: e.scalar_tensor_tensor(
                                out=acc[:, :], in0=v[:, j, :], scalar=sc, in1=acc[:, :], op0=ALU.mult, op1=ALU.add),
                                arrived(i), t)
                    mstate[dest, g][2] = t
                    toks.append(t)
                raw_free[i] = toks
            issue()

        mod_tok = {}

        def reduce_mod(i):
            which, g, k0 = plan[i][1]
            if k0 == 0:
                return
            for dest in [which] + ([2] if which == 1 and g < 4 else []):
                kk, acc, t = mstate.pop((dest, g))
                b, bank, fr = PT.get()
                for j in range(4):
                    f = lambda e, j=j, acc=acc, bank=bank: e.matmul(bank[:, j:j + 1], acc[:, j * 128:(j + 1) * 128],
                                                                    one[:, 0:1], start=True, stop=True)
                    if j < 3:
                        pe.run(f, t, fr, t_c)
                    else:
                        tp = pe.do(f)
                MA.put(kk, tp)
                bias = {0: vec("b_mod"), 1: vec("ada_b0"), 2: vec("ada_b0"), 3: vec("ada_b1")}[dest]
                td = dve.do(lambda e, g=g, bank=bank, dest=dest: e.tensor_tensor(
                    modT[dest][:, 4 * g:4 * g + 4], bank[:, 0:4], bias[:, 4 * g:4 * g + 4], ALU.add), tp, vec_tok)
                PT.put(b, td)
                mod_tok[dest, g] = td

        def advance(n):
            while ahead[0] < min(n, len(plan)):
                prepare(ahead[0])
                ahead[0] += 1


        def look_ahead():
            while ahead[0] < len(plan) and gcount[0] - taken[0] < LOOK:
                kind, tag = plan[ahead[0]][:2]
                if kind == "M" and tag[2] == 0 and len(MA.order) < 2:
                    return
                prepare(ahead[0])
                ahead[0] += 1

        def skip_mods():
            while pos[0] < len(plan) and plan[pos[0]][0] == "M":
                advance(pos[0] + 1)
                look_ahead()
                reduce_mod(pos[0])
                pos[0] += 1

        def take(tag):
            skip_mods()
            i = pos[0]
            assert plan[i][1] == tag, (plan[i][1], tag)
            advance(i + 1)
            if i not in pair_tok:
                flush_lows()
            k = pair_of[i]
            taken[0] += 1
            pe.wait(pair_tok[i])
            nk, w = plan[i][3], plan[i][4]
            h = whi[k][:, :nk * w].rearrange("p (k n) -> p k n", k=nk)
            l = wlo[k][:, :nk * w].rearrange("p (k n) -> p k n", k=nk)
            pos[0] += 1
            return i, h, l, nk

        def done(i, tok):
            pair_free[pair_of[i]] = [tok]
            look_ahead()
            skip_mods()

        live, pending, urgent = [], [], []
        LIMIT = [2]

        running = [False]

        def pump():
            if running[0] or not (live or pending or urgent):
                return False
            tick()
            return True

        Slots.pump = pump

        def tick():
            flush_lows()
            running[0] = True
            for g in list(urgent):
                try:
                    next(g)
                except StopIteration:
                    urgent.remove(g)
            step()
            running[0] = False

        RATE = [2]

        def step():
            while pending and len(live) < LIMIT[0]:
                live.append(pending.pop(0))
            for _ in range(min(RATE[0], len(live))):
                g = live.pop(0)
                try:
                    next(g)
                    live.append(g)
                except StopIteration:
                    pass
                while pending and len(live) < LIMIT[0]:
                    live.append(pending.pop(0))

        def drain():
            while live or pending or urgent:
                tick()

        def now(g):
            for _ in g:
                pass

        def step_wait(xt, kk):
            if isinstance(xt, Chunks):
                while xt[kk] is None:
                    tick()
                pe.wait(xt[kk])

        def gemmT(tags_kts, xh, xl, xt, evac, two=None, keep=False):
            k_all = sum(k for _, k in tags_kts)
            if not isinstance(xt, Chunks):
                pe.wait(xt)
            b, bank, fr = PG.get()
            pe.wait(fr)
            if two:
                b2, bank2, fr2 = PG.get()
                pe.wait(fr2)
                jobs = [(two[0], two[1], two[2], m, (bank, bank2)[m][:, 0:S], True) for m in range(2)]
                jobs += [(xh, xl, xt, m, (bank, bank2)[m][:, S:512], False) for m in range(2)]
            else:
                jobs = [(xh, xl, xt, m, bank[:, m * S:(m + 1) * S], m == 0) for m in range(2)]
            kb = 0
            for n_, (tag, _) in enumerate(tags_kts):
                i, h, l, nk = take(tag)
                for n, (hi, lo, tk, m, o, first) in enumerate(jobs):
                    for k in range(nk):
                        kk = kb + k
                        step_wait(tk, kk)
                        for q, (w, xx) in enumerate([(h, hi), (h, lo), (l, hi)]):
                            st = kk == 0 and q == 0 and first
                            sp_ = kk == k_all - 1 and q == 2
                            f = lambda e, w=w, xx=xx, k=k, kk=kk, m=m, st=st, sp_=sp_, o=o: e.matmul(
                                o, w[:, k, m * 128:(m + 1) * 128], xx[:, kk, :], start=st, stop=sp_,
                                skip_group_check=True)
                            if n == len(jobs) - 1 and k == nk - 1 and q == 2:
                                t = pe.do(f)
                            else:
                                pe.run(f)
                    if n < len(jobs) - 1:
                        tick()
                kb += nk
                done(i, t)
                if n_ < len(tags_kts) - 1:
                    tick()
            if two:
                r1, r2 = evac((bank, bank2), t)
                PG.put(b, *r1)
                PG.put(b2, *r2)
            else:
                if keep:
                    evac(bank, t, b)
                else:
                    PG.put(b, *evac(bank, t))
            tick()

        vrows = {}
        vlist = [[("norm_mix", a["norm_mix"], 8), ("norm_ffn", a["norm_ffn"], 8), ("b_mod", a["b_mod"], 48),
                  ("rcb", a["rnn_conv_b"], 8), ("rcw", a["rnn_conv_w"], 32), ("gab", a["rnn_gate_a_b"], 8),
                  ("gxb", a["rnn_gate_x_b"], 8), ("lam", a["rnn_lambda"], 8)],
                 [("ada_b0", a["ada_b_2"][0:1], 48), ("ada_b1", a["ada_b_2"][1:2], 48),
                  ("n10", a["norm1_g_2"][0:1], 8), ("n11", a["norm1_g_2"][1:2], 8),
                  ("n20", a["norm2_g_2"][0:1], 8), ("n21", a["norm2_g_2"][1:2], 8)],
                 [("fcw01", a["ffn_conv_w"][:, 0:2, :], 88), ("fbo", a["fnet_b_o_2"], 8),
                  ("fing", a["final_g_2"].rearrange("(o d) -> o d", o=1), 8)],
                 [("fcw2", a["ffn_conv_w"][:, 2:3, :], 44), ("fcb", a["ffn_conv_b"], 44), ("sub", a["attn_subln_g_2"], 1),
                  ("qa", a["qnorm_a"], 0), ("ka", a["knorm_a"], 0), ("qc", a["qnorm_c"], 0), ("kc", a["knorm_c"], 0)]]

        def split(dst_h, dst_l, src, toks, wfree=None):
            th = act.do(lambda e: e.copy(dst_h, src), toks, wfree)
            return [th, dve.do(lambda e: e.tensor_tensor(dst_l, src, dst_h.bitcast(F), ALU.subtract), toks, wfree, th)]

        def split_later(toks, c, hh, hl, src, t, wf):
            hi, lo = hh[:, 2 * c:2 * c + 2, :], hl[:, 2 * c:2 * c + 2, :]
            th = act.do(lambda e: e.copy(hi, src), t, wf)
            yield
            tl = dve.do(lambda e: e.tensor_tensor(lo, src, hi.bitcast(F), ALU.subtract), t, wf, th)
            toks[2 * c] = toks[2 * c + 1] = [th, tl]

        def coeff(col, g, scale, mt):
            o = nA[:, col:col + 8]
            return o, dve.do(lambda e: e.scalar_tensor_tensor(out=o, in0=scale, scalar=1.0, in1=g, op0=ALU.add, op1=ALU.mult), mt, vec_tok)

        def modulate(*args):
            toks = Chunks()
            now(modulate_steps(toks, *args))
            return toks

        def modulate_steps(toks, x, rs, xtoks, A, At, shift, st, hh, hl, wfree):
            k, r, tr = rs
            r_ = r[:, 0:S]
            q = []

            def low(c, kt, tt, t2s):
                for m, t2 in enumerate(t2s):
                    t3 = dve.do(lambda e, m=m: e.scalar_tensor_tensor(
                        out=hl[:, c + m, :], in0=tt[:, m * S:(m + 1) * S], scalar=shift[:, c + m:c + m + 1],
                        in1=hh[:, c + m, :].bitcast(F), op0=ALU.add, op1=ALU.subtract), t2, wfree)
                    toks.append([t2, t3])
                SQ.put(kt, t3)
            for c in range(0, 8, 2):
                while running[0] and SQ.busy():
                    yield
                kt, tt, ft = SQ.get()
                t2s = []
                for m in range(2):
                    t1 = dve.do(lambda e, c=c, tt=tt, m=m: e.scalar_tensor_tensor(
                        out=tt[:, m * S:(m + 1) * S], in0=x[:, c + m, :], scalar=A[:, c + m:c + m + 1],
                        in1=r_, op0=ALU.mult, op1=ALU.mult), tr, At, ft, xtoks)
                    t2s.append(act.do(lambda e, c=c, tt=tt, m=m: e.activation(
                        hh[:, c + m, :], tt[:, m * S:(m + 1) * S], ACT.Identity, bias=shift[:, c + m:c + m + 1]), t1, st, wfree))
                q.append((c, kt, tt, t2s))
                yield
                if len(q) > 1:
                    low(*q.pop(0))
            low(*q.pop(0))
            RS.put(k, t1)

        c1 = ctx.enter_context(ExitStack())
        HH, HL = sb("HH", [128, 8, S], R, c1), sb("HL", [128, 8, S], R, c1)
        with ExitStack() as c0:
            vn = [sb(f"vn{i}", [128, 128], F, c0) for i in range(4)]
            rnat = sb("rnat", [64, 16], F, c0)
            rows = sb("rrow", [16, 384], F, c0)
            oh = sb("oh", [64, 768], F, c0)
            bias_dram = nc.dram_tensor("bias_rows", (16, 384), F, kind="Internal")
            crow = sb("crow", [24, 128], F, c0)
            t_cr = load("crow", [(crow[8 * n:8 * n + 8, :], ap) for n, ap in enumerate((
                a["c"].rearrange("o (n p) -> (o n) p", p=128), a["c_2"].rearrange("o (n p) -> (o n) p", p=128),
                a["c_ctx_2"].rearrange("(n p) -> n p", p=128)))], q=sp)
            t_c = load("cst", [(cst[:, :], a["consts"][:, 0:384]), (one[:, :], a["consts"][:, C_ONE:C_ONE + 128])], q=act)
            issue()
            b, bank, fr = PT.get()
            t = pe.do(lambda e: e.transpose(bank[:, 0:24], crow[:, :], ident[0:24, 0:24]), t_cr, t_c)
            pairs, npair = [], []
            t_ms = [dve.do(lambda e, i=i: e.memset(vn[i][:, :], 0.0)) for i in range(4)]
            for ti, vl in enumerate(vlist):
                r0 = 0
                for name, ap, n in vl:
                    vrows[name] = (ti, r0, max(n, 1))
                    if n == 0:
                        for hh_ in range(2):
                            pairs.append((vn[ti][r0:r0 + 1, hh_ * 64:hh_ * 64 + 64], ap))
                        r0 += 1
                        continue
                    flat = ap
                    while len(flat.shape) > 2:
                        flat = flat.rearrange("a b c -> a (b c)")
                    pairs.append((vn[ti][r0:r0 + n, :], flat.rearrange("o (n p) -> (o n) p", p=128)))
                    r0 += n
                assert r0 <= 128
                npair.append(len(pairs))
            csil_tok = act.do(lambda e: e.activation(csil[:, :], bank[:, 0:24], ACT.Silu), t)
            PT.put(b, csil_tok)
            t_v = load("vec", pairs[:npair[0]], t_ms, q=act)
            t_v1 = load("vec1", pairs[npair[0]:npair[1]], t_ms)
            xn = sb("xn", [128, 2, 1024], F, c0)
            t_x = load("xn", [(xn[:, tb_, :], a["x"][0, tb_ * 128:(tb_ + 1) * 128, :]) for tb_ in range(2)], q=act)
            t_v2 = load("vec2", pairs[npair[1]:], t_ms)
            t_r = load("rel", [(rnat[0:32, :], a["rel_bias"]), (oh[0:33, :], a["consts"][0:33, C_OHA:C_OHA + 768])])
            t_r1 = pool.do(lambda e: e.memset(rnat[32:64, :], 1.0))
            t_eps = dve.do(lambda e: e.memset(eps_c[:, :], EPS))

            def vec(name):
                ti, r0, n = vrows[name]
                return vt[ti][:, r0:r0 + n]

            x_tok = []

            def transpose_in(src, t_src, dst, toks=()):
                r = Chunks()
                for c in range(0, 8, 2):
                    b, bank, fr = PT.get()
                    for m in range(2):
                        for tb_ in range(2):
                            t = pe.do(lambda e, m=m, tb_=tb_, c=c, bank=bank: e.transpose(
                                bank[:, m * 256 + tb_ * 128:m * 256 + tb_ * 128 + 128],
                                src[:, tb_, (c + m) * 128:(c + m + 1) * 128], ident), fr, t_src, t_c)
                    tt = act.do(lambda e, c=c, bank=bank: e.copy(
                        dst[:, c:c + 2, :], bank[:, :].rearrange("p (m t) -> p m t", m=2)), t, *toks)
                    PT.put(b, tt)
                    r += [[tt], [tt]]
                    yield r

            class Stats:

                def __init__(self):
                    self.b, self.bank, self.fr = PT.get()
                    self.n, self.q, self.late = 0, [], []

                def flush(self, last=False):
                    k, sq, t = self.q.pop(0)
                    for m in range(2):
                        st, sp_ = self.n == 0 and m == 0, last and m == 1
                        t = pe.do(lambda e, m=m, st=st, sp_=sp_, sq=sq: e.matmul(self.bank[:, 0:S], one[:, :], sq[:, m * S:(m + 1) * S],
                                                                          start=st, stop=sp_), t, self.fr, t_c)
                    SQ.put(k, t)
                    self.n += 1
                    return t

                def add(self, src, toks):
                    if len(self.q) > 1:
                        self.flush()
                    k, sq, fs = SQ.get()
                    t = act.do(lambda e: e.activation(sq[:, :].rearrange("p (m t) -> p m t", m=2), src, ACT.Square), toks, fs)
                    self.q.append((k, sq, t))

                def later(self, src, toks):
                    def g():
                        yield
                        self.late.pop(0)()
                    self.late.append(lambda: self.add(src, toks))
                    urgent.append(g())

                def close(self, width):
                    while self.late:
                        tick()
                    while self.q:
                        t = self.flush(len(self.q) == 1)
                    k, r, fr = RS.get()
                    t = act.do(lambda e: e.activation(r[:, 0:S], self.bank[:, 0:S], ACT.Ln, bias=eps_c[:, 0:1], scale=1.0 / width), t, fr, t_eps)
                    PT.put(self.b, t)
                    return k, r, act.do(lambda e: e.activation(r[:, 0:S], r[:, 0:S], ACT.Exp, scale=-0.5), t)

            xst = Stats()
            for r in transpose_in(xn, t_x, X):
                c = len(r) - 2
                xst.add(X[:, c:c + 2, :], r[-1])
            x_tok = r
            xrs = xst.close(D)

            def vec_tiles(tiles):
                b, bank, fr = PT.get()
                for i, tl in tiles:
                    t = pe.do(lambda e, i=i: e.transpose(bank[:, i * 128:(i + 1) * 128], vn[i][:, :], ident), fr, tl, t_c)
                for i, _ in tiles:
                    t1 = act.do(lambda e, i=i: e.copy(vt[i][:, :], bank[:, i * 128:(i + 1) * 128]), t)
                PT.put(b, t1)
                return t1
            vec_tok = vec_tiles([(0, t_v)])
            skip_mods()
            A0, At0 = coeff(0, vec("norm_mix"), modT[0][:, 8:16], mod_tok[0, 3])
            h_tok = modulate(X, xrs, x_tok, A0, At0, modT[0][:, 0:8], mod_tok[0, 1], HH, HL, None)
            held = []
            for j in range(2):
                gemmT([(("z", 256 * j), 8)], HH, HL, h_tok, lambda *x: held.append(x), keep=True)
            vec_tok = vec_tiles([(1, t_v1), (2, t_v2), (3, t_v2)])
            b, bank, fr = PT.get()
            b2, bank2, fr2 = PT.get()
            t1 = pe.do(lambda e: e.matmul(bank[0:16, 0:384], rnat[0:33, :], oh[0:33, 0:384], start=True, stop=True),
                       fr, t_r, t_r1)
            t2 = pe.do(lambda e: e.matmul(bank2[0:16, 0:384], rnat[0:33, :], oh[0:33, 384:768], start=True, stop=True), fr2)
            rows2 = sb("rrow2", [16, 384], F, c0)
            ta = act.do(lambda e: e.activation(rows[:, :], bank[0:16, 0:384], ACT.Copy, scale=8.0), t1)
            tb = act.do(lambda e: e.activation(rows2[:, :], bank2[0:16, 0:384], ACT.Copy, scale=8.0), t2)
            PT.put(b, ta)
            PT.put(b2, tb)
            t_bias = load("brow", [(bias_dram[0:8, :], rows[0:8, :]), (bias_dram[8:16, :], rows2[8:16, :])], ta, tb)
            init_fence = fence() + [t_bias]

        O = sb("O", [128, 16, S], F, c1)
        QA, QC = O[:, 0:4, :], O[:, 12:16, :]
        GT1 = sb("GT1", [128, 3, 4, S], F, c1)
        o_tok = [[] for _ in range(16)]
        c2 = ctx.enter_context(ExitStack())
        KA, KC = sb("KA", [128, 2, S], F, c2), sb("KC", [128, 4, S], F, c2)
        VA, VC = sb("VA", [128, 2, 128], F, c2), sb("VC", [128, 2, 512], F, c2)
        BI = Slots([sb(f"bi{i}", [128, S], F, c2) for i in range(4)])
        SS = Slots([sb(f"ss{i}", [128, 384], F, c2) for i in range(4)])
        PTB = Slots([sb(f"ptb{i}", [128, 384], F, c2) for i in range(4)])
        st8 = Slots([sb(f"st{i}", [128, 16], F, c2) for i in range(5)])
        snk = sb("snk", [128, 16], F, c2)
        GW = Slots([sb(f"gw{i}", [128, 2, 2, 128], F, c2) for i in range(2)])
        clam = sb("clam", [128, 48], F, c2)
        RT = Slots([[sb(f"rt{i}_{n}", [128, 2, S], F, c2) for n in range(5)] for i in range(2)])
        t_snk = load("snk", [(snk[:, 0:8], a["sinks"].broadcast_to([128, 8]))], init_fence)
        t_snk = dve.do(lambda e: e.tensor_scalar(snk[:, 8:16], snk[:, 0:8], -1.0, None, ALU.mult), t_snk)
        t_m = [pool.do(lambda e, w=w: e.memset(w[:, :, :, :], 0.0), init_fence) for w in GW.bufs]
        gsrc = [w.rearrange("(m two) c d -> two c m d", two=2) for w in (a["rnn_gate_a_w"][0], a["rnn_gate_x_w"][0])]

        def load_gates(j):
            k, gw, fr = GW.get()
            prs = [(gw[two * 64:two * 64 + 64, w, :, two * 64:two * 64 + 64], gsrc[w][two][:, 2 * j:2 * j + 2, :])
                   for w in range(2) for two in range(2)]
            return k, gw, load(f"gw{k}", prs, t_m, fr)

        L = vec("lam")
        cl = lambda i: clam[:, 8 * i:8 * i + 8]
        t = dve.do(lambda e: e.tensor_scalar(cl(1), L, -1.0, None, ALU.mult), vec_tok, init_fence)
        t = dve.do(lambda e: e.tensor_tensor(cl(1), cl(1), L, ALU.min), t)
        t = act.do(lambda e: e.activation(cl(2), cl(1), ACT.Exp), t)
        t = dve.do(lambda e: e.tensor_scalar(cl(3), cl(2), 1.0, None, ALU.add), t)
        ta = act.do(lambda e: e.activation(cl(4), cl(3), ACT.Ln), t)
        t = dve.do(lambda e: e.tensor_scalar(cl(3), cl(3), -1.0, None, ALU.add), ta)
        t = dve.do(lambda e: e.tensor_scalar(cl(5), cl(3), 0.0, None, ALU.is_equal), t)
        t = dve.do(lambda e: e.tensor_tensor(cl(4), cl(4), cl(2), ALU.mult), ta, t)
        t = dve.do(lambda e: e.tensor_tensor(cl(2), cl(2), cl(5), ALU.mult), t)
        t = dve.do(lambda e: e.tensor_tensor(cl(3), cl(3), cl(5), ALU.add), t)
        t = dve.do(lambda e: e.reciprocal(cl(3), cl(3)), t)
        t = dve.do(lambda e: e.tensor_tensor(cl(4), cl(4), cl(3), ALU.mult), t)
        t = dve.do(lambda e: e.tensor_tensor(cl(4), cl(4), cl(2), ALU.add), t)
        t = dve.do(lambda e: e.tensor_scalar(cl(5), L, -1.0, 0.0, ALU.mult, ALU.max), t)
        t = dve.do(lambda e: e.tensor_tensor(cl(4), cl(4), cl(5), ALU.add), t)
        t_lam = dve.do(lambda e: e.tensor_scalar(cl(0), cl(4), -8.0, None, ALU.mult), t)

        z_ready = {}

        def norm_pair(bank, b, tok, dst, gains, n=512):
            while SQ.busy() or RS.busy():
                yield
            k, sq, fs = SQ.get()
            t = act.do(lambda e: e.activation(sq[:, 0:n], bank[:, 0:n], ACT.Square), tok, fs)
            yield
            while PT.busy() or RS.busy():
                yield
            b2, bank2, fr2 = PT.get()
            t = pe.do(lambda e: e.matmul(bank2[:, 0:n], bones, sq[:, 0:n], start=True, stop=True), t, fr2)
            SQ.put(k, t)
            kr, r, fr = RS.get()
            t = act.do(lambda e: e.activation(r[:, 0:n], bank2[:, 0:n], ACT.Ln, bias=eps_c[:, 0:1], scale=1.0 / 64), t, fr, t_eps)
            PT.put(b2, t)
            t = act.do(lambda e: e.activation(r[:, 0:n], r[:, 0:n], ACT.Exp, scale=-0.5), t)
            yield
            td = dve.do(lambda e: e.scalar_tensor_tensor(out=dst, in0=bank[:, 0:n], scalar=gains,
                                                         in1=r[:, 0:n], op0=ALU.mult, op1=ALU.mult), t, vec_tok, init_fence)
            RS.put(kr, td)
            PT.put(b, td)
            return td

        def norm_heads(dst, gains, key):
            def ev(bank, tok, b):
                def rest():
                    z_ready.setdefault(key, []).append((yield from norm_pair(bank, b, tok, dst, gains)))
                pending.append(rest())
            return ev

        LIMIT[0], RATE[0] = 12, 12
        for j in range(2):
            (lambda ev: ev(*held[j]))(norm_heads(QA[:, 2 * j:2 * j + 2, :].rearrange("p m t -> p (m t)"), vec("qa"), "qa"))

        i, h, l, nk = take(("z", 512))
        b, bank, fr = PG.get()
        b2, bank2, fr2 = PG.get()
        pe.wait(fr, fr2)
        for k in range(8):
            for q, (w, xx) in enumerate([(h, HH), (h, HL), (l, HH)]):
                pe.run(lambda e, w=w, xx=xx, k=k, q=q: e.matmul(bank[:, 0:S], w[:, k, 0:128], xx[:, k, :],
                                                                 start=(k == 0 and q == 0), stop=(k == 7 and q == 2)))

        def natural(bankx, h, l, hi, lo, tbs, nks=8, cols=256):
            for n, tb_ in enumerate(tbs):
                for k in range(nks):
                    for q, (xx, w) in enumerate([(hi, h), (lo, h), (hi, l)]):
                        f = lambda e, w=w, xx=xx, k=k, q=q, n=n, tb_=tb_: e.matmul(
                            bankx[:, n * 256:n * 256 + cols], xx[:, k, tb_ * 128:(tb_ + 1) * 128], w[:, k, 0:cols],
                            start=(k == 0 and q == 0), stop=(k == nks - 1 and q == 2))
                        if n == len(tbs) - 1 and k == nks - 1 and q == 2:
                            return pe.do(f)
                        pe.run(f)
                tick()

        t = natural(bank2, h, l, HH, HL, [0, 1])
        done(i, t)
        t_va = act.do(lambda e: e.copy(VA[:, :, :], bank2[:, :].rearrange("p (b n) -> p b n", b=2)[:, :, 128:256]), t, init_fence)
        PG.put(b2, t_va)

        def ka_rest(b, bank, tok):
            kr, r, fr = RT.get()
            z = r[0].rearrange("p m t -> p (m t)")[:, 0:S]
            td = yield from norm_pair(bank, b, tok, z, vec("ka"), S)
            yield
            while PT.busy():
                yield
            b, bank, fr = PT.get()
            for j in range(2):
                for r0 in (0, 64):
                    t = pe.do(lambda e, j=j, r0=r0: e.matmul(bank[r0:r0 + 64, j * S:(j + 1) * S], ident[:, 64 * j:64 * j + 64],
                                                             z, start=True, stop=True), fr, td)
            t = act.do(lambda e: e.copy(KA[:, :, :], bank[:, :].rearrange("p (m t) -> p m t", m=2)), t, init_fence)
            PT.put(b, t)
            RT.put(kr, t)
            z_ready["ka"] = [t]
        pending.append(ka_rest(b, bank, t))
        tick()

        def load_bias(h):
            kb, bi, fb = BI.get()
            src = bass.AP(bias_dram, h * 384, [[1, 128], [1, 256]])
            return kb, bi, load("bi%d" % kb, [(bi[:, :], src)], fb, t_bias, init_fence)

        def attention(h, q, k, v, toks, och, swa):
            while BI.busy():
                yield
            kb, bi, t_b = load_bias(h)
            yield
            while PT.busy() or SS.busy() or PTB.busy() or st8.busy():
                yield
            b, bank, fr = PT.get()
            spans = [(0, 128), (128, 256)]
            for qb, (o0, nk) in enumerate(spans):
                o = bank[:, o0:o0 + nk]
                pe.run(lambda e: e.matmul(o, q[:, qb * 128:qb * 128 + 128], k[:, 0:nk], start=True, stop=False), fr, toks)
                t = pe.do(lambda e: e.matmul(o, JJ[:, :], bi[:, 256 - nk:256], start=False, stop=True), t_b, t_snk)
            BI.put(kb, t)
            ks, s, fs = SS.get()
            kp, pt, fp = PTB.get()
            kq, st, fq = st8.get()
            yield
            for qb, (o0, nk) in enumerate(spans):
                t1 = dve.do(lambda e: e.tensor_reduce(st[:, qb:qb + 1], bank[:, o0:o0 + nk], AX, ALU.max), t, fq, init_fence)
            if swa:
                t1 = dve.do(lambda e: e.tensor_scalar(st[:, 2:4], st[:, 0:2], -0.125, snk[:, 8 + h:9 + h], ALU.mult, ALU.min), t1, t_snk)
            else:
                t1 = dve.do(lambda e: e.tensor_scalar(st[:, 2:4], st[:, 0:2], -0.125, None, ALU.mult), t1)
            yield
            for qb, (o0, nk) in enumerate(spans):
                t2 = act.do(lambda e: e.activation(s[:, o0:o0 + nk], bank[:, o0:o0 + nk], ACT.Exp, bias=st[:, 2 + qb:3 + qb], scale=0.125,
                                                   accum_out=st[:, 4 + qb:5 + qb]), t1, fs, init_fence)
            PT.put(b, t2)
            if swa:
                t3 = act.do(lambda e: e.activation(st[:, 6:8], st[:, 2:4], ACT.Exp, bias=snk[:, h:h + 1]), t_snk)
            yield
            if swa:
                t2 = dve.do(lambda e: e.tensor_tensor(st[:, 4:6], st[:, 4:6], st[:, 6:8], ALU.add), t3)
            t4 = dve.do(lambda e: e.reciprocal(st[:, 8:10], st[:, 4:6]), t2)
            for qb, (o0, nk) in enumerate(spans):
                t5 = dve.do(lambda e: e.tensor_scalar(s[:, o0:o0 + nk], s[:, o0:o0 + nk], st[:, 8 + qb:9 + qb], None, ALU.mult), t4)
            st8.put(kq, t5)
            yield
            while PT.busy():
                yield
            b, bank, fr = PT.get()
            for j in range(3):
                t = pe.do(lambda e, j=j: e.transpose(bank[:, j * 128:(j + 1) * 128], s[:, j * 128:(j + 1) * 128], ident), fr, t5)
            SS.put(ks, t)
            yield
            t5 = act.do(lambda e: e.copy(pt[:, :], bank[:, 0:384]), t, fp, init_fence)
            PT.put(b, t5)
            yield
            while PT.busy():
                yield
            b, bank, fr = PT.get()
            r0 = 64 * (h % 2)
            o = bank[r0:r0 + 64, 0:S]
            pe.run(lambda e: e.matmul(o, v[:, 0, :], pt[:, 0:S], start=True, stop=False, skip_group_check=True), fr, t5, toks)
            t = pe.do(lambda e: e.matmul(bank[r0:r0 + 64, 128:S], v[:, 1, :], pt[:, S:384], start=False, stop=True, skip_group_check=True))
            PTB.put(kp, t)
            yield
            th = act.do(lambda e: e.copy(O[r0:r0 + 64, och, :], o), t)
            PT.put(b, th)
            o_tok[och].append(th)

        def swa(h):
            r0 = 64 * (h % 2)
            while "ka" not in z_ready or len(z_ready.get("qa", ())) < 2:
                yield
            yield from attention(h, QA[r0:r0 + 64, h // 2, :], KA[r0:r0 + 64, h // 4, :],
                                 VA[:, :, (h // 4) * 64:(h // 4) * 64 + 64], z_ready["qa"] + z_ready["ka"] + [t_va], h // 2, True)

        for j in range(2):
            gemmT([(("z", 2816 + 256 * j), 8)], HH, HL, h_tok, norm_heads(QC[:, 2 * j:2 * j + 2, :].rearrange("p m t -> p (m t)"), vec("qc"), "qc"), keep=True)
        pending += [swa(h) for h in range(0, 4)]
        for j in range(2):
            gemmT([(("z", 3328 + 256 * j), 8)], HH, HL, h_tok, norm_heads(KC[:, 2 * j:2 * j + 2, :].rearrange("p m t -> p (m t)"), vec("kc"), "kc"), keep=True)
        pending += [swa(h) for h in range(4, 8)]
        t_vc = []
        for j in range(2):
            i, h, l, nk = take(("z", 3840 + 256 * j))
            b, bank, fr = PG.get()
            pe.wait(fr)
            t = natural(bank, h, l, HH, HL, [0, 1])
            done(i, t)
            tt = act.do(lambda e, j=j, bank=bank: e.copy(VC[:, :, 256 * j:256 * j + 256], bank[:, :].rearrange("p (b n) -> p b n", b=2)), t, init_fence)
            PG.put(b, tt)
            t_vc.append(tt)
            tick()

        def moba(h):
            r0 = 64 * (h % 2)
            while len(z_ready.get("qc", ())) < 2 or len(z_ready.get("kc", ())) < 2:
                yield
            yield from attention(8 + h, QC[r0:r0 + 64, h // 2, :], KC[r0:r0 + 64, h // 2, :],
                                 VC[:, :, h * 64:h * 64 + 64], z_ready["qc"] + z_ready["kc"] + t_vc, 12 + h // 2, False)
        pending += [moba(h) for h in range(8)]

        def tt2(o, x, y, op, *t):
            return dve.do(lambda e: e.tensor_tensor(o, x, y, op), *t)

        rcw, rcb = vec("rcw"), vec("rcb")
        def rnn_xr(j, kr, rt, fr):
            def ev(bank, tok, b):
                for m in range(2):
                    c = 2 * j + m
                    t = act.do(lambda e: e.activation(rt[0][:, m, :], bank[:, m * S:(m + 1) * S], ACT.Identity,
                                                      bias=rcb[:, c:c + 1], scale=rcw[:, 24 + c:25 + c]), tok, fr, init_fence, vec_tok)
                yield
                for k in (2, 1, 0):
                    for m in range(2):
                        c, d = 2 * j + m, 3 - k
                        t = dve.do(lambda e: e.scalar_tensor_tensor(
                            out=rt[0][:, m, d:S], in0=bank[:, m * S:(m + 1) * S - d], scalar=rcw[:, 8 * k + c:8 * k + c + 1],
                            in1=rt[0][:, m, d:S], op0=ALU.mult, op1=ALU.add), t, dve.now() if m == 0 else None)
                rnn_x[j] = [t]
                PG.put(b, t)
            return lambda bank, tok, b: urgent.append(ev(bank, tok, b))

        def rnn_yr(j):
            def ev(bank, tok):
                t = act.do(lambda e: e.copy(O[:, 4 + 2 * j:6 + 2 * j, :], bank[:, :].rearrange("p (m t) -> p m t", m=2)), tok, init_fence)
                rnn_y[j] = [t]
                return [t]
            return ev
        rnn_x, rnn_y = {}, {}

        def rnn(j, kr, rt, fr, kgw, gw, t_gw):
            xc, ga, gx, ww, gl = rt
            yy = O[:, 4 + 2 * j:6 + 2 * j, :]
            yield
            t = tt2(gl[:, :, :], yy, yy, ALU.mult, rnn_y[j], fr, init_fence)
            t = dve.do(lambda e: e.tensor_scalar(gl[:, :, :], gl[:, :, :], 0.044715, 1.0, ALU.mult, ALU.add), t)
            t_gl = tt2(gl[:, :, :], gl[:, :, :], yy, ALU.mult, t)
            bks = []
            for w in range(2):
                while PT.busy():
                    yield
                b, bank, f = PT.get()
                for m in range(2):
                    t = pe.do(lambda e: e.matmul(bank[:, m * S:(m + 1) * S], gw[:, w, m, :], xc[:, m, :],
                                                 start=True, stop=True), f, rnn_x[j], t_gw)
                bks.append((b, bank, t))
            GW.put(kgw, t)
            yield
            t_gate = []
            for (b, bank, t), dst, bn in zip(bks, (ga, gx), ("gab", "gxb")):
                for m in range(2):
                    c = 2 * j + m
                    t = act.do(lambda e: e.activation(dst[:, m, :], bank[:, m * S:(m + 1) * S], ACT.Sigmoid, bias=vec(bn)[:, c:c + 1]),
                               t, fr, init_fence, vec_tok)
                PT.put(b, t)
                t_gate.append(t)
            tg = act.do(lambda e: e.activation(gl[:, :, :], gl[:, :, :], ACT.Sigmoid, scale=2.0 * math.sqrt(2.0 / math.pi)), t_gl)
            yield
            for m in range(2):
                c = 2 * j + m
                ta = act.do(lambda e: e.activation(ga[:, m, :], ga[:, m, :], ACT.Exp, scale=clam[:, c:c + 1]), t_gate[0], t_lam)
            tu = tt2(gx[:, :, :], gx[:, :, :], xc[:, :, :], ALU.mult, t_gate[1])
            tg = tt2(gl[:, :, :], gl[:, :, :], yy, ALU.mult, tg)
            yield
            t = dve.do(lambda e: e.tensor_scalar(ww[:, :, :], ga[:, :, :], -1.0, 1.0, ALU.mult, ALU.add), ta, fr, init_fence)
            t = dve.do(lambda e: e.scalar_tensor_tensor(out=ww[:, :, :], in0=ga[:, :, :], scalar=1.0, in1=ww[:, :, :], op0=ALU.add, op1=ALU.mult), t)
            t = dve.do(lambda e: e.tensor_scalar(ww[:, :, :], ww[:, :, :], 0.0, None, ALU.max), t)
            yield
            t = act.do(lambda e: e.activation(ww[:, :, :], ww[:, :, :], ACT.Sqrt), t)
            yield
            t = dve.do(lambda e: e.memset(ww[:, :, 0:1], 1.0), t)
            t = tt2(gx[:, :, :], gx[:, :, :], ww[:, :, :], ALU.mult, tu, t)
            for m in range(2):
                ts = dve.do(lambda e: e.tensor_tensor_scan(ww[:, m, :], ga[:, m, :], gx[:, m, :], 0.0, ALU.mult, ALU.add), t)
            t = tt2(yy, ww[:, :, :], gl[:, :, :], ALU.mult, tg, ts)
            o_tok[4 + 2 * j] = o_tok[5 + 2 * j] = [t]
            RT.put(kr, t)

        for j in range(4):
            RTj = RT.get()
            gwj = load_gates(j)
            gemmT([(("z", 768 + 256 * j), 8)], HH, HL, h_tok, rnn_xr(j, *RTj), keep=True)
            gemmT([(("z", 1792 + 256 * j), 8)], HH, HL, h_tok, rnn_yr(j))
            pending.insert(0, rnn(j, *RTj, *gwj))

        def gate_ev(dst, wf):
            def ev(bank, tok):
                t = act.do(lambda e: e.copy(dst, bank[:, :].rearrange("p (m t) -> p m t", m=2)), tok, wf)
                g_raw.append(t)
                return [t]
            return ev
        g_raw = []
        for c in range(2):
            for g in range(3):
                gemmT([(("z", 4352 + 1024 * g + 256 * c), 8)], HH, HL, h_tok, gate_ev(GT1[:, g, 2 * c:2 * c + 2, :], init_fence))
        drain()
        fz1 = fence()
        c2.close()

        c2 = ctx.enter_context(ExitStack())
        GT2 = sb("GT2", [128, 3, 4, S], F, c2)
        OH, OL = sb("OH", [128, 16, S], R, c2), sb("OL", [128, 16, S], R, c2)
        g_tok = [act.do(lambda e: e.activation(GT1[:, :, :, :], GT1[:, :, :, :], ACT.Sigmoid), g_raw)]
        oh_tok = Chunks([None] * 16)

        def split_o():
            for c in range(8):
                yield from split_later(oh_tok, c, OH, OL, O[:, 2 * c:2 * c + 2, :], [o_tok[2 * c], o_tok[2 * c + 1]], fz1)
        urgent.append(split_o())
        for c in range(2):
            for g in range(3):
                def ev(bank, tok):
                    t = act.do(lambda e: e.activation(GT2[:, g, 2 * c:2 * c + 2, :], bank[:, :].rearrange("p (m t) -> p m t", m=2), ACT.Sigmoid), tok, fz1)
                    g_tok.append(t)
                    return [t]
                gemmT([(("z", 4352 + 1024 * g + 256 * (c + 2)), 8)], HH, HL, h_tok, ev)
        mtok = Chunks([None] * 8)
        hfree = pe.now()

        def merge(c, bk, t):
            G_, c_ = (GT1, 2 * c) if c < 2 else (GT2, 2 * c - 4)
            gs = [G_[:, g, c_:c_ + 2, :] for g in range(3)]
            bv = [x[1][:, :].rearrange("p (m t) -> p m t", m=2) for x in bk]
            yield
            tts = [tt2(gs[g], bv[g], gs[g], ALU.mult, t, g_tok) for g in range(3)]
            for g in range(3):
                PG.put(bk[g][0], tts[g])
            t1 = tt2(gs[0], gs[0], gs[1], ALU.add, tts)
            t1 = tt2(gs[0], gs[0], gs[2], ALU.add, t1)
            yield
            yield from split_later(mtok, c, HH, HL, gs[0], t1, hfree)

        for c in range(4):
            bk = [PG.get(), PG.get(), PG.get()]
            pe.wait(*[x[2] for x in bk])
            kb = 0
            for s_ in range(2):
                i, h, l, nk = take(("br", c))
                for m in range(2):
                    for k in range(8):
                        kk = kb + k
                        g = 0 if kk < 4 else (1 if kk < 12 else 2)
                        step_wait(oh_tok, kk)
                        lo_, hi_ = ((0, 3), (4, 11), (12, 15))[g]
                        for q, (w, xx) in enumerate([(h, OH), (h, OL), (l, OH)]):
                            st = kk == lo_ and q == 0 and m == 0
                            sp_ = kk == hi_ and q == 2
                            f = lambda e, w=w, xx=xx, k=k, kk=kk, m=m, g=g, st=st, sp_=sp_, bk=bk: e.matmul(
                                bk[g][1][:, m * S:(m + 1) * S], w[:, k, m * 128:(m + 1) * 128], xx[:, kk, :],
                                start=st, stop=sp_, skip_group_check=True)
                            if m == 1 and k == 7 and q == 2:
                                t = pe.do(f)
                            else:
                                pe.run(f)
                    if m == 0:
                        tick()
                kb += 8
                done(i, t)
                tick()
            urgent.append(merge(c, bk, t))
        def residual(gate, gt):
            r, st_ = Chunks(), Stats()

            def mk(c):
                def ev(bank, tok):
                    for m in range(2):
                        cc = 2 * c + m
                        tk = dve.do(lambda e, cc=cc, m=m: e.scalar_tensor_tensor(
                            out=X[:, cc, :], in0=bank[:, m * S:(m + 1) * S], scalar=gate[:, cc:cc + 1], in1=X[:, cc, :],
                            op0=ALU.mult, op1=ALU.add), tok, gt)
                    r.extend([[tk], [tk]])
                    st_.later(X[:, 2 * c:2 * c + 2, :], tk)
                    return [tk]
                return ev
            return r, mk, st_

        skip_mods()
        r, mk, xst = residual(modT[0][:, 16:24], mod_tok[0, 5])
        for c in range(4):
            gemmT([(("out", c), 8)], HH, HL, mtok, mk(c))
        x_tok, xrs = r, xst.close(D)
        c2.close()
        hfree = fence()

        c1.close()
        c1 = ctx.enter_context(ExitStack())
        HHc, HLc = sb("HHc", [128, 8, S], R, c1), sb("HLc", [128, 8, S], R, c1)
        HH, HL = sb("HH2", [128, 8, S], R, c1), sb("HL2", [128, 8, S], R, c1)
        c2 = ctx.enter_context(ExitStack())
        FH, FL = sb("FH", [128, 22, S], R, c2), sb("FL", [128, 22, S], R, c2)
        A1, At1 = coeff(8, vec("norm_ffn"), modT[0][:, 32:40], mod_tok[0, 9])
        h_tok = modulate(X, xrs, x_tok, A1, At1, modT[0][:, 24:32], mod_tok[0, 7], HH, HL, hfree)
        UC = Slots([sb(f"uc{i}", [128, 2, S], F, c2) for i in range(3)])
        cw = lambda k, c: (vec("fcw01")[:, 44 * k + c:44 * k + c + 1] if k < 2 else vec("fcw2")[:, c:c + 1])
        f_tok = Chunks([None] * 22)

        def conv_ev(which, c):
            def ev(bank, tok, b):
                k_, u, fu = UC.get()
                for m in range(2):
                    ch = 22 * which + 2 * c + m
                    t = act.do(lambda e: e.activation(u[:, m, :], bank[:, m * S:(m + 1) * S], ACT.Identity,
                                                      bias=vec("fcb")[:, ch:ch + 1], scale=cw(2, ch)), tok, fu, hfree)
                urgent.append(rest(bank, b, k_, u, t))

            def rest(bank, b, k_, u, t):
                yield
                for k in (1, 0):
                    for m in range(2):
                        ch, d = 22 * which + 2 * c + m, 2 - k
                        t = dve.do(lambda e: e.scalar_tensor_tensor(
                            out=u[:, m, d:S], in0=bank[:, m * S:(m + 1) * S - d], scalar=cw(k, ch), in1=u[:, m, d:S],
                            op0=ALU.mult, op1=ALU.add), t)
                PG.put(b, t)
                yield
                if which == 0:
                    ta = act.do(lambda e: e.activation(u[:, :, :], u[:, :, :], ACT.Silu), t)
                    gate[c] = (k_, u, ta)
                    return
                kg, g, ta = gate.pop(c)
                tm = tt2(u[:, :, :], u[:, :, :], g[:, :, :], ALU.mult, ta, t)
                UC.put(kg, tm)
                yield
                yield from split_later(f_tok, c, FH, FL, u[:, :, :], tm, hfree)
                UC.put(k_, *f_tok[2 * c])
            return ev
        gate = {}

        c3 = ctx.enter_context(ExitStack())
        cn, cT = sb("cn", [128, 1, 1024], F, c3), sb("cT", [128, 8, S], F, c3)

        def context():
            ct = Chunks([[] for _ in range(8)])
            wf = hfree
            for tb_ in range(2):
                t_x = load("cn", [(cn[:, 0, :], a["ctx_2"][0, tb_ * 128:(tb_ + 1) * 128, :])], wf)
                yield
                yield
                for c in range(0, 8, 4):
                    while PT.busy():
                        yield
                    b, bank, fr = PT.get()
                    for j in range(4):
                        t = pe.do(lambda e: e.transpose(bank[:, j * 128:(j + 1) * 128], cn[:, 0, (c + j) * 128:(c + j + 1) * 128], ident), fr, t_x)
                    wf = t
                    t = act.do(lambda e: e.copy(cT[:, c:c + 4, tb_ * 128:tb_ * 128 + 128], bank[:, :].rearrange("p (j t) -> p j t", j=4)), t, hfree)
                    PT.put(b, t)
                    for j in range(4):
                        ct[c + j].append(t)
                    yield
            while PT.busy():
                yield
            st_ = Stats()
            for c in range(0, 8, 2):
                while SQ.busy():
                    yield
                st_.add(cT[:, c:c + 2, :], ct[c])
                yield
            while RS.busy():
                yield
            while (2, 3) not in mod_tok:
                yield
            Ac, Act_ = coeff(16, vec("n10"), modT[2][:, 8:16], mod_tok[2, 3])
            rs = st_.close(D)
            yield
            yield from modulate_steps(ctx_tok, cT, rs, ct, Ac, Act_, modT[2][:, 0:8], mod_tok[2, 1], HHc, HLc, hfree)
        ctx_tok = Chunks()
        pending.append(context())
        for c in range(11):
            gemmT([(("ug", c), 8)], HH, HL, h_tok, conv_ev(0, c), keep=True)
            gemmT([(("uv", c), 8)], HH, HL, h_tok, conv_ev(1, c), keep=True)
        skip_mods()
        r, mk, xst = residual(modT[0][:, 40:48], mod_tok[0, 11])
        for c in range(4):
            gemmT([(("dn", c), 8), (("dn", c), 8), (("dn", c), 6)], FH, FL, f_tok, mk(c))
        drain()
        x_tok, xrs = r, xst.close(D)
        c3.close()
        c2.close()
        hfree = fence()

        c2 = ctx.enter_context(ExitStack())
        Ax, Axt = coeff(24, vec("n10"), modT[1][:, 8:16], mod_tok[1, 3])
        h_tok = modulate(X, xrs, x_tok, Ax, Axt, modT[1][:, 0:8], mod_tok[1, 1], HH, HL, hfree)
        Q2, K2 = sb("Q2", [128, 8, S], F, c2), sb("K2", [128, 8, 512], F, c2)
        V2 = sb("V2", [128, 4, 1024], F, c2)
        cs = sb("cs", [128, 640], F, c2)
        rot = cs[:, 512:640]
        cfree = hfree
        t_cs = load("cs", [(cs[:, 0:512], a["consts"][:, C_COS:C_COS + 512]), (rot, a["consts"][:, C_ROT:C_ROT + 128])], cfree)
        z_ready = {}

        def rope(c, dst, tz, key):
            while PT.busy() or SQ.busy():
                yield
            b, bank, fr = PT.get()
            k, z, fz = SQ.get()
            zz = z[:, :].rearrange("p (m t) -> p m t", m=2)
            for m in range(2):
                t = pe.do(lambda e: e.matmul(bank[:, m * S:(m + 1) * S], rot, dst[:, m, :], start=True, stop=True), fr, tz, t_cs)
            yield
            for m in range(2):
                t1 = tt2(z[:, m * S:(m + 1) * S], bank[:, m * S:(m + 1) * S], cs[:, 256:512], ALU.mult, t, t_cs, fz)
            PT.put(b, t1)
            for m in range(2):
                t2 = tt2(dst[:, m, :], dst[:, m, :], cs[:, 0:256], ALU.mult, t, t_cs)
            t3 = tt2(dst, dst, zz, ALU.add, t1, t2)
            SQ.put(k, t3)
            z_ready[key, c] = t3

        def q_ev(c):
            def ev(bank, tok):
                tz = act.do(lambda e: e.copy(Q2[:, 2 * c:2 * c + 2, :], bank[:, :].rearrange("p (m t) -> p m t", m=2)), tok, cfree)
                pending.append(rope(c, Q2[:, 2 * c:2 * c + 2, :], tz, "q"))
                return [tz]
            return ev

        def k_ev(c):
            def ev(bks, tok):
                tz = [act.do(lambda e: e.copy(K2[:, 2 * c + m, :], bks[m][:, :]), tok, cfree) for m in range(2)]
                pending.append(rope(c, K2[:, 2 * c:2 * c + 2, S:512], tz, "k"))
                return [tz[0:1], tz[1:2]]
            return ev

        lq = sb("lq", [128, 4, 64], F, c2)
        lt = sb("lt", [128, 16], F, c2)
        t_l = load("lq", [(lq[:, n, :], a[nm].broadcast_to([128, 64])) for n, nm in
                          enumerate(("attn_lq1_2", "attn_lk1_2", "attn_lq2_2", "attn_lk2_2"))], cfree)
        lam_init = 0.8 - 0.6 * math.exp(-0.3 * 0)
        for n in range(2):
            t = dve.do(lambda e, n=n: e.tensor_tensor_reduce(lq[:, 2 * n, :], lq[:, 2 * n, :], lq[:, 2 * n + 1, :], 1.0, 0.0,
                                                             ALU.mult, ALU.add, lt[:, n:n + 1]), t_l, cfree)
        t = act.do(lambda e: e.activation(lt[:, 2:4], lt[:, 0:2], ACT.Exp), t)
        t_lm = dve.do(lambda e: e.scalar_tensor_tensor(out=lt[:, 4:5], in0=lt[:, 2:3], scalar=lam_init, in1=lt[:, 3:4],
                                                       op0=ALU.add, op1=ALU.subtract), t)
        LAM = lt[:, 4:5]
        t_sg = dve.do(lambda e: e.tensor_scalar(lt[:, 5:6], vec("sub"), 1.0 - lam_init, None, ALU.mult), vec_tok, t_lm)
        SUBG = lt[:, 5:6]
        PP = Slots([sb(f"pp{i}", [128, 2, 512], F, c2) for i in range(3)])
        AT = Slots([sb(f"at{i}", [128, 4, S], F, c2) for i in range(2)])
        ST = Slots([sb(f"sr{i}", [128, 12], F, c2) for i in range(2)])
        a_tok = [None] * 8

        def da_head(h):
            while ("q", h // 2) not in z_ready or ("k", h // 2) not in z_ready:
                yield
            tq = [z_ready["q", h // 2], z_ready["k", h // 2]]
            for qb in range(2):
                while PP.busy() or ST.busy() or len(PT.order) < 2:
                    yield
                kp, pp, fp = PP.get()
                ks, s, fs = ST.get()
                bks = []
                for n in range(2):
                    r0 = 64 * n
                    b, bank, fr = PT.get()
                    t = pe.do(lambda e: e.matmul(bank[:, :], Q2[r0:r0 + 64, h, qb * 128:qb * 128 + 128],
                                                 K2[r0:r0 + 64, h, :], start=True, stop=True), fr, tq)
                    bks.append((b, bank))
                yield
                for n, (b, bank) in enumerate(bks):
                    t = dve.do(lambda e: e.tensor_reduce(s[:, n:n + 1], bank[:, :], AX, ALU.max), t, fs, cfree)
                t = dve.do(lambda e: e.tensor_scalar(s[:, 2:4], s[:, 0:2], -0.125, None, ALU.mult), t)
                for n, (b, bank) in enumerate(bks):
                    te = act.do(lambda e: e.activation(pp[:, n, :], bank[:, :], ACT.Exp, bias=s[:, 2 + n:3 + n], scale=0.125,
                                                       accum_out=s[:, 4 + n:5 + n]), t, fp, cfree)
                    PT.put(b, te)
                yield
                t = dve.do(lambda e: e.reciprocal(s[:, 6:8], s[:, 4:6]), te)
                t = tt2(s[:, 8:9], s[:, 7:8], LAM, ALU.mult, t, t_lm)
                t = dve.do(lambda e: e.tensor_scalar(pp[:, 1, :], pp[:, 1, :], s[:, 8:9], None, ALU.mult), t)
                t = dve.do(lambda e: e.scalar_tensor_tensor(out=pp[:, 0, :], in0=pp[:, 0, :], scalar=s[:, 6:7], in1=pp[:, 1, :],
                                                            op0=ALU.mult, op1=ALU.subtract), t)
                ST.put(ks, t)
                yield
                while PT.busy() or (qb == 0 and AT.busy()):
                    yield
                if qb == 0:
                    ka, at, fa = AT.get()
                b, bank, fr = PT.get()
                for j in range(4):
                    tp = pe.do(lambda e: e.transpose(bank[:, j * 128:(j + 1) * 128], pp[:, 0, j * 128:(j + 1) * 128], ident), fr, t)
                PP.put(kp, tp)
                t = act.do(lambda e: e.copy(at[:, :, qb * 128:qb * 128 + 128], bank[:, :].rearrange("p (j q) -> p j q", j=4)),
                           tp, fa if qb == 0 else None, cfree)
                PT.put(b, t)
            yield
            while PT.busy():
                yield
            while ("v", h // 2) not in z_ready or PT.busy():
                yield
            b, bank, fr = PT.get()
            for j in range(4):
                tp = pe.do(lambda e: e.matmul(bank[:, 0:S], V2[:, j, h * 128:(h + 1) * 128], at[:, j, :], start=(j == 0), stop=(j == 3)),
                           fr, t, z_ready["v", h // 2])
            AT.put(ka, tp)
            while SQ.busy():
                yield
            k, sq, fs = SQ.get()
            yield
            ts = act.do(lambda e: e.activation(sq[:, 0:S], bank[:, 0:S], ACT.Square), tp, fs)
            to = act.do(lambda e: e.copy(Q2[:, h, :], bank[:, 0:S]), tp)
            PT.put(b, to)
            yield
            while PT.busy() or RS.busy():
                yield
            b, bank, fr = PT.get()
            tp = pe.do(lambda e: e.matmul(bank[:, 0:S], one[:, :], sq[:, 0:S], start=True, stop=True), ts, fr)
            SQ.put(k, tp)
            kr, r, fr = RS.get()
            t = act.do(lambda e: e.activation(r[:, 0:S], bank[:, 0:S], ACT.Ln, bias=eps_c[:, 0:1], scale=1.0 / 128), tp, fr)
            PT.put(b, t)
            t = act.do(lambda e: e.activation(r[:, 0:S], r[:, 0:S], ACT.Exp, scale=-0.5), t)
            yield
            t = dve.do(lambda e: e.scalar_tensor_tensor(out=Q2[:, h, :], in0=Q2[:, h, :], scalar=SUBG, in1=r[:, 0:S], op0=ALU.mult, op1=ALU.mult), t, t_sg, to)
            RS.put(kr, t)
            a_tok[h] = [t]

        for c in range(4):
            gemmT([(("qkv", 4 + c), 8)], HH, HL, h_tok, k_ev(c), two=(HHc, HLc, ctx_tok))
            gemmT([(("qkv", c), 8)], HH, HL, h_tok, q_ev(c))
            pending += [da_head(2 * c), da_head(2 * c + 1)]
            i, h, l, nk = take(("qkv", 8 + c))
            bb = [PG.get(), PG.get()]
            pe.wait(bb[0][2], bb[1][2])
            t = natural(bb[0][1], h, l, HHc, HLc, [0, 1])
            tick()
            t2 = natural(bb[1][1], h, l, HH, HL, [0, 1])
            done(i, t2)
            vt_ = []
            for n in range(2):
                tt = act.do(lambda e: e.copy(V2[:, 2 * n:2 * n + 2, 256 * c:256 * c + 256],
                                             bb[n][1][:, :].rearrange("p (b n) -> p b n", b=2)), (t, t2)[n], cfree)
                PG.put(bb[n][0], tt)
                vt_.append(tt)
            z_ready["v", c] = vt_
            tick()
        hf3 = pe.now()
        aready = Chunks([None] * 8)

        def split_a():
            for c in range(4):
                while a_tok[2 * c] is None or a_tok[2 * c + 1] is None:
                    yield
                yield from split_later(aready, c, HH, HL, Q2[:, 2 * c:2 * c + 2, :], a_tok[2 * c:2 * c + 2], hf3)
        urgent.append(split_a())
        r, mk, xst = residual(modT[1][:, 16:24], mod_tok[1, 5])
        for c in range(4):
            gemmT([(("wo", c), 8)], HH, HL, aready, mk(c))
        x_tok, xrs = r, xst.close(D)
        c2.close()
        c1.close()
        hfree = fence()
        cm = ctx.enter_context(ExitStack())
        misc = sb("misc", [128, 264], F, cm)
        rw = sb("rw", [128, 8, 8], F, cm)
        t_rw = load("rw", [(rw[:, :, :], a["moe_router_2"][0].rearrange("(k p) e -> p k e", p=128))], hfree)
        t_mi = load("misc", [(misc[:, 0:264], a["consts"][:, C_TRI:C_TRI + 264])], hfree)
        cm2 = ctx.enter_context(ExitStack())
        fcs = sb("fcs", [128, 1280], F, cm2)
        t_f = load("fcs", [(fcs[:, :], a["consts"][:, C_FD:C_FD + 1280])], hfree)
        c2 = ctx.enter_context(ExitStack())
        HH, HL = sb("HH4", [128, 8, S], R, c2), sb("HL4", [128, 8, S], R, c2)
        FH, FL = sb("FH4", [128, 28, S], R, c2), sb("FL4", [128, 28, S], R, c2)
        UC = Slots([sb(f"ud{i}", [128, 2, S], F, c2) for i in range(2)])
        A1, At1 = coeff(32, vec("n20"), modT[1][:, 32:40], mod_tok[1, 9])
        h_tok = modulate(X, xrs, x_tok, A1, At1, modT[1][:, 24:32], mod_tok[1, 7], HH, HL, hfree)
        f_tok, gate = Chunks([None] * 28), {}

        def f1_ev(c):
            def ev(bank, tok):
                k, u, fu = UC.get()
                t = act.do(lambda e: e.activation(u[:, :, :], bank[:, :].rearrange("p (m t) -> p m t", m=2), ACT.Silu), tok, fu, hfree)
                gate[c] = (k, u, t)
                return [t]
            return ev

        def f3_ev(c):
            def rest(k, u, tm):
                yield
                yield from split_later(f_tok, c, FH, FL, u[:, :, :], tm, hfree)
                UC.put(k, *f_tok[2 * c])

            def ev(bank, tok):
                k, u, tu = gate[c]
                tm = tt2(u[:, :, :], bank[:, :].rearrange("p (m t) -> p m t", m=2), u[:, :, :], ALU.mult, tok, tu)
                urgent.append(rest(k, u, tm))
                return [tm]
            return ev
        for c in range(14):
            gemmT([(("f1", c), 8)], HH, HL, h_tok, f1_ev(c))
            gemmT([(("f3", c), 8)], HH, HL, h_tok, f3_ev(c))
        skip_mods()
        r, mk, xst = residual(modT[1][:, 40:48], mod_tok[1, 11])
        for c in range(4):
            gemmT([(("f2", c), 8), (("f2", c), 8), (("f2", c), 8), (("f2", c), 4)], FH, FL, f_tok, mk(c))
        x_tok, xrs = r, xst.close(D)
        c2.close()
        hfree = fence()

        skip_mods()
        c2 = ctx.enter_context(ExitStack())
        FX = sb("FX", [128, 8, S], F, c2)
        FN = sb("FN", [128, 2, 8, 256], F, c2)
        HH, HL = sb("HH5", [128, 8, S], R, c2), sb("HL5", [128, 8, S], R, c2)
        A1, At1 = coeff(40, vec("n11"), modT[3][:, 8:16], mod_tok[3, 3])

        def norm_full(dst, rs, A, At, shift, st, toks, wf):
            k, r, t = rs
            o = Chunks()
            for c in range(8):
                t1 = dve.do(lambda e, c=c: e.scalar_tensor_tensor(out=dst[:, c, :], in0=X[:, c, :], scalar=A[:, c:c + 1],
                                                                  in1=r[:, 0:S], op0=ALU.mult, op1=ALU.mult), t, toks, At, wf)
                if shift is not None:
                    t1 = act.do(lambda e, c=c: e.activation(dst[:, c, :], dst[:, c, :], ACT.Identity, bias=shift[:, c:c + 1]), t1, st)
                o.append([t1])
            RS.put(k, dve.now())
            return o
        xt = norm_full(FX, xrs, A1, At1, modT[3][:, 0:8], mod_tok[3, 1], x_tok, hfree)
        gb = nA[:, 56:64]
        t_gb = tt2(gb, modT[3][:, 16:24], vec("fbo"), ALU.mult, mod_tok[3, 5], vec_tok)
        for c in range(8):
            t_gb = dve.do(lambda e: e.tensor_scalar(X[:, c, :], X[:, c, :], gb[:, c:c + 1], None, ALU.add), t_gb, xt)
        tn = []
        for g in range(8):
            b, bank, fr = PG.get()
            for tb_ in range(2):
                t = pe.do(lambda e, g=g, tb_=tb_, bank=bank: e.matmul(bank[:, tb_ * 256:tb_ * 256 + 256], FX[:, g, tb_ * 128:tb_ * 128 + 128],
                                                                     fcs[:, 0:256], start=True, stop=True), fr, xt[g], t_f)
            t = act.do(lambda e, g=g, bank=bank: e.copy(FN[:, :, g, :], bank[:, :].rearrange("p (b n) -> p b n", b=2)), t, hfree)
            PG.put(b, t)
            tn.append(t)
        f_tok = Chunks()
        for g in range(0, 8, 2):
            b, bank, fr = PG.get()
            for m in range(2):
                for s_ in range(4):
                    tb_, part = s_ // 2, s_ % 2
                    t = pe.do(lambda e, g=g, m=m, tb_=tb_, part=part, s_=s_, bank=bank: e.matmul(
                        bank[:, m * S:(m + 1) * S], FN[:, tb_, g + m, part * 128:part * 128 + 128],
                        fcs[:, 256 + tb_ * 512 + part * 256:256 + tb_ * 512 + part * 256 + 256],
                        start=(s_ == 0), stop=(s_ == 3)), fr, tn)
            rr = split(HH[:, g:g + 2, :], HL[:, g:g + 2, :], bank[:, :].rearrange("p (m t) -> p m t", m=2), t, hfree)
            PG.put(b, *rr)
            f_tok += [rr, rr]
        r, mk, xst = residual(modT[3][:, 16:24], [mod_tok[3, 5], t_gb])
        for c in range(4):
            gemmT([(("fn", c), 8)], HH, HL, f_tok, mk(c))
        x_tok, xrs = r, xst.close(D)
        c2.close()
        cm2.close()
        hfree = fence()

        c2 = ctx.enter_context(ExitStack())
        MO = sb("MO", [128, 8, S], F, cm)
        TH, TL = sb("TH", [128, 2, 1024], R, c2), sb("TL", [128, 2, 1024], R, c2)
        RO = sb("RO", [128, 2, 96], F, c2)
        RK = sb("RK", [128, 2, 8], F, c2)
        CN = sb("CN", [128, 64], F, c2)
        OV = sb("OV", [128, 2, 8], F, c2)
        CI = sb("CI", [128, 4], I32, c2)
        raw += [sb(f"raw{NR + i}", [128, 2048], F, c2) for i in range(NX)]
        wide[0] = hfree
        issue()
        c3 = ctx.enter_context(ExitStack())
        H2 = sb("H2", [128, 8, S], F, c3)
        A1, At1 = coeff(48, vec("n21"), modT[3][:, 32:40], mod_tok[3, 9])
        xt = norm_full(H2, xrs, A1, At1, modT[3][:, 24:32], mod_tok[3, 7], x_tok, hfree)
        tri, iota, eix = misc[:, 0:128], misc[:, 128:256], misc[:, 256:264]
        ro = lambda tb_, i, n=8: RO[:, tb_, 8 * i:8 * i + n]
        b, bank, fr = PT.get()
        for tb_ in range(2):
            for k in range(8):
                t = pe.do(lambda e: e.matmul(bank[:, 8 * tb_:8 * tb_ + 8], H2[:, k, tb_ * 128:tb_ * 128 + 128], rw[:, k, :],
                                             start=(k == 0), stop=(k == 7)), fr, xt[k], t_rw)
        rb = lambda i: RO[:, :, 8 * i:8 * i + 8]
        lg, eq1, s1, eq2, s2, l2, mk_, gt_, tmp_ = (rb(i) for i in range(9))
        col = lambda i: RO[:, :, 72 + i:73 + i]
        wide_ = lambda v: v.broadcast_to([128, 2, 8])
        eix2 = eix.rearrange("p (o e) -> p o e", o=1).broadcast_to([128, 2, 8])
        t = dve.do(lambda e: e.tensor_copy(lg, bank[:, 0:16].rearrange("p (b e) -> p b e", b=2)), t, hfree)
        PT.put(b, t)

        def top(lg, eq, sel, v, t):
            t = dve.do(lambda e: e.tensor_reduce(v, lg, AX, ALU.max), t)
            t = tt2(eq, lg, wide_(v), ALU.is_equal, t)
            t = tt2(eq, eq, eix2, ALU.mult, t, t_mi)
            t = dve.do(lambda e: e.tensor_reduce(col(7), eq, AX, ALU.max), t)
            return tt2(sel, eq, wide_(col(7)), ALU.is_equal, t)
        t = top(lg, eq1, s1, col(0), t)
        t = dve.do(lambda e: e.scalar_tensor_tensor(out=l2, in0=s1, scalar=-3.0e38, in1=lg, op0=ALU.mult, op1=ALU.add), t)
        t = top(l2, eq2, s2, col(1), t)
        t_mk = tt2(mk_, s1, s2, ALU.add, t)
        tok_t, tts_ = [], []
        for tb_ in range(2):
            for c in range(0, 8, 4):
                b, bank, fr = PG.get()
                for j in range(4):
                    t = pe.do(lambda e: e.transpose(bank[:, j * 128:(j + 1) * 128],
                                                    H2[:, c + j, tb_ * 128:tb_ * 128 + 128], ident), fr, xt)
                th = act.do(lambda e: e.copy(TH[:, tb_, c * 128:c * 128 + 512], bank[:, :]), t, hfree)
                tts_.append((b, bank, tb_, c, th))
        b, bank_r, fr = PT.get()
        pe.do(lambda e: e.matmul(bank_r[:, 0:8], tri, ro(0, 6), start=True, stop=True), fr, t_mk, t_mi)
        pe.do(lambda e: e.matmul(bank_r[:, 8:16], one[:, :], ro(0, 6), start=True, stop=False))
        t = pe.do(lambda e: e.matmul(bank_r[:, 8:16], tri, ro(1, 6), start=False, stop=True))
        t = dve.do(lambda e: e.scalar_tensor_tensor(out=RK[:, :, :], in0=bank_r[:, 0:16].rearrange("p (b e) -> p b e", b=2), scalar=1e4,
                                                    in1=mk_, op0=ALU.add, op1=ALU.mult), t, hfree)
        PT.put(b, t)
        tr = [dve.do(lambda e: e.tensor_scalar(RK[:, :, :], RK[:, :, :], -1e4, None, ALU.add), t)]
        def lows_and_gates():
            for b, bank, tb_, c, th in tts_:
                tl = dve.do(lambda e: e.tensor_tensor(TL[:, tb_, c * 128:c * 128 + 512], bank[:, :], TH[:, tb_, c * 128:c * 128 + 512].bitcast(F),
                                                      ALU.subtract), th, hfree)
                PG.put(b, tl)
                tok_t.extend([th, tl])
            t = tt2(col(2), col(1), col(0), ALU.subtract, t_mk)
            t = act.do(lambda e: e.activation(col(3), col(2), ACT.Exp), t)
            t = dve.do(lambda e: e.tensor_scalar(col(4), col(3), 1.0, None, ALU.add), t)
            t = dve.do(lambda e: e.reciprocal(col(4), col(4)), t)
            t = tt2(col(5), col(3), col(4), ALU.mult, t)
            t = tt2(gt_, s1, wide_(col(4)), ALU.mult, t)
            t1 = tt2(tmp_, s2, wide_(col(5)), ALU.mult, t)
            tm.append(tt2(gt_, gt_, tmp_, ALU.add, t, t1))
        tm = []
        mfree = [hfree, pe.now()]
        t_mo = pool.do(lambda e: e.memset(MO[:, :, :], 0.0), hfree)
        t_gain = load("gain", [(macc[n][:, :], a["final_g_2"].rearrange("(o d) -> o d", o=1)[:, n * 512:n * 512 + 512].broadcast_to([128, 512]))
                               for n in range(2)], hfree)
        c3.close()
        XH = Slots([sb(f"xh{i}", [128, 8, 256], R, c2) for i in range(2)])
        XL = [sb(f"xl{i}", [128, 8, 256], R, c2) for i in range(2)]
        PB = Slots([sb(f"pb{i}", [128, 2, 256], R, c2) for i in range(1)])
        PTT = Slots([sb(f"ptt{i}", [128, 2, 256], R, c2) for i in range(2)])
        GS = Slots([sb(f"gsl{i}", [128, 2], F, c2) for i in range(3)])
        HB = Slots(macc[2:4])
        TT = Slots([sb(f"tth{i}", [128, 4, 128], R, c2) for i in range(2)])
        TTL = [sb(f"ttl{i}", [128, 4, 128], R, c2) for i in range(2)]
        YH, YL = sb("YH", [128, 1024], R, c2), sb("YL", [128, 1024], R, c2)
        def gather(cols, rk, off, gate, m0, mid=None):
            k_, pb, fp = PB.get()
            kt_, ptt, ft = PTT.get()
            kg_, gsl, fg = GS.get()
            tb = []
            for n in range(2):
                for tb_ in range(2):
                    rc = rk(n, tb_)
                    tb.append(dve.do(lambda e, n=n, tb_=tb_, rc=rc: e.tensor_scalar(
                        pb[:, tb_, n * 128:(n + 1) * 128], iota, rc, None, ALU.is_equal), fp, m0, t_mi, mfree))
            if mid:
                mid()
            kx, xh, fx = XH.get()
            xl = XL[kx]
            tx = []
            for c in range(8):
                for (src, dst) in ((TH, xh), (TL, xl)):
                    if dst is xh:
                        b, bank, fr = PG.get()
                    o = bank[:, 0:256] if dst is xh else bank[:, 256:512]
                    for tb_ in range(2):
                        t = pe.do(lambda e, c=c, tb_=tb_, src=src, o=o: e.matmul(o, src[:, tb_, c * 128:(c + 1) * 128], pb[:, tb_, :],
                                                                                start=(tb_ == 0), stop=(tb_ == 1)), fr, tb, tok_t)
                t1 = act.do(lambda e, c=c, bank=bank: e.copy(xh[:, c, :], bank[:, 0:256]), t, fx, mfree)
                if mid:
                    t2 = dve.do(lambda e, c=c, bank=bank: e.tensor_copy(xl[:, c, :], bank[:, 256:512]), t, t1, fx, mfree)
                else:
                    t2 = act.do(lambda e, c=c, bank=bank: e.copy(xl[:, c, :], bank[:, 256:512]), t)
                PG.put(b, t1, t2)
                tx.append([t1, t2])
            b, bank, fr = PT.get()
            for n in range(2):
                for tb_ in range(2):
                    t = pe.do(lambda e, n=n, tb_=tb_, bank=bank: e.transpose(
                        bank[:, n * 256 + tb_ * 128:n * 256 + tb_ * 128 + 128], pb[:, tb_, n * 128:(n + 1) * 128].bitcast(F), ident), fr, tb)
            t = act.do(lambda e, bank=bank: e.copy(ptt[:, :, :], bank[:, :].rearrange("p (n t) -> p n t", n=2)), t, ft, mfree)
            PT.put(b, t)
            b, bank, fr = PT.get()
            for n in range(2):
                for tb_ in range(2):
                    gc = gate(n, tb_)
                    tg = pe.do(lambda e, n=n, tb_=tb_, bank=bank, gc=gc: e.matmul(
                        bank[:, n:n + 1], pb[:, tb_, n * 128:(n + 1) * 128].bitcast(F), gc, start=(tb_ == 0), stop=(tb_ == 1)), fr, tb, tm)
            PB.put(k_, tg)
            tg = dve.do(lambda e, bank=bank: e.tensor_copy(gsl[:, :], bank[:, 0:2]), tg, fg, mfree)
            PT.put(b, tg)
            return dict(kx=kx, xh=xh, xl=xl, tx=tx, kt=kt_, ptt=ptt, tp=t, kg=kg_, gsl=gsl, tg=tg)

        def up(G, n_in, tags):
            res = []
            for w in range(2):
                b, bank, fr = PG.get()
                pe.wait(fr)
                for k0 in range(2):
                    i, h, l, nk = take(tags[2 * w + k0])
                    for k in range(4):
                        kk = 4 * k0 + k
                        pe.wait(G["tx"][kk])
                        xs, ls = G["xh"][:, kk, n_in * 128:(n_in + 1) * 128], G["xl"][:, kk, n_in * 128:(n_in + 1) * 128]
                        for q, (x_, w_) in enumerate([(xs, h), (ls, h), (xs, l)]):
                            f = lambda e, x_=x_, w_=w_, k=k, kk=kk, q=q, bank=bank: e.matmul(
                                bank[:, :], x_, w_[:, k, :], start=(kk == 0 and q == 0), stop=(kk == 7 and q == 2))
                            if k == 3 and q == 2:
                                t = pe.do(f)
                            else:
                                pe.run(f)
                    done(i, t)
                res.append((b, bank, t))
            kh, hb, fh = HB.get()
            t1 = act.do(lambda e: e.activation(hb[:, :], res[0][1][:, :], ACT.Silu), res[0][2], fh, mfree)
            PG.put(res[0][0], t1)
            t2 = tt2(hb[:, :], res[1][1][:, :], hb[:, :], ALU.mult, t1, res[1][2])
            PG.put(res[1][0], t2)
            return kh, hb, t2

        def turn(kh, hb, th):
            b, bank, fr = PT.get()
            for j in range(4):
                t = pe.do(lambda e, j=j, bank=bank: e.transpose(bank[:, j * 128:(j + 1) * 128], hb[:, j * 128:(j + 1) * 128], ident), fr, th)
            HB.put(kh, t)
            kt, tt_, ft = TT.get()
            v = bank[:, :].rearrange("p (j t) -> p j t", j=4)
            rr = split(tt_[:, :, :], TTL[kt][:, :, :], v, t, [ft, mfree])
            PT.put(b, *rr)
            return kt, tt_, rr

        def down(kt, tt_, rr, n, tags, yfree):
            pe.wait(rr, yfree)
            for j in range(2):
                i, h, l, nk = take(tags[j])
                for k in range(2):
                    kk = 2 * j + k
                    for half in range(2):
                        for q, (x_, w_) in enumerate([(tt_, h), (TTL[kt], h), (tt_, l)]):
                            f = lambda e, x_=x_, w_=w_, k=k, kk=kk, q=q, half=half: e.matmul(
                                YB[half][:, :], x_[:, kk, :], w_[:, k, half * 512:(half + 1) * 512],
                                start=(n == 0 and kk == 0 and q == 0), stop=(n == 6 and kk == 3 and q == 2), skip_group_check=True)
                            if k == 1 and half == 1 and q == 2:
                                t = pe.do(f)
                            else:
                                pe.run(f)
                done(i, t)
            TT.put(kt, t)
            return t

        def collect(G, n_in, t):
            gs = G["gsl"][:, n_in:n_in + 1]
            tl = []
            for half in range(2):
                sl = slice(half * 512, half * 512 + 512)
                th = act.do(lambda e, half=half, sl=sl: e.activation(YH[:, sl], YB[half][:, :], ACT.Copy, scale=gs), t, G["tg"], state["ys"], mfree)
                tl.append(dve.do(lambda e, half=half, sl=sl: e.scalar_tensor_tensor(
                    out=YL[:, sl], in0=YB[half][:, :], scalar=gs, in1=YH[:, sl].bitcast(F), op0=ALU.mult, op1=ALU.subtract), th, state["ys"], mfree))
            state["yfree"] = tl
            return tl + [th]

        def scatter(G, n_in, ty):
            for c in range(0, 8, 2):
                b, bank, fr = PG.get()
                for m in range(2):
                    for q, y in enumerate((YH, YL)):
                        t = pe.do(lambda e, c=c, m=m, q=q, y=y, bank=bank: e.matmul(
                            bank[:, m * S:(m + 1) * S], y[:, (c + m) * 128:(c + m + 1) * 128], G["ptt"][:, n_in, :],
                            start=(q == 0), stop=(q == 1)), fr, ty, G["tp"])
                tv = tt2(MO[:, c:c + 2, :], bank[:, :].rearrange("p (m t) -> p m t", m=2), MO[:, c:c + 2, :], ALU.add, t, state["mo"])
                PG.put(b, tv)
            state["ys"] = [t]
            return t

        def etags(e, n):
            return [(tag, e, n, k0) for tag in ("w1", "w3") for k0 in range(2)]

        def dtags(e, n):
            return [("w2", e, n, j) for j in range(2)]

        def run_experts(order, gathers, extra=False, aside=None):
            prev = None
            late = None

            def finish_step(p):
                (e, n), (kt, tt_, rr) = p
                return down(kt, tt_, rr, n, dtags(e, n), state["yfree"] if n == 0 else None)
            for (e, n) in order:
                G = gathers[e // 2]
                h = up(G, e % 2, etags(e, n))
                if prev is not None:
                    (pe_, pn), t_ = prev
                    t = finish_step(prev)
                    if pn == 6:
                        Gp = gathers[pe_ // 2]
                        late = (Gp, pe_ % 2, collect(Gp, pe_ % 2, t), pe_)
                if n == 1 and late is not None:
                    t = scatter(*late[:3])
                    release(late, t, gathers)
                    late = None
                if n == 2 and e == 0 and aside:
                    aside()
                if n == 3 and e % 2 == 0 and e + 2 < NEXP and not extra:
                    gathers[e // 2 + 1] = gather(None, *gargs(e // 2 + 1))
                prev = ((e, n), turn(*h))
            t = finish_step(prev)
            (pe_, pn), _ = prev
            Gp = gathers[pe_ // 2]
            ty = collect(Gp, pe_ % 2, t)
            t = scatter(Gp, pe_ % 2, ty)
            release((Gp, pe_ % 2, ty, pe_), t, gathers)

        def release(late, t, gathers):
            G, n_in, _, e = late
            if e % 2 == 1:
                XH.put(G["kx"], pe.now())
                PTT.put(G["kt"], pe.now())
                GS.put(G["kg"], dve.now(), act.now())

        def gargs(p):
            return (lambda n, tb_: RK[:, tb_, 2 * p + n:2 * p + n + 1], 0,
                    lambda n, tb_: ro(tb_, 7)[:, 2 * p + n:2 * p + n + 1], tr)
        moe[0] = True
        flush_lows()
        gathers = {0: gather(None, *gargs(0), mid=lows_and_gates)}
        YB = (banks[6], banks[7])
        ytok = PT.free[6] + PT.free[7]
        assert len(PT.order) == 8
        fb = PT.free
        PG, PT = Slots(banks[0:4]), Slots(banks[4:6])
        PG.free, PT.free = fb[0:4], fb[4:6]
        state = {"yfree": ytok, "ys": [], "mo": [t_mo]}
        t_ci = []

        def overflow():
            b, bank, fr = PT.get()
            pe.do(lambda e: e.matmul(bank[:, 0:8], one[:, :], ro(0, 6), start=True, stop=False), fr)
            t_cnt = pe.do(lambda e: e.matmul(bank[:, 0:8], one[:, :], ro(1, 6), start=False, stop=True))
            t_cn = dve.do(lambda e: e.tensor_copy(CN[:, 0:8], bank[:, 0:8]), t_cnt, hfree)
            PT.put(b, t_cn)
            t = dve.do(lambda e: e.tensor_scalar(CN[:, 8:16], CN[:, 0:8], float(CAP), None, ALU.is_gt), t_cn)
            t = dve.do(lambda e: e.memset(CN[:, 56:64], 1.0), hfree)
            t = dve.do(lambda e: e.tensor_tensor_scan(CN[:, 16:24], CN[:, 56:64], CN[:, 8:16], 0.0, ALU.mult, ALU.add), t)
            t_ov = [dve.do(lambda e: e.tensor_copy(CN[:, 48:49], CN[:, 23:24]), t)]
            for j in range(3):
                sj = CN[:, 24 + 8 * j:32 + 8 * j]
                t1 = dve.do(lambda e: e.tensor_scalar(sj, CN[:, 16:24], float(j + 1), None, ALU.is_equal), t)
                t1 = tt2(sj, sj, CN[:, 8:16], ALU.mult, t1)
                t1 = dve.do(lambda e: e.tensor_tensor_reduce(CN[:, 56:64], sj, eix, 1.0, 0.0, ALU.mult, ALU.add, CN[:, 49 + j:50 + j]), t1, t_ov)
                t1 = dve.do(lambda e: e.tensor_scalar(CN[:, 49 + j:50 + j], CN[:, 49 + j:50 + j], -1.0, 8.0, ALU.mult, ALU.add), t1)
                t1 = dve.do(lambda e: e.tensor_scalar(CN[:, 49 + j:50 + j], CN[:, 49 + j:50 + j], 7.0, None, ALU.min), t1)
                for tb_ in range(2):
                    t1 = dve.do(lambda e: e.tensor_tensor_reduce(CN[:, 56:64], sj, RK[:, tb_, :], 1.0, -float(CAP), ALU.mult, ALU.add,
                                                                 OV[:, tb_, j:j + 1]), t1, tr, hfree)
                    t1 = dve.do(lambda e: e.tensor_tensor_reduce(CN[:, 56:64], sj, ro(tb_, 7), 1.0, 0.0, ALU.mult, ALU.add,
                                                                 OV[:, tb_, 4 + j:5 + j]), t1, tm)
                t_ov.append(t1)
            t_ov.append(dve.do(lambda e: e.memset(OV[:, :, 3:4], -1.0), hfree))
            t_ci.append(dve.do(lambda e: e.tensor_copy(CI[:, :], CN[:, 48:52]), t_ov))

        run_experts(steps, gathers, aside=overflow)
        t_ci = t_ci[0]

        for q in (pe, act, dve, pool, sp):
            q.wait(fence(), t_ci)
        main = (pe, act, dve)
        n_over = nc.values_load(CI[0:1, 0:1], min_val=0, max_val=3)
        pe, act, dve = (Queue(q.eng, sem("s_over_" + n)) for q, n in zip(main, ("pe", "act", "dve")))
        s_raw = [sem(f"s_over_raw{i}") for i in range(NR + NX)]
        plan, raw_free, where, used = [], {}, [], {}
        wide[0], nxt[0], first_moe[0] = [], 0, 0
        pos[0] = ahead[0] = gcount[0] = taken[0] = 0
        pair_free = [[] for _ in range(NP)]
        for ring in (PG, PT, XH, PB, PTT, GS, HB, TT):
            assert len(ring.order) == len(ring.bufs)
            ring.free = [[] for _ in ring.bufs]
        state = {"yfree": [], "ys": [], "mo": []}
        ovt = lambda n, tb_, j, o: OV[:, tb_, o + j:o + j + 1] if n == 0 else OV[:, tb_, 3:4]
        for j in range(3):
            with nc.If(n_over > j):
                ex = nc.sync.value_load(CI[0:1, 1 + j:2 + j], min_val=0, max_val=7)
                eu = [a[f"moe_w{w}_2"] for w in (1, 3)]
                for n in range(8):
                    if n < 7:
                        for tag, w in (("w1", eu[0]), ("w3", eu[1])):
                            for k0 in range(2):
                                src = w[0, bass.ds(ex, 1), k0 * 512:(k0 + 1) * 512, n * 512:(n + 1) * 512]
                                plan.append(("G", (tag, 0, n, k0), src.rearrange("a (k p) n -> p (a k) n", p=128), 4, 512))
                    if n:
                        for k0 in range(2):
                            r0 = (n - 1) * 512 + k0 * 256
                            src = a["moe_w2_2"][0, bass.ds(ex, 1), r0:r0 + 256, :]
                            plan.append(("G", ("w2", 0, n - 1, k0), src.rearrange("a (k p) n -> p (a k) n", p=128), 2, 1024))
                issue()
                G = gather(None, lambda n, tb_: ovt(n, tb_, j, 0), 0, lambda n, tb_: ovt(n, tb_, j, 4), None)
                run_experts([(0, n) for n in range(7)], {0: G}, extra=True)
                XH.put(G["kx"], pe.now())
                PTT.put(G["kt"], pe.now())
                GS.put(G["kg"], dve.now(), act.now())
                for q in (pe, act, dve, pool, sp):
                    q.wait([pe.now(), act.now(), dve.now()])
            for q in (pe, act, dve, pool, sp):
                q.eng.wait_ge(t_ci[0], t_ci[1])
        pe, act, dve = main
        for ring in (PG, PT, SQ, RS):
            ring.free = [[] for _ in ring.bufs]

        c2.close()
        ofree = fence()
        c2 = ctx.enter_context(ExitStack())
        o = sb("onat", [128, 2, 1024], F, c2)
        ss = sb("ss", [128, 16], F, c2)
        tx = []
        for c in range(8):
            tx.append(dve.do(lambda e: e.scalar_tensor_tensor(out=X[:, c, :], in0=MO[:, c, :], scalar=modT[3][:, 40 + c:41 + c],
                                                              in1=X[:, c, :], op0=ALU.mult, op1=ALU.add), dve.now(), mod_tok[3, 11]))
        bks = {}
        for half in range(2):
            for tb in range(2):
                b, bank, fr = PG.get()
                for j in range(4):
                    c = 4 * half + j
                    t = pe.do(lambda e: e.transpose(bank[:, j * 128:(j + 1) * 128], X[:, c, tb * 128:tb * 128 + 128], ident), fr, tx[c])
                bks[half, tb] = bank, t
        for half in range(2):
            for tb in range(2):
                bank, t = bks[half, tb]
                n = 2 * tb + half
                t = act.do(lambda e: e.activation(o[:, tb, half * 512:half * 512 + 512], bank[:, :], ACT.Square,
                                                  accum_out=ss[:, n:n + 1]), t, ofree)
        sv = ss[:, 0:4].rearrange("p (b h) -> p b h", b=2)
        t_sq = t
        t = tt2(ss[:, 4:6].rearrange("p (b o) -> p b o", b=2), sv[:, :, 0:1], sv[:, :, 1:2], ALU.add, t, ofree)
        t = act.do(lambda e: e.activation(ss[:, 6:8], ss[:, 4:6], ACT.Ln, bias=eps_c[:, 0:1], scale=1.0 / D), t)
        t = act.do(lambda e: e.activation(ss[:, 6:8], ss[:, 6:8], ACT.Exp, scale=-0.5), t)
        for half in range(2):
            for tb in range(2):
                bank = bks[half, tb][0]
                oo = o[:, tb, half * 512:half * 512 + 512]
                t1 = dve.do(lambda e: e.scalar_tensor_tensor(out=oo, in0=bank[:, :], scalar=ss[:, 6 + tb:7 + tb], in1=macc[half][:, :],
                                                             op0=ALU.mult, op1=ALU.mult), t, t_sq, t_gain)
                t_out = load("out", [(out[0, tb * 128:(tb + 1) * 128, half * 512:half * 512 + 512], oo)], t1, q=sp)
        sp.wait(t_out)
        c2.close()


_USED = ["x", "c", "w_mod", "b_mod", "norm_mix", "norm_ffn", "w_in", "qnorm_a", "knorm_a", "sinks", "rnn_conv_w",
         "rnn_conv_b", "rnn_gate_a_w", "rnn_gate_a_b", "rnn_gate_x_w", "rnn_gate_x_b", "rnn_lambda", "qnorm_c",
         "knorm_c", "rel_bias", "w_branch", "w_out", "w_up", "ffn_conv_w", "ffn_conv_b", "w_down", "c_2", "ctx_2",
         "c_ctx_2", "ada_w_2", "ada_b_2", "norm1_g_2", "norm2_g_2", "attn_w_qkv_2", "attn_lq1_2", "attn_lk1_2",
         "attn_lq2_2", "attn_lk2_2", "attn_subln_g_2", "attn_w_o_2", "fnet_w_o_2", "fnet_b_o_2", "ff_w1_2",
         "ff_w3_2", "ff_w2_2", "moe_router_2", "moe_w1_2", "moe_w3_2", "moe_w2_2", "final_g_2"]


def kernel(**inputs):
    import concourse.bacc as bacc
    from concourse.bass_utils import run_bass_kernel_spmd

    nc = bacc.Bacc("TRN2", target_bir_lowering=False, num_devices=1)
    arrays, aps = {}, {}
    for name in _USED:
        v = np.ascontiguousarray(inputs[name])
        arrays[f"in_{name}"] = v
        aps[name] = nc.dram_tensor(f"in_{name}", v.shape, mybir.dt.from_np(v.dtype), kind="ExternalInput").ap()
    v = constants()
    arrays["in_consts"] = v
    aps["consts"] = nc.dram_tensor("in_consts", v.shape, F, kind="ExternalInput").ap()
    out = nc.dram_tensor("out_0", (1, S, D), F, kind="ExternalOutput").ap()
    build(nc, aps, out)
    r = run_bass_kernel_spmd(nc, [arrays], core_ids=[0])
    return r.results[0]["out_0"]
```
